# Optimizing a Trainium2 kernel written in Bass

```python
import jax, jax.numpy as jnp
from jax import lax
import numpy as np

D_MODEL = 2048
BATCH = 1
SEQ = 512
DEPTH = 1

CHUNK = 64
N_MEM = 256
EPS = 1e-6

DSA_HEADS = 8
DSA_HEAD_DIM = 128
DSA_LATENT = 256
IDX_HEADS = 8
IDX_DIM = 64
TOPK_MAX = 256
Q_BLOCK = 128

ML_HEADS = 4
ML_QK_DIM = 128
ML_V_DIM = 256
CONV_W = 4

D_MIX = DSA_HEADS * DSA_HEAD_DIM + ML_HEADS * ML_V_DIM

IN_SIZES = (
    DSA_HEADS * DSA_HEAD_DIM,
    DSA_LATENT,
    IDX_HEADS * IDX_DIM,
    IDX_DIM,
    IDX_HEADS,
    ML_HEADS * ML_QK_DIM,
    ML_HEADS * ML_QK_DIM,
    ML_HEADS * ML_V_DIM,
    ML_HEADS,
    ML_HEADS,
    ML_HEADS * ML_V_DIM,
)
D_IN = sum(IN_SIZES)

X_HEADS = 4
X_HEAD_DIM = D_MODEL // X_HEADS

N_GROUPS = 4
EXP_PER_GROUP = 8
N_EXPERTS = N_GROUPS * EXP_PER_GROUP
TOPK_IN_GROUP = 2
D_EXPERT = 512
MOE_BLOCK = 128

kernel_name = "hybrid_dsa_mlstm_hiermoe_layer"

def rmsnorm(x, g):
    xf = x.astype(jnp.float32)
    y = xf * lax.rsqrt(jnp.mean(xf * xf, axis=-1, keepdims=True) + EPS)
    return (y * g.astype(jnp.float32)).astype(x.dtype)

def dsa_mixer(q, c_kv, q_idx, k_idx, w_idx, w_uk, w_uv, kv_norm_g, k_idx_norm_g):
    B, T = q.shape[:2]
    topk = min(TOPK_MAX, T // 4)
    c_kv = rmsnorm(c_kv, kv_norm_g)
    k_idx = rmsnorm(k_idx, k_idx_norm_g).astype(jnp.float32)
    q_abs = jnp.einsum('bthd,chd->bthc', q, w_uk)
    key_chunk = jnp.arange(T) // CHUNK
    nb = T // Q_BLOCK
    bidx = jnp.arange(B)[:, None, None]

    def to_blocks(a):
        return jnp.moveaxis(a.reshape((B, nb, Q_BLOCK) + a.shape[2:]), 1, 0)

    def block_fn(args):
        qi, wi, qa, start = args
        q_chunk = (start + jnp.arange(Q_BLOCK)) // CHUNK
        admissible = key_chunk[None, :] <= q_chunk[:, None]
        dots = jnp.einsum('bqhd,bsd->bqhs', qi.astype(jnp.float32), k_idx) * IDX_DIM ** -0.5
        score = jnp.einsum('bqh,bqhs->bqs', wi.astype(jnp.float32) * IDX_HEADS ** -0.5,
                           jax.nn.relu(dots))
        score = jnp.where(admissible[None], score, -jnp.inf)
        _, sel = lax.top_k(score, topk)
        valid = key_chunk[sel] <= q_chunk[None, :, None]
        c_sel = c_kv[bidx, sel]
        logits = jnp.einsum('bqhc,bqkc->bqhk', qa.astype(jnp.float32),
                            c_sel.astype(jnp.float32)) * DSA_HEAD_DIM ** -0.5
        logits = jnp.where(valid[:, :, None, :], logits, -jnp.inf)
        p = jax.nn.softmax(logits, axis=-1)
        return jnp.einsum('bqhk,bqkc->bqhc', p.astype(c_sel.dtype), c_sel)

    o_lat = lax.map(block_fn, (to_blocks(q_idx), to_blocks(w_idx), to_blocks(q_abs),
                               jnp.arange(nb) * Q_BLOCK))
    o_lat = jnp.moveaxis(o_lat, 0, 1).reshape(B, T, DSA_HEADS, DSA_LATENT)
    o = jnp.einsum('bthc,chd->bthd', o_lat, w_uv)
    return o.reshape(B, T, DSA_HEADS * DSA_HEAD_DIM)

def causal_conv(x, w, b):
    T = x.shape[1]
    xp = jnp.pad(x, ((0, 0), (CONV_W - 1, 0), (0, 0)))
    y = b
    for j in range(CONV_W):
        y = y + xp[:, j:j + T] * w[j]
    return y

def mlstm_mixer(q, k, v, i_pre, f_pre, o_pre, head_norm_g):
    B, T, H, DK = q.shape
    DV = v.shape[-1]
    nc = T // CHUNK
    f32 = jnp.float32

    def chunks(a):
        a = a.reshape((B, nc, CHUNK) + a.shape[2:])
        return jnp.moveaxis(jnp.moveaxis(a, 3, 2), 1, 0)

    qc = chunks(q.astype(f32) * DK ** -0.5)
    kc = chunks(k.astype(f32))
    vc = chunks(v.astype(f32))
    li = chunks(i_pre.astype(f32))
    lf = chunks(jax.nn.log_sigmoid(f_pre.astype(f32)))
    causal = jnp.tril(jnp.ones((CHUNK, CHUNK), bool))

    def step(carry, inp):
        C, n, m = carry
        qh, kh, vh, li_c, lf_c = inp
        b = jnp.cumsum(lf_c, axis=-1)
        g = b[..., -1]
        dmat = b[..., :, None] - b[..., None, :] + li_c[..., None, :]
        dmat = jnp.where(causal, dmat, -jnp.inf)
        inter = b + m[..., None]
        m_t = jnp.maximum(inter, jnp.max(dmat, axis=-1))
        w_intra = jnp.exp(dmat - m_t[..., None])
        a_inter = jnp.exp(inter - m_t)
        qk = jnp.einsum('bhtd,bhsd->bhts', qh, kh) * w_intra
        num = (a_inter[..., None] * jnp.einsum('bhtd,bhdv->bhtv', qh, C)
               + jnp.einsum('bhts,bhsv->bhtv', qk, vh))
        den = a_inter * jnp.einsum('bhtd,bhd->bht', qh, n) + qk.sum(-1)
        h = num / jnp.maximum(jnp.abs(den), jnp.exp(-m_t))[..., None]
        decay_s = g[..., None] - b + li_c
        m_new = jnp.maximum(g + m, decay_s.max(-1))
        ws = jnp.exp(decay_s - m_new[..., None])
        a_state = jnp.exp(g + m - m_new)
        wk = ws[..., None] * kh
        C_new = a_state[..., None, None] * C + jnp.einsum('bhsd,bhsv->bhdv', wk, vh)
        n_new = a_state[..., None] * n + wk.sum(-2)
        return (C_new, n_new, m_new), h

    init = (jnp.zeros((B, H, DK, DV), f32), jnp.zeros((B, H, DK), f32), jnp.zeros((B, H), f32))
    _, hs = lax.scan(step, init, (qc, kc, vc, li, lf))
    hs = jnp.moveaxis(jnp.moveaxis(hs, 0, 1), 2, 3).reshape(B, T, H, DV).astype(v.dtype)
    hs = rmsnorm(hs, head_norm_g.reshape(H, DV)).reshape(B, T, H * DV)
    return hs * jax.nn.sigmoid(o_pre)

def memory_cross_attn(h, mem_n, w_cq, w_ckv, w_co):
    B, T, D = h.shape
    M = mem_n.shape[1]
    q = (h @ w_cq).reshape(B, T, X_HEADS, X_HEAD_DIM)
    kv = (mem_n @ w_ckv).reshape(B, M, 2, X_HEADS, X_HEAD_DIM)
    k, v = kv[:, :, 0], kv[:, :, 1]
    logits = jnp.einsum('bthd,bmhd->bhtm', q.astype(jnp.float32),
                        k.astype(jnp.float32)) * X_HEAD_DIM ** -0.5
    p = jax.nn.softmax(logits, axis=-1).astype(v.dtype)
    o = jnp.einsum('bhtm,bmhd->bthd', p, v).reshape(B, T, D)
    return o @ w_co

def hier_moe(h, w_group, b_group, w_router, b_router, w_gate, w_up, w_down):
    B, T, D = h.shape
    N = B * T
    xt = h.reshape(N, D)
    g_logits = (xt @ w_group).astype(jnp.float32) + b_group
    g_prob = jax.nn.softmax(g_logits, axis=-1)
    g_sel = jnp.argmax(g_logits, axis=-1)
    p_g = jnp.take_along_axis(g_prob, g_sel[:, None], axis=-1)
    e_logits = ((xt @ w_router).astype(jnp.float32) + b_router).reshape(N, N_GROUPS, EXP_PER_GROUP)
    e_logits = jnp.take_along_axis(e_logits, g_sel[:, None, None], axis=1)[:, 0]
    top_p, top_local = lax.top_k(jax.nn.softmax(e_logits, axis=-1), TOPK_IN_GROUP)
    gates = p_g * top_p / top_p.sum(-1, keepdims=True)
    expert_id = g_sel[:, None] * EXP_PER_GROUP + top_local

    A = N * TOPK_IN_GROUP
    flat_e = expert_id.reshape(A).astype(jnp.int32)
    flat_tok = jnp.repeat(jnp.arange(N, dtype=jnp.int32), TOPK_IN_GROUP)
    flat_w = gates.reshape(A)
    order = jnp.argsort(flat_e)
    se, stok, sw = flat_e[order], flat_tok[order], flat_w[order]
    counts = jnp.zeros((N_EXPERTS,), jnp.int32).at[flat_e].add(1)
    starts = jnp.cumsum(counts) - counts
    padded = (counts + MOE_BLOCK - 1) // MOE_BLOCK * MOE_BLOCK
    pad_ends = jnp.cumsum(padded)
    pad_starts = pad_ends - padded
    row = pad_starts[se] + (jnp.arange(A, dtype=jnp.int32) - starts[se])
    nblk = -(-A // MOE_BLOCK) + N_EXPERTS
    n_rows = nblk * MOE_BLOCK
    row_tok = jnp.full((n_rows,), N, jnp.int32).at[row].set(stok)
    row_w = jnp.zeros((n_rows,), jnp.float32).at[row].set(sw)
    blk_expert = jnp.minimum(
        jnp.searchsorted(pad_ends, jnp.arange(nblk, dtype=jnp.int32) * MOE_BLOCK, side='right'),
        N_EXPERTS - 1)
    x_pad = jnp.concatenate([xt, jnp.zeros((1, D), xt.dtype)], axis=0)

    def expert_block(args):
        tok, e = args
        xb = x_pad[tok]
        a = jax.nn.silu(xb @ w_gate[e]) * (xb @ w_up[e])
        return a @ w_down[e]

    y_rows = lax.map(expert_block, (row_tok.reshape(nblk, MOE_BLOCK), blk_expert))
    y_rows = y_rows.reshape(n_rows, D) * row_w[:, None].astype(y_rows.dtype)
    y = jax.ops.segment_sum(y_rows, row_tok, num_segments=N + 1)[:N]
    return y.reshape(B, T, D)

def setup_inputs(seed: int = 0) -> dict:
    key = jax.random.key(seed)
    ks = jax.random.split(key, 32)
    f32 = jnp.float32
    L = DEPTH

    def nrm(k, shape, scale):
        return jax.random.normal(k, shape, f32) * scale

    def gain(k, shape):
        return 1.0 + 0.02 * jax.random.normal(k, shape, f32)

    return {
        "x": nrm(ks[0], (BATCH, SEQ, D_MODEL), 1.0),
        "mem": nrm(ks[1], (BATCH, N_MEM, D_MODEL), 1.0),
        "norm_mix_g": gain(ks[2], (L, D_MODEL)),
        "w_in": nrm(ks[3], (L, D_MODEL, D_IN), D_MODEL ** -0.5),
        "kv_norm_g": gain(ks[4], (L, DSA_LATENT)),
        "k_idx_norm_g": gain(ks[5], (L, IDX_DIM)),
        "w_uk": nrm(ks[6], (L, DSA_LATENT, DSA_HEADS, DSA_HEAD_DIM), DSA_LATENT ** -0.5),
        "w_uv": nrm(ks[7], (L, DSA_LATENT, DSA_HEADS, DSA_HEAD_DIM), DSA_LATENT ** -0.5),
        "conv_w": nrm(ks[8], (L, CONV_W, 2 * ML_HEADS * ML_QK_DIM), CONV_W ** -0.5),
        "conv_b": nrm(ks[9], (L, 2 * ML_HEADS * ML_QK_DIM), 0.01),
        "gate_b": jnp.concatenate([nrm(ks[10], (L, ML_HEADS), 0.1),
                                   3.0 + nrm(ks[11], (L, ML_HEADS), 0.1)], axis=-1),
        "ml_norm_g": gain(ks[12], (L, ML_HEADS * ML_V_DIM)),
        "w_out": nrm(ks[13], (L, D_MIX, D_MODEL), D_MIX ** -0.5),
        "norm_x_g": gain(ks[14], (L, D_MODEL)),
        "mem_norm_g": gain(ks[15], (L, D_MODEL)),
        "w_cq": nrm(ks[16], (L, D_MODEL, D_MODEL), D_MODEL ** -0.5),
        "w_ckv": nrm(ks[17], (L, D_MODEL, 2 * D_MODEL), D_MODEL ** -0.5),
        "w_co": nrm(ks[18], (L, D_MODEL, D_MODEL), D_MODEL ** -0.5),
        "norm_ffn_g": gain(ks[19], (L, D_MODEL)),
        "w_group": nrm(ks[20], (L, D_MODEL, N_GROUPS), D_MODEL ** -0.5),
        "b_group": nrm(ks[21], (L, N_GROUPS), 0.01),
        "w_router": nrm(ks[22], (L, D_MODEL, N_EXPERTS), D_MODEL ** -0.5),
        "b_router": nrm(ks[23], (L, N_EXPERTS), 0.01),
        "w_gate": nrm(ks[24], (L, N_EXPERTS, D_MODEL, D_EXPERT), D_MODEL ** -0.5),
        "w_up": nrm(ks[25], (L, N_EXPERTS, D_MODEL, D_EXPERT), D_MODEL ** -0.5),
        "w_down": nrm(ks[26], (L, N_EXPERTS, D_EXPERT, D_MODEL), D_EXPERT ** -0.5),
        "final_norm_g": gain(ks[27], (D_MODEL,)),
    }

def reference(x, mem, norm_mix_g, w_in, kv_norm_g, k_idx_norm_g, w_uk, w_uv, conv_w, conv_b,
              gate_b, ml_norm_g, w_out, norm_x_g, mem_norm_g, w_cq, w_ckv, w_co, norm_ffn_g,
              w_group, b_group, w_router, b_router, w_gate, w_up, w_down, final_norm_g):
    B, T, _ = x.shape
    split_points = np.cumsum(IN_SIZES)[:-1].tolist()
    for layer in range(DEPTH):
        h = rmsnorm(x, norm_mix_g[layer])
        proj = h @ w_in[layer]
        dq, ckv, qi, ki, wi, mq, mk, mv, mi, mf, mo = jnp.split(proj, split_points, axis=-1)
        dsa_out = dsa_mixer(dq.reshape(B, T, DSA_HEADS, DSA_HEAD_DIM), ckv,
                            qi.reshape(B, T, IDX_HEADS, IDX_DIM), ki, wi,
                            w_uk[layer], w_uv[layer], kv_norm_g[layer], k_idx_norm_g[layer])
        qk = jax.nn.silu(causal_conv(jnp.concatenate([mq, mk], axis=-1), conv_w[layer], conv_b[layer]))
        mq, mk = jnp.split(qk, 2, axis=-1)
        gb = gate_b[layer]
        ml_out = mlstm_mixer(mq.reshape(B, T, ML_HEADS, ML_QK_DIM),
                             mk.reshape(B, T, ML_HEADS, ML_QK_DIM),
                             mv.reshape(B, T, ML_HEADS, ML_V_DIM),
                             mi + gb[:ML_HEADS], mf + gb[ML_HEADS:], mo, ml_norm_g[layer])
        x = x + jnp.concatenate([dsa_out, ml_out], axis=-1) @ w_out[layer]
        mem_n = rmsnorm(mem, mem_norm_g[layer])
        x = x + memory_cross_attn(rmsnorm(x, norm_x_g[layer]), mem_n,
                                  w_cq[layer], w_ckv[layer], w_co[layer])
        x = x + hier_moe(rmsnorm(x, norm_ffn_g[layer]), w_group[layer], b_group[layer],
                         w_router[layer], b_router[layer], w_gate[layer], w_up[layer], w_down[layer])
    return rmsnorm(x, final_norm_g)


_drawn_inputs = setup_inputs


def setup_inputs(seed=0):
    import zlib

    import numpy as np

    out = dict(_drawn_inputs(seed))
    spreads = {}
    factors = {'kv_norm_g': 4.255,
     'k_idx_norm_g': 3.072,
     'conv_b': 4.284,
     'norm_x_g': 4.498,
     'mem_norm_g': 5.383,
     'b_group': 64.0,
     'b_router': 35.656,
     'final_norm_g': 7.966,
     'ml_norm_g': 3.433,
     'norm_ffn_g': 8.0}
    for name, (base, spread) in spreads.items():
        noise = np.random.default_rng([zlib.crc32(name.encode()), seed]).standard_normal(out[name].shape)
        drawn = base * np.exp(spread * noise) if base else spread * noise
        out[name] = __import__('jax').numpy.asarray(drawn.astype(out[name].dtype))
    for name, factor in factors.items():
        out[name] = (out[name] * factor).astype(out[name].dtype)
    return out
```

```python
from contextlib import ExitStack

import numpy as np

import concourse.bass as bass
from concourse import mybir

F32 = mybir.dt.float32
F32R = mybir.dt.float32r
I32 = mybir.dt.int32
U32 = mybir.dt.uint32
ALU = mybir.AluOpType
ACT = mybir.ActivationFunctionType
AX = mybir.AxisListType

P = 128
EPS = 1e-6
T, D = 512, 2048
TT = T // P
KT = D // P
CHUNK = 64
N_MEM = 256
MT = N_MEM // P
DSA_H, DSA_D, DSA_C = 8, 128, 256
CT = DSA_C // P
IDX_H, IDX_D = 8, 64
TOPK = min(256, T // 4)
ML_H, ML_K, ML_V = 4, 128, 256
CONV = 4
X_H, X_D = 4, D // 4
G, EG = 4, 8
NE = G * EG
F = 512
FT = F // P
BLOCK = 64
MAX_MORE = (2 * T - 1) // BLOCK
NB = NE + MAX_MORE
OUT_OF_RANGE = 1 << 20
NEG = -1.0e38
TAKEN = -3.0e38
HIDE = -1.0e30
MISC = DSA_C + IDX_D + IDX_H + 2 * ML_H

KB = 1024
BASE = 16512


def layer(nc, x, mem, norm_mix_g, w_in, kv_norm_g, k_idx_norm_g, w_uk, w_uv, conv_w, conv_b, gate_b,
          ml_norm_g, w_out, norm_x_g, mem_norm_g, w_cq, w_ckv, w_co, norm_ffn_g, w_group, b_group,
          w_router, b_router, w_gate, w_up, w_down, final_norm_g, out):
    with ExitStack() as ctx:
        def at(name, shape, off_kb, dt=F32):
            return nc.alloc_sbuf_tensor_at(name, shape, dt, offset=BASE + int(off_kb * KB))

        def sem(name):
            return ctx.enter_context(nc.semaphore(name))

        w_raw = [at(f"w_raw{r}", [P, 2, 512], 4 * r) for r in range(4)]
        w_hi = [at(f"w_hi{r}", [P, 2, 512], 16 + 4 * r, F32R) for r in range(2)]
        w_lo = [at(f"w_lo{r}", [P, 2, 512], 24 + 4 * r, F32R) for r in range(2)]
        act_hi = at("act_hi", [P, KT, T], 32, F32R)
        act_lo = at("act_lo", [P, KT, T], 64, F32R)
        proj_t = at("proj_t", [P, 20, T], 96)
        proj_n = at("proj_n", [P, TT, 2048], 136)
        misc = at("misc", [P, TT, MISC], 168)
        gain = at("gain", [P, D], 174)
        x_in = at("x_in", [P, TT, D], 96)
        xs = [at(f"xs{r}", [P, D], 182 + 8 * r) for r in range(2)]
        junk = at("junk", [P, D], 136)

        w_uk_raw = at("w_uk_raw", [P, CT, 1024], 144)
        w_uk_t = at("w_uk_t", [P, DSA_H, DSA_C], 182)
        c_kv = at("c_kv", [P, TT, DSA_C], 190)
        c_kv_t = at("c_kv_t", [P, CT, T], 194)
        k_idx_t = at("k_idx_t", [P, T], 198)
        relu_dot = [at(f"relu_dot{r}", [P, T], 174 + 2 * r) for r in range(2)]
        k_idx_n = at("k_idx_n", [P, TT, 2 * IDX_D], 178)
        kv_gain = at("kv_gain", [P, DSA_C], 180)
        ki_gain = at("ki_gain", [P, IDX_D], 181)
        sq_junk = at("sq_junk", [P, ML_V], 200)
        w_uv_s = at("w_uv_s", [P, CT, 1024], 174)
        q_abs = at("q_abs", [P, CT, DSA_H, P], 48)
        prob = [at(f"prob{r}", [P, T], 56 + 2 * r) for r in range(2)]
        bias0 = at("bias0", [P, P], 60)
        prob_t = at("prob_t", [P, TT, 4, P], 80)
        o_lat = at("o_lat", [P, CT, DSA_H, P], 88)

        qk_t = at("qk_t", [P, 2 * ML_H, T], 96)
        w_exp = [at(f"w_exp{r}", [P, T], 112 + 2 * r) for r in range(2)]
        pick_row = at("pick_row", [ML_H, ML_H, P], 116)
        hs = at("hs", [P, TT, ML_H * ML_V], 120)
        p_ml = at("p_ml", [P, TT, T], 182)
        ml_gain = at("ml_gain", [P, ML_H * ML_V], 190)
        rows = [at(f"rows{r}", [ML_H, T], 174 + 2 * r) for r in range(4)]
        rows += [at(f"rows{r}", [ML_H, T], 194 + 2 * (r - 4)) for r in range(4, 7)]
        r_ones = at("r_ones", [ML_H, T], 118)

        x_res = at("x_res", [P, TT, D], 136)
        x_q = at("x_q", [P, KT, T], 96)
        mem_in = at("mem_in", [P, MT, D], 64)
        mem_hi = at("mem_hi", [P, KT, N_MEM], 32, F32R)
        mem_lo = at("mem_lo", [P, KT, N_MEM], 48, F32R)
        mem_gain = at("mem_gain", [P, D], 174)
        mem_xs = [at(f"mem_xs{r}", [P, D], 182 + 8 * r) for r in range(2)]
        mem_junk = at("mem_junk", [P, D], 80)
        x_k = at("x_k", [P, KT, N_MEM], 168)
        x_v = at("x_v", [P, MT, D], 184)
        xp = [at(f"xp{r}", [P, N_MEM], 200 + r) for r in range(2)]
        xp_t = at("xp_t", [P, 2, MT, T], 128)

        e_raw = [at(f"e_raw{r}", [P, 2048], 8 * r) for r in range(12)]
        h_t = at("h_t", [P, KT, T], 96)
        xg = at("xg", [BLOCK, D], 96)
        y_sb = at("y_sb", [BLOCK, D], 104)
        xg_t = at("xg_t", [P, KT, BLOCK], 112)
        he_g = at("he_g", [P, FT, BLOCK], 116)
        he = at("he", [P, FT, BLOCK], 117)
        ffn_xs = [at(f"ffn_xs{r}", [P, D], 182 + 8 * r) for r in range(2)]
        ffn_junk = at("ffn_junk", [P, D], 128)
        w_r = at("w_r", [P, KT, G + NE], 168)
        fin_gain = at("fin_gain", [P, D], 174)
        y_back = at("y_back", [P, 2, D], 96)
        xs_f = at("xs_f", [P, D], 128)
        fin_o = [at(f"fin_o{r}", [P, D], 112 + 8 * r) for r in range(2)]

        low = [204.0]

        def small(name, shape, dt=F32):
            n = int(np.prod(shape[1:])) * 4
            t = at(name, shape, low[0], dt)
            low[0] += ((n + 31) // 32 * 32) / KB
            assert BASE + low[0] * KB <= nc.sbuf_usable_end, (name, low[0])
            return t

        ident = small("ident", [P, P])
        ones_col = small("ones_col", [P, 1])
        stats = small("stats", [P, 4, 16])
        idx_w = small("idx_w", [P, TT, IDX_H])
        head_max = small("head_max", [P, 16])
        head_neg = small("head_neg", [P, 16])
        head_sum = small("head_sum", [P, 16])
        head_inv = small("head_inv", [P, 16])
        best = small("best", [P, TT, 8])
        chosen = [None, small("chosen1", [P, 2 * P]), at("chosen2", [P, 3 * P], 202), at("chosen3", [P, 4 * P], 200)]
        conv_t = small("conv_t", [P, (CONV + 1) * 8])
        conv_rows = small("conv_rows", [(CONV + 1) * 8, P])
        gate_i = small("gate_i", [ML_H, 1])
        gate_f = small("gate_f", [ML_H, 1])
        u_tok = small("u_tok", [P, TT, ML_H])
        em_tok = small("em_tok", [P, TT, ML_H])
        den_inv = small("den_inv", [P, TT, ML_H])
        assert low[0] < 207.8

        psd = [ctx.enter_context(nc.psum_tensor(f"psd{m}", [P, 512], F32)) for m in range(4)]
        psx = [ctx.enter_context(nc.psum_tensor(f"psx{m}", [P, 512], F32)) for m in range(4)]
        low[0] = 198.0
        before = small("before", [P, P])
        ones_sq = small("ones_sq", [P, P])
        slot_none = small("slot_none", [2 * NB, BLOCK // 2 * 4], I32)
        slot_new = small("slot_new", [P, TT, 2, 4], I32)
        slots = small("slots", [BLOCK, NB, 4], I32)
        take_idx = small("take_idx", [BLOCK, 4], I32)
        put_idx = small("put_idx", [BLOCK, 4], I32)
        tok_f = small("tok_f", [P, TT, 2, 2])
        ones32 = small("ones32", [P, NE])
        iota_e = small("iota_e", [P, NE])
        iota_m = small("iota_m", [P, 8])
        iota_b = small("iota_b", [1, MAX_MORE])
        r_bias = small("r_bias", [P, G + NE])
        more_i = small("more_i", [1, MAX_MORE + 1], I32)
        g_log8 = small("g_log8", [P, TT, 8])
        assert low[0] <= 204.0, low

        low[0] = 128.0
        r_log = small("r_log", [P, TT, G + NE])
        g_top = small("g_top", [P, TT, 8])
        g_idx = small("g_idx", [P, TT, 8], U32)
        g_sel = small("g_sel", [P, TT])
        g_oh = small("g_oh", [P, TT, G])
        g_exp = small("g_exp", [P, TT, G])
        g_sum = small("g_sum", [P, TT])
        e_mul = small("e_mul", [P, TT, G, EG])
        e_log = small("e_log", [P, TT, EG])
        e_top = small("e_top", [P, TT, 8])
        e_exp = small("e_exp", [P, TT, EG])
        e_best = small("e_best", [P, TT, 8])
        e_idx = small("e_idx", [P, TT, 8], U32)
        neg_m = small("neg_m", [P, 2, TT])
        e_id = small("e_id", [P, TT, 2])
        e_den = small("e_den", [P, TT])
        gate = small("gate", [P, TT, 2])
        one_hot = small("one_hot", [P, TT, 2, NE])
        chose = small("chose", [P, TT, NE])
        assert low[0] <= 136.0, low
        low[0] = 174.0
        rank = small("rank", [P, TT, NE])
        picked = small("picked", [P, TT, 2, NE])
        count = small("count", [P, NE])
        full = small("full", [P, NE, 8])
        more = small("more", [P, NE])
        more_end = small("more_end", [P, NE])
        more_at = small("more_at", [P, NE])
        pos = small("pos", [P, TT, 2])
        pos_at = small("pos_at", [P, TT, 2])
        pos_q = small("pos_q", [P, TT, 2])
        pos_full = small("pos_full", [P, TT, 2, 8])
        row_f = small("row_f", [P, TT, 2])
        row_t = small("row_t", [P, TT, 2])
        row_i = small("row_i", [P, TT, 2], I32)
        more_f = small("more_f", [1, MAX_MORE + 1])
        more_cmp = small("more_cmp", [1, MAX_MORE, NE])
        assert low[0] <= 182.0, low

        h_rows = nc.dram_tensor("h_rows", (T, D), F32, kind="Internal").ap()
        y_rows = nc.dram_tensor("y_rows", (2 * T, D), F32, kind="Internal").ap()
        slot_rows = nc.dram_tensor("slot_rows", (NB * BLOCK, 4), I32, kind="Internal").ap()

        x_land = [sem(f"x_land{t}") for t in range(TT)]
        gain_land = sem("gain_land")
        const_land = sem("const_land")
        kv_land = sem("kv_land")
        uv_land = sem("uv_land")
        ml_land = sem("ml_land")
        res_land = sem("res_land")
        mem_land = sem("mem_land")
        w_land = [sem(f"w_land{r}") for r in range(4)]
        hi_done = sem("hi_done")
        lo_done = sem("lo_done")
        w_used = sem("w_used")
        bank_done = [sem(f"bank_done{m}") for m in range(4)]
        bank_free = [sem(f"bank_free{m}") for m in range(4)]
        dve_own = sem("dve_own")
        act_own = sem("act_own")
        pool_own = sem("pool_own")
        consts = sem("consts")
        n_sq, n_var, n_sd, n_xs = sem("n_sq"), sem("n_var"), sem("n_sd"), sem("n_xs")
        n_turned, n_hi, n_lo = sem("n_turned"), sem("n_hi"), sem("n_lo")
        k_sq, k_norm, k_turned, k_out_a, k_out_d = (sem(s) for s in (
            "k_sq", "k_norm", "k_turned", "k_out_a", "k_out_d"))
        uk_turned, uk_out = sem("uk_turned"), sem("uk_out")
        dot_done, relu_done, score_done, round_done = (sem(s) for s in (
            "dot_done", "relu_done", "score_done", "round_done"))
        bias_done = sem("bias_done")
        qa_done, qa_out_a, qa_out_d = sem("qa_done"), sem("qa_out_a"), sem("qa_out_d")
        lg_done, lg_masked, lg_max, exp_done, prob_done = (sem(s) for s in (
            "lg_done", "lg_masked", "lg_max", "exp_done", "prob_done"))
        pt_done, pt_out, pv_done, ol_out_a, ol_out_d, o_done, o_hi, o_lo = (sem(s) for s in (
            "pt_done", "pt_out", "pv_done", "ol_out_a", "ol_out_d", "o_done", "o_hi", "o_lo"))
        g_turned, g_abs, g_ln, g_sumd, g_em, g_pick, g_tok, g_tok_out = (sem(s) for s in (
            "g_turned", "g_abs", "g_ln", "g_sumd", "g_em", "g_pick", "g_tok", "g_tok_out"))
        c_turned, c_out, conv_done, silu_done, sig_done = (sem(s) for s in (
            "c_turned", "c_out", "conv_done", "silu_done", "sig_done"))
        m_row, m_exp, m_sel, m_qk, m_p, m_pv, m_den, m_hs, m_sq, m_norm, m_turned, m_hi, m_lo = (
            sem("m_" + s) for s in ("row", "exp", "sel", "qk", "p", "pv", "den", "hs", "sq", "norm",
                                    "turned", "hi", "lo"))
        xl_done, xl_max, x_exp, x_prob, xt_done, xt_out, xo_done, xo_hi, xo_lo = (
            sem(s) for s in ("xl_done", "xl_max", "x_exp", "x_prob", "xt_done", "xt_out", "xo_done",
                             "xo_hi", "xo_lo"))
        r_land, r_done, r_chose, r_neg, r_exp, r_rank, r_row, none_land, slot_store, slot_land = (
            sem(s) for s in ("r_land", "r_done", "r_chose", "r_neg", "r_exp", "r_rank",
                             "r_row", "none_land", "slot_store", "slot_land"))
        more_done, route_consts = sem("more_done"), sem("route_consts")
        e_land = [sem(f"e_land{r}") for r in range(12)]
        e_used = sem("e_used")
        xg_zero, xg_land, xg_turned, xg_out = sem("xg_zero"), sem("xg_land"), sem("xg_turned"), sem("xg_out")
        he_silu, he_done, y_out_a, y_out_d, y_store = (sem(s) for s in (
            "he_silu", "he_done", "y_out_a", "y_out_d", "y_store"))
        take_copied, put_copied, put_used, experts_done = (sem(s) for s in (
            "take_copied", "put_copied", "put_used", "experts_done"))
        back_land, f_add, f_sq, f_out = (sem(s) for s in ("back_land", "f_add", "f_sq", "f_out"))
        h_store = [sem(f"h_store{r}") for r in range(2)]
        f_store = [sem(f"f_store{r}") for r in range(2)]
        fg_land = sem("fg_land")

        SEGS = [("misc", 1, MISC), ("head_t", 5, 512), ("head_n", 4, 512), ("out", 4, 512),
                ("cq", 4, 512), ("k", 4, 512), ("v", 4, 512), ("co", 4, 512)]
        first = {}
        blocks = 0
        for name, n, _ in SEGS:
            first[name] = blocks
            blocks += n
        SEG_N = {name: n for name, n, _ in SEGS}
        SEG_W = {name: w for name, _, w in SEGS}
        NEXT = {a[0]: b[0] for a, b in zip(SEGS, SEGS[1:])}
        w_in_v = w_in[0].rearrange("(k p) n -> p k n", p=P)
        ckv_v = w_ckv[0].rearrange("(k p) n -> p k n", p=P)
        SEG_SRC = {
            "misc": (w_in_v, 0), "head_t": (w_in_v, MISC), "head_n": (w_in_v, MISC + 5 * 512),
            "out": (w_out[0].rearrange("(k p) n -> p k n", p=P), 0),
            "cq": (w_cq[0].rearrange("(k p) n -> p k n", p=P), 0),
            "k": (ckv_v, 0), "v": (ckv_v, D),
            "co": (w_co[0].rearrange("(k p) n -> p k n", p=P), 0),
        }
        NORM_AT = {"mix": 0, "x": 4, "mem": 8, "ffn": 10}
        NORM_N = {"mix": 4, "x": 4, "mem": 2, "ffn": 4}
        RSTD_AT = {"mix": 0, "kv": 1, "ml": 2, "x": 3, "mem": 4, "ffn": 5, "fin": 6}
        block = ctx.enter_context(nc.Block())

        def wait_alone(eng, sem_, value, base_sem, base_value):
            if not isinstance(value, int):
                eng.compute_val(value)
            eng.wait_ge(base_sem, base_value)
            eng.wait_ge(sem_, value)

        @block.sync
        def _(sp):
            def piece(name, i, j, wait=True):
                src, c0 = SEG_SRC[name]
                w = SEG_W[name]
                if wait:
                    sp.wait_ge(lo_done, (first[name] + i) * 8 + (j - 3))
                col = i * 512 + c0
                cols = slice(col, col + w) if isinstance(col, int) else bass.ds(col, w)
                sp.dma_start(w_raw[j % 4][:, :, 0:w], src[:, 2 * j:2 * j + 2, cols]).then_inc(w_land[j % 4], 16)

            def stream(name):
                n = SEG_N[name]
                if n > 1:
                    with sp.Fori(0, n - 1) as i:
                        for j in range(4, 8):
                            piece(name, i, j)
                        for j in range(4):
                            piece(name, i + 1, j)
                for j in range(4, 8):
                    piece(name, n - 1, j)
                if name in NEXT:
                    for j in range(4):
                        piece(NEXT[name], 0, j)

            sp.dma_start(gain[:, :], norm_mix_g[0:1, :].to_broadcast([P, D])).then_inc(gain_land, 16)
            for t in range(TT):
                sp.dma_start(x_in[:, t, :], x[0, t * P:(t + 1) * P, :]).then_inc(x_land[t], 16)
            for j in range(4):
                piece("misc", 0, j, wait=False)
            sp.dma_start(w_uk_raw[:, :, :], w_uk[0].rearrange("(c p) h d -> p c (h d)", p=P)).then_inc(const_land, 16)
            sp.dma_start(conv_rows[0:CONV * 8, :], conv_w[0].rearrange("j (f p) -> (j f) p", p=P)).then_inc(const_land, 16)
            sp.dma_start(conv_rows[CONV * 8:(CONV + 1) * 8, :],
                         conv_b[0].rearrange("(f p) -> f p", p=P)).then_inc(const_land, 16)
            gb = gate_b.rearrange("a (k g) -> g (a k)", k=2)
            sp.dma_start(gate_i[:, :], gb[:, 0:1]).then_inc(const_land, 16)
            sp.dma_start(gate_f[:, :], gb[:, 1:2]).then_inc(const_land, 16)
            sp.wait_ge(n_xs, 4)
            sp.dma_start(kv_gain[:, :], kv_norm_g[0:1, :].to_broadcast([P, DSA_C])).then_inc(kv_land, 16)
            sp.dma_start(ki_gain[:, :], k_idx_norm_g[0:1, :].to_broadcast([P, IDX_D])).then_inc(kv_land, 16)
            stream("misc")
            stream("head_t")
            stream("head_n")
            sp.wait_ge(bias_done, 1)
            sp.dma_start(w_uv_s[:, :, :], w_uv[0].rearrange("(c p) h d -> p c (h d)", p=P)).then_inc(uv_land, 16)
            sp.wait_ge(o_done, 2 * TT)
            sp.dma_start(ml_gain[:, :], ml_norm_g[0:1, :].to_broadcast([P, ML_H * ML_V])).then_inc(ml_land, 16)
            sp.wait_ge(m_norm, TT)
            sp.dma_start(x_res[:, :, :], x[0].rearrange("(t p) d -> p t d", p=P)).then_inc(res_land, 16)
            sp.dma_start(gain[:, :], norm_x_g[0:1, :].to_broadcast([P, D])).then_inc(gain_land, 16)
            stream("out")
            stream("cq")
            sp.wait_ge(n_xs, 8)
            sp.dma_start(mem_gain[:, :], mem_norm_g[0:1, :].to_broadcast([P, D])).then_inc(gain_land, 16)
            sp.wait_ge(bank_done[3], first["k"])
            sp.dma_start(mem_in[:, :, :], mem[0].rearrange("(t p) d -> p t d", p=P)).then_inc(mem_land, 16)
            stream("k")
            stream("v")
            sp.wait_ge(xl_done, 16)
            for m in (0, 2):
                sp.wait_ge(bank_free[m], first["co"])
            sp.wait_ge(xo_done, 16)
            sp.dma_start(gain[:, :], norm_ffn_g[0:1, :].to_broadcast([P, D])).then_inc(gain_land, 16)
            sp.dma_start(w_r[:, :, 0:G], w_group[0].rearrange("(k p) g -> p k g", p=P)).then_inc(r_land, 16)
            sp.dma_start(w_r[:, :, G:G + NE], w_router[0].rearrange("(k p) g -> p k g", p=P)).then_inc(r_land, 16)
            sp.dma_start(r_bias[:, 0:G], b_group[0:1, :].to_broadcast([P, G])).then_inc(r_land, 16)
            sp.dma_start(r_bias[:, G:G + NE], b_router[0:1, :].to_broadcast([P, NE])).then_inc(r_land, 16)
            sp.wait_ge(route_consts, 1)
            sp.dma_start(slot_rows.rearrange("(p n) c -> p (n c)", p=2 * NB), slot_none[:, :]).then_inc(none_land, 16)
            stream("co")
            sp.wait_ge(bank_done[3], blocks)

            def expert_piece(e, r):
                if r < 8:
                    w = (w_gate, w_up)[r % 2][0]
                    q = r // 2
                    src = w[bass.ds(e, 1) if not isinstance(e, int) else slice(e, e + 1)].rearrange(
                        "e (p k) f -> p (e k) f", k=KT)[:, 4 * q:4 * q + 4, :]
                    dst = e_raw[r][:, :].rearrange("p (k f) -> p k f", k=4)
                else:
                    w = w_down[0]
                    src = w[bass.ds(e, 1) if not isinstance(e, int) else slice(e, e + 1)].rearrange(
                        "e f d -> (e f) d")[P * (r - 8):P * (r - 7), :]
                    dst = e_raw[r][:, :]
                sp.dma_start(dst, src).then_inc(e_land[r], 16)

            def store_rows(t):
                sp.wait_ge(n_xs, NORM_AT["ffn"] + t + 1)
                sp.dma_start(h_rows[t * P:(t + 1) * P, :], ffn_xs[t % 2][:, :]).then_inc(h_store[t % 2], 16)

            for r in range(12):
                expert_piece(0, r)
                if r % 2 == 1 and r < 8:
                    store_rows(r // 2)
            sp.wait_ge(slot_store, 16 * 2 * TT)
            sp.dma_start(slots[:, :, :], slot_rows.rearrange("(b s) c -> s b c", s=BLOCK)).then_inc(slot_land, 16)
            with sp.Fori(1, NE) as e:
                for r in range(12):
                    sp.wait_ge(e_used, e * 12 + (r - 11))
                    expert_piece(e, r)
            sp.wait_ge(more_done, 1)
            n_more = sp.value_load(more_i[0:1, MAX_MORE:MAX_MORE + 1], min_val=0, max_val=MAX_MORE)
            with sp.Fori(0, MAX_MORE) as b:
                with sp.If(n_more > b):
                    e = sp.value_load(more_i[0:1, bass.ds(b, 1)], min_val=0, max_val=NE - 1)
                    for r in range(12):
                        sp.wait_ge(e_used, b * 12 + (12 * (NE - 1) + r + 1))
                        expert_piece(e, r)
            sp.wait_ge(experts_done, 1)
            sp.dma_start(fin_gain[:, :], final_norm_g.rearrange("(a d) -> a d", a=1).to_broadcast([P, D])).then_inc(fg_land, 16)
            for t in range(TT):
                if t >= 1:
                    sp.wait_ge(f_add, 2 * t)
                sp.dma_start(y_back[:, :, :], y_rows.rearrange("(k t p) d -> t p k d", k=2, p=P)[t]).then_inc(back_land, 16)
            for t in range(TT):
                sp.wait_ge(f_out, t + 1)
                sp.dma_start(out[0, t * P:(t + 1) * P, :], fin_o[t % 2][:, :]).then_inc(f_store[t % 2], 16)
            for r in range(2):
                sp.wait_ge(f_store[r], 16 * TT // 2)

        @block.gpsimd
        def _(pool):
            pool.memset(ident[:, :], 0.0).then_inc(pool_own, 1)
            pool.memset(ones_col[:, :], 1.0).then_inc(consts, 1)
            pool.wait_ge(pool_own, 1)
            pool.affine_select(out=ident[:, :], in_=ident[:, :], compare_op=ALU.not_equal, fill=1.0, base=0,
                               pattern=[[-1, P]], channel_multiplier=1).then_inc(consts, 1)
            pool.wait_ge(bank_done[3], first["out"])
            pool.memset(bias0[:, :], 0.0).then_inc(pool_own, 1)
            pool.wait_ge(pool_own, 2)
            pool.memset(bias0[0:CHUNK, CHUNK:P], HIDE).then_inc(bias_done, 1)
            for n in range(4 * ML_H):
                pool.wait_ge(m_exp, n + 1)
                w = w_exp[n % 2][:, 0:P]
                pool.affine_select(out=w, in_=w, compare_op=ALU.is_ge, fill=0.0, base=0,
                                   pattern=[[1, P]], channel_multiplier=-1).then_inc(m_sel, 1)
            pool.wait_ge(xo_done, 16)
            pool.wait_ge(x_prob, 16)
            pool.memset(slot_none[:, :], OUT_OF_RANGE).then_inc(route_consts, 1)
            pool.memset(before[:, :], 1.0).then_inc(pool_own, 1)
            pool.memset(ones_sq[:, :], 1.0).then_inc(pool_own, 1)
            pool.memset(ones32[:, :], 1.0).then_inc(pool_own, 1)
            pool.memset(slot_new[:, :, :, :], 0).then_inc(pool_own, 1)
            pool.iota(iota_e[:, :], [[1, NE]], base=0, channel_multiplier=0,
                      allow_small_or_imprecise_dtypes=True).then_inc(pool_own, 1)
            pool.iota(iota_m[:, :], [[BLOCK, 8]], base=BLOCK, channel_multiplier=0,
                      allow_small_or_imprecise_dtypes=True).then_inc(pool_own, 1)
            pool.iota(iota_b[:, :], [[1, MAX_MORE]], base=0, channel_multiplier=0,
                      allow_small_or_imprecise_dtypes=True).then_inc(pool_own, 1)
            pool.iota(tok_f[:, :, :, 0], [[P, TT], [0, 2]], base=0, channel_multiplier=1,
                      allow_small_or_imprecise_dtypes=True).then_inc(pool_own, 1)
            pool.iota(tok_f[:, :, :, 1], [[P, TT], [T, 2]], base=0, channel_multiplier=1,
                      allow_small_or_imprecise_dtypes=True).then_inc(pool_own, 1)
            pool.memset(g_log8[:, :, :], NEG).then_inc(pool_own, 1)
            pool.wait_ge(pool_own, 12)
            pool.affine_select(out=before[:, :], in_=before[:, :], compare_op=ALU.is_gt, fill=0.0, base=0,
                               pattern=[[1, P]], channel_multiplier=-1).then_inc(route_consts, 1)
            pool.wait_ge(r_done, TT)
            pool.memset(xg[:, :], 0.0).then_inc(xg_zero, 1)
            pool.wait_ge(none_land, 16)
            pool.wait_ge(r_row, 1)
            for t in range(TT):
                for k in range(2):
                    pool.indirect_dma_start(
                        out=slot_rows[:, :], out_offset=bass.IndirectOffsetOnAxis(ap=row_i[:, t, k:k + 1], axis=0),
                        in_=slot_new[:, t, k, :], in_offset=None,
                        bounds_check=NB * BLOCK - 1, oob_is_err=False).then_inc(slot_store, 16)
            pool.wait_ge(slot_land, 16)
            for r in range(2):
                pool.wait_ge(h_store[r], 16 * TT // 2)
            col = lambda b: bass.ds(b, 1) if not isinstance(b, int) else slice(b, b + 1)

            def take(b):
                if not (isinstance(b, int) and b == 0):
                    pool.wait_ge(xg_turned, b)
                pool.tensor_copy(take_idx[:, :], slots[:, col(b), :].rearrange("s b c -> s (b c)")).then_inc(take_copied, 1)
                wait_alone(pool, take_copied, b + 1, slot_land, 16)
                pool.indirect_dma_start(
                    out=xg[:, :], out_offset=None, in_=h_rows[:, :],
                    in_offset=bass.IndirectOffsetOnAxis(ap=take_idx[:, 0:1], axis=0),
                    bounds_check=T - 1, oob_is_err=False).then_inc(xg_land, 16)

            def put(b):
                if not (isinstance(b, int) and b == 0):
                    wait_alone(pool, y_store, b * 16, slot_land, 16)
                pool.tensor_copy(put_idx[:, :], slots[:, col(b), :].rearrange("s b c -> s (b c)")).then_inc(put_copied, 1)
                pool.wait_ge(put_copied, b + 1)
                wait_alone(pool, y_out_a, b * 2 + 2, slot_land, 16)
                pool.wait_ge(y_out_d, b * 2 + 2)
                pool.indirect_dma_start(
                    out=y_rows[:, :], out_offset=bass.IndirectOffsetOnAxis(ap=put_idx[:, 1:2], axis=0),
                    in_=y_sb[:, :], in_offset=None,
                    bounds_check=2 * T - 1, oob_is_err=False).then_inc(y_store, 16)

            pool.wait_ge(xg_zero, 1)
            take(0)
            take(1)
            put(0)
            with pool.Fori(1, NE - 1) as b:
                take(b + 1)
                put(b)
            put(NE - 1)
            pool.wait_ge(more_done, 1)
            n_more = pool.value_load(more_i[0:1, MAX_MORE:MAX_MORE + 1], min_val=0, max_val=MAX_MORE)
            with pool.Fori(0, MAX_MORE) as b:
                with pool.If(n_more > b):
                    take(b + NE)
                    put(b + NE)
            pool.wait_ge(y_store, n_more * 16 + 16 * NE)
            pool.sem_inc(experts_done, 1)

        @block.tensor
        def _(pe):
            def dense(name, mode, n_tok=512):
                base, n, w = first[name], SEG_N[name], SEG_W[name]
                hi, lo = (mem_hi, mem_lo) if name in ("k", "v") else (act_hi, act_lo)

                def one(i):
                    b = base + i
                    for j in range(8):
                        pe.wait_ge(lo_done, b * 8 + (j + 1))
                        for kk in range(2):
                            kt = 2 * j + kk
                            for m in range(4):
                                if kt == 0 and not (isinstance(b, int) and b == 0):
                                    pe.wait_ge(bank_free[m], b)
                                wh, wl = w_hi[j % 2][:, kk, :], w_lo[j % 2][:, kk, :]
                                if mode == "features":
                                    o = psd[m][:, 0:n_tok]
                                    c = slice(P * m, P * m + P)
                                    pairs = [(wh[:, c], hi[:, kt, 0:n_tok]), (wh[:, c], lo[:, kt, 0:n_tok]),
                                             (wl[:, c], hi[:, kt, 0:n_tok])]
                                elif mode == "tokens":
                                    o = psd[m][:, 0:w]
                                    c = slice(P * m, P * m + P)
                                    pairs = [(hi[:, kt, c], wh[:, 0:w]), (hi[:, kt, c], wl[:, 0:w]),
                                             (lo[:, kt, c], wh[:, 0:w])]
                                else:
                                    o = psd[m][:, 0:256]
                                    c = slice(P * (m // 2), P * (m // 2) + P)
                                    v = slice(256 * (m % 2), 256 * (m % 2) + 256)
                                    pairs = [(hi[:, kt, c], wh[:, v]), (hi[:, kt, c], wl[:, v]),
                                             (lo[:, kt, c], wh[:, v])]
                                for q, (a, c) in enumerate(pairs):
                                    ins = pe.matmul(o, a, c, start=(kt == 0 and q == 0), stop=(kt == KT - 1 and q == 2))
                                if kt == KT - 1:
                                    ins.then_inc(bank_done[m], 1)
                        if j < 7:
                            ins.then_inc(w_used, 1)

                if n == 1:
                    one(0)
                else:
                    with pe.Fori(0, n) as i:
                        one(i)

            def turn_norm(name, src):
                for t in range(NORM_N[name]):
                    pe.wait_ge(n_xs, NORM_AT[name] + t + 1)
                    for g in range(4):
                        q = 4 * (NORM_AT[name] + t) + g
                        if q >= 4:
                            pe.wait_ge(n_lo, q - 3)
                        for k in range(4):
                            kt = 4 * g + k
                            ins = pe.transpose(psx[g][:, P * k:P * k + P], src[t % 2][:, kt * P:kt * P + P], ident[:, :])
                        ins.then_inc(n_turned, 1)

            pe.wait_ge(consts, 2)
            turn_norm("mix", xs)
            pe.wait_ge(n_lo, 16)
            dense("misc", "tokens")
            dense("head_t", "features")

            pe.wait_ge(k_norm, 3 * TT)
            for c in range(CT):
                for t in range(TT):
                    ins = pe.transpose(psx[c][:, P * t:P * t + P], c_kv[:, t, P * c:P * c + P], ident[:, :])
                ins.then_inc(k_turned, 1)
            for t in range(TT):
                ins = pe.transpose(psx[2][:, P * t:P * t + P], k_idx_n[:, t, :], ident[:, :])
            ins.then_inc(k_turned, 1)
            pe.wait_ge(const_land, 5 * 16)
            for b in range(4):
                if b == 0:
                    pe.wait_ge(k_out_a, 2)
                if b == 1:
                    pe.wait_ge(k_out_d, 1)
                for h in range(2):
                    for c in range(CT):
                        d0 = (2 * b + h) * DSA_D
                        ins = pe.transpose(psx[b][:, DSA_C * h + P * c:DSA_C * h + P * c + P],
                                           w_uk_raw[:, c, d0:d0 + DSA_D], ident[:, :])
                ins.then_inc(uk_turned, 1)
            for m in range(4):
                pe.wait_ge(bank_free[m], first["head_n"])
            for n in range(3 * IDX_H):
                i, h = 1 + n // IDX_H, n % IDX_H
                if n < 4:
                    pe.wait_ge(uk_out, n + 1)
                else:
                    pe.wait_ge(relu_done, n - 3)
                r = slice(IDX_D * (h % 2), IDX_D * (h % 2) + IDX_D)
                pe.matmul(psx[n % 4][:, 0:P * (i + 1)], proj_t[r, 8 + h // 2, P * i:P * i + P],
                          k_idx_t[r, 0:P * (i + 1)], start=True, stop=True).then_inc(dot_done, 1)
            dense("head_n", "tokens")

            pe.wait_ge(relu_done, 3 * IDX_H)
            for m in range(4):
                pe.wait_ge(bank_free[m], first["out"])
            for i in range(TT):
                qs = slice(P * i, P * i + P)
                if i:
                    pe.wait_ge(pt_out, 8 * i)
                for b in range(4):
                    c, g = b // 2, b % 2
                    for h in range(4):
                        ins = pe.matmul(psx[b][:, P * h:P * h + P], w_uk_t[:, 4 * g + h, P * c:P * c + P],
                                        proj_t[:, 4 * g + h, qs], start=True, stop=True)
                    ins.then_inc(qa_done, 1)

                def logits(h):
                    n = 8 * i + h
                    if h == 0:
                        pe.wait_ge(qa_out_a, 2 * i + 2)
                        pe.wait_ge(qa_out_d, 2 * i + 2)
                    if h >= 2:
                        pe.wait_ge(lg_masked, n - 1)
                    for c in range(CT):
                        ins = pe.matmul(psx[h % 2][:, 0:P * (i + 1)], q_abs[:, c, h, :], c_kv_t[:, c, 0:P * (i + 1)],
                                        start=(c == 0), stop=(c == CT - 1))
                    ins.then_inc(lg_done, 1)

                def turn(h):
                    n = 8 * i + h
                    pe.wait_ge(prob_done, n + 1)
                    if n >= 2:
                        pe.wait_ge(pt_out, n - 1)
                    for k in range(i + 1):
                        ins = pe.transpose(psx[2 + h % 2][:, P * k:P * k + P], prob[h % 2][:, P * k:P * k + P], ident[:, :])
                    ins.then_inc(pt_done, 1)

                logits(0)
                for h in range(DSA_H):
                    if h + 1 < DSA_H:
                        logits(h + 1)
                    turn(h)
                    if h % 4 == 3:
                        g = h // 4
                        pe.wait_ge(pt_out, 8 * i + h + 1)
                        if 2 * i + g:
                            pe.wait_ge(ol_out_a, 2 * i + g)
                            pe.wait_ge(ol_out_d, 2 * i + g)
                        for c in range(CT):
                            for k in range(i + 1):
                                ins = pe.matmul(psd[c][:, :], c_kv[:, k, P * c:P * c + P],
                                                prob_t[:, k, :, :].rearrange("p h q -> p (h q)"),
                                                start=(k == 0), stop=(k == i))
                            ins.then_inc(pv_done, 1)
                if i == 0:
                    pe.wait_ge(uv_land, 16)
                pe.wait_ge(ol_out_a, 2 * i + 2)
                pe.wait_ge(ol_out_d, 2 * i + 2)
                if i:
                    pe.wait_ge(o_lo, 2 * i)
                for g in range(2):
                    for h in range(4):
                        for c in range(CT):
                            hh = 4 * g + h
                            ins = pe.matmul(psd[2 + g][:, P * h:P * h + P], w_uv_s[:, c, DSA_D * hh:DSA_D * hh + DSA_D],
                                            o_lat[:, c, hh, :], start=(c == 0), stop=(c == CT - 1))
                    ins.then_inc(o_done, 1)

            pe.wait_ge(pt_out, 8 * TT)
            pe.wait_ge(o_lo, 2 * TT)
            for g in range(2):
                for t in range(TT):
                    ins = pe.transpose(psx[g][0:ML_H, P * t:P * t + P],
                                       misc[:, t, MISC - 8 + 4 * g:MISC - 4 + 4 * g], ident[:, :])
                ins.then_inc(g_turned, 1)
            nr = (CONV + 1) * 8
            pe.transpose(psx[3][:, 0:nr], conv_rows[:, :], ident[0:nr, 0:nr]).then_inc(c_turned, 1)
            pe.wait_ge(g_sumd, 1)
            pe.wait_ge(g_em, 1)
            for t in range(TT):
                pe.transpose(psx[2][:, 4 * t:4 * t + 4], rows[4][:, P * t:P * t + P], ident[0:ML_H, 0:ML_H])
                ins = pe.transpose(psx[2][:, 16 + 4 * t:20 + 4 * t], rows[6][:, P * t:P * t + P], ident[0:ML_H, 0:ML_H])
            ins.then_inc(g_tok, 1)
            pe.wait_ge(g_pick, 1)
            pe.wait_ge(g_tok_out, 2)
            pe.wait_ge(c_out, 1)
            for h in range(ML_H):
                if h >= 2:
                    pe.wait_ge(m_exp, 4 * (h - 1))
                pe.matmul(psx[h % 2][:, :], pick_row[:, h, :], rows[5][:, :], start=True, stop=True).then_inc(m_row, 1)
                if h == 0:
                    pe.wait_ge(silu_done, 8)
                for j in range(TT):
                    n = 4 * h + j
                    if n >= 2:
                        pe.wait_ge(m_p, n - 1)
                    pe.matmul(psx[2 + n % 2][:, 0:T - P * j], qk_t[:, ML_H + h, P * j:P * j + P], qk_t[:, h, P * j:T],
                              start=True, stop=True).then_inc(m_qk, 1)
                pe.wait_ge(m_p, 4 * h + 4)
                if h:
                    pe.wait_ge(m_hs, 4 * h)
                if h >= 2:
                    pe.wait_ge(m_den, h - 1)
                for i in range(TT):
                    o = psd[i // 2][:, 256 * (i % 2):256 * (i % 2) + 256]
                    for j in range(i + 1):
                        pe.matmul(o, p_ml[:, j, P * i:P * i + P], proj_n[:, j, ML_V * h:ML_V * h + ML_V],
                                  start=(j == 0), stop=(j == i))
                    for j in range(i + 1):
                        ins = pe.matmul(psd[2 + h % 2][:, i:i + 1], p_ml[:, j, P * i:P * i + P], ones_col[:, :],
                                        start=(j == 0), stop=(j == i))
                    ins.then_inc(m_pv, 1)
            for t in range(TT):
                pe.wait_ge(m_norm, t + 1)
            for f in range(8):
                if f >= 4:
                    pe.wait_ge(m_lo, f - 3)
                for t in range(TT):
                    ins = pe.transpose(psx[f % 4][:, P * t:P * t + P], hs[:, t, P * f:P * f + P], ident[:, :])
                ins.then_inc(m_turned, 1)
            pe.wait_ge(m_lo, 8)
            dense("out", "tokens")
            turn_norm("x", xs)
            pe.wait_ge(n_lo, 4 * NORM_AT["mem"])
            dense("cq", "features")
            turn_norm("mem", mem_xs)
            pe.wait_ge(n_lo, 4 * NORM_AT["ffn"])
            dense("k", "features", N_MEM)
            dense("v", "halves")

            for m in range(4):
                pe.wait_ge(bank_free[m], first["co"])

            def x_logits(n):
                h, i = n // TT, n % TT
                if n >= 2:
                    pe.wait_ge(x_exp, n - 1)
                for d in range(4):
                    ins = pe.matmul(psx[n % 2][:, 0:N_MEM], x_q[:, 4 * h + d, P * i:P * i + P], x_k[:, 4 * h + d, :],
                                    start=(d == 0), stop=(d == 3))
                ins.then_inc(xl_done, 1)

            def x_turn(n):
                pe.wait_ge(x_prob, n + 1)
                if n >= 2:
                    pe.wait_ge(xt_out, n - 1)
                for m in range(MT):
                    ins = pe.transpose(psx[2 + n % 2][:, P * m:P * m + P], xp[n % 2][:, P * m:P * m + P], ident[:, :])
                ins.then_inc(xt_done, 1)

            def x_values(h):
                pe.wait_ge(xt_out, TT * h + TT)
                for d in range(4):
                    if h:
                        pe.wait_ge(xo_lo, 4 * (h - 1) + d + 1)
                    for m in range(MT):
                        c = X_D * h + P * d
                        ins = pe.matmul(psd[d][:, :], x_v[:, m, c:c + P], xp_t[:, h % 2, m, :],
                                        start=(m == 0), stop=(m == MT - 1))
                    ins.then_inc(xo_done, 1)

            x_logits(0)
            for n in range(X_H * TT):
                if n + 1 < X_H * TT:
                    x_logits(n + 1)
                x_turn(n)
                if n % TT == TT - 1:
                    x_values(n // TT)
            pe.wait_ge(xo_lo, 16)
            dense("co", "tokens")
            turn_norm("ffn", ffn_xs)
            pe.wait_ge(n_lo, 4 * 14)
            pe.wait_ge(r_land, 4 * 16)
            for t in range(TT):
                for kt in range(KT):
                    ins = pe.matmul(psx[t][:, 0:G + NE], h_t[:, kt, P * t:P * t + P], w_r[:, kt, :],
                                    start=(kt == 0), stop=(kt == KT - 1))
                ins.then_inc(r_done, 1)
            pe.wait_ge(r_chose, 1)
            for t in range(TT):
                for s in range(t + 1):
                    ins = pe.matmul(psx[0][:, NE * t:NE * t + NE], before[:, :] if s == t else ones_sq[:, :],
                                    chose[:, s, :], start=(s == 0), stop=(s == t))
            for s in range(TT):
                ins = pe.matmul(psx[1][:, 0:NE], ones_sq[:, :], chose[:, s, :], start=(s == 0), stop=(s == TT - 1))
            ins.then_inc(r_rank, 1)

            def turn_rows(b):
                wait_alone(pe, xg_land, b * 16 + 16, consts, 2)
                for k in range(KT):
                    ins = pe.transpose(psx[2 + k // 8][:, BLOCK * (k % 8):BLOCK * (k % 8) + BLOCK],
                                       xg[:, k:D:KT], ident[0:BLOCK, 0:BLOCK])
                ins.then_inc(xg_turned, 1)

            def gate_up(b):
                pe.wait_ge(xg_out, b * 2 + 2)
                for q in range(4):
                    for u in range(2):
                        r = 2 * q + u
                        pe.wait_ge(e_land[r], b * 16 + 16)
                        for k in range(4):
                            for f in range(FT):
                                c = 256 * u + BLOCK * f
                                ins = pe.matmul(psx[0][:, c:c + BLOCK],
                                                e_raw[r][:, 512 * k + P * f:512 * k + P * f + P], xg_t[:, 4 * q + k, :],
                                                start=(q == 0 and u == 0 and k == 0 and f == 0),
                                                stop=(q == 3 and k == 3), skip_group_check=True)
                        ins.then_inc(e_used, 1)

            def down(b):
                pe.wait_ge(he_done, b + 1)
                for f in range(FT):
                    pe.wait_ge(e_land[8 + f], b * 16 + 16)
                    for m in range(4):
                        ins = pe.matmul(psd[m][0:BLOCK, :], he[:, f, :], e_raw[8 + f][:, 512 * m:512 * m + 512],
                                        start=(f == 0), stop=(f == FT - 1))
                    ins.then_inc(e_used, 1)

            turn_rows(0)
            gate_up(0)
            turn_rows(1)
            down(0)
            with pe.Fori(1, NE - 1) as b:
                gate_up(b)
                turn_rows(b + 1)
                pe.wait_ge(y_out_a, b * 2)
                pe.wait_ge(y_out_d, b * 2)
                down(b)
            gate_up(NE - 1)
            pe.wait_ge(y_out_a, 2 * (NE - 1))
            pe.wait_ge(y_out_d, 2 * (NE - 1))
            down(NE - 1)
            pe.wait_ge(more_done, 1)
            n_more = pe.value_load(more_i[0:1, MAX_MORE:MAX_MORE + 1], min_val=0, max_val=MAX_MORE)
            with pe.Fori(0, MAX_MORE) as b:
                with pe.If(n_more > b):
                    turn_rows(b + NE)
                    gate_up(b + NE)
                    pe.wait_ge(y_out_a, b * 2 + 2 * NE)
                    pe.wait_ge(y_out_d, b * 2 + 2 * NE)
                    down(b + NE)

        @block.scalar
        def _(act):
            def split(name, i, j):
                b = first[name] + i
                w = SEG_W[name] if j < 8 else SEG_W[NEXT[name]] if SEG_N[name] == 1 or isinstance(i, int) else SEG_W[name]
                act.wait_ge(w_land[j % 4], (b * 2 + (j // 4 + 1)) * 16)
                if j == 9:
                    act.wait_ge(bank_done[3], b + 1)
                elif j >= 2:
                    act.wait_ge(w_used, b * 7 + min(j - 1, 7))
                act.activation(w_hi[j % 2][:, :, 0:w], w_raw[j % 4][:, :, 0:w], ACT.Copy).then_inc(hi_done, 1)

            def dense(name, evac):
                base, n = first[name], SEG_N[name]

                def one(i, top):
                    for j in range(2, top):
                        split(name, i, j)
                    if evac is not None:
                        for m in (0, 2):
                            act.wait_ge(bank_done[m], base + i + 1)
                            evac(i, m).then_inc(bank_free[m], 1)

                if n > 1:
                    with act.Fori(0, n - 1) as i:
                        one(i, 10)
                one(n - 1, 10 if name in NEXT else 8)
                act.wait_ge(bank_done[3], base + n)
                for m in range(4):
                    act.wait_ge(bank_free[m], base + n)

            def norm(name, src, junk_, turned_out):
                n, base = NORM_N[name], NORM_AT[name]
                for t in range(n):
                    src_ready = src(t)
                    if base + t:
                        act.wait_ge(n_sq, base + t)
                    act.activation(junk_[:, :], src_ready, ACT.Square, accum_out=stats[:, 0, t:t + 1]).then_inc(n_sq, 1)
                root(name, n)
                for t in range(n):
                    for g in range(4):
                        q = 4 * (base + t) + g
                        act.wait_ge(n_turned, q + 1)
                        turned_out(t, g)

            def root(name, n):
                k = RSTD_AT[name]
                act.wait_ge(n_var, k + 1)
                act.activation(stats[:, 3, 0:n], stats[:, 1, 0:n], ACT.Sqrt).then_inc(n_sd, 1)

            def turned_to(hi):
                def go(t, g):
                    act.activation(hi[:, 4 * g:4 * g + 4, P * t:P * t + P],
                                   psx[g][:, :].rearrange("p (k n) -> p k n", k=4), ACT.Copy).then_inc(n_hi, 1)
                return go

            def x_tile(t):
                act.wait_ge(x_land[t], 16)
                return x_in[:, t, :]

            for j in range(2):
                split("misc", 0, j)
            norm("mix", x_tile, junk, turned_to(act_hi))

            dense("misc", lambda i, m: act.activation(misc[:, m, :], psd[m][:, 0:MISC], ACT.Copy))
            act.wait_ge(n_xs, 4)
            for t in range(TT):
                if t:
                    act.wait_ge(k_sq, t)
                act.activation(relu_dot[0][:, 0:DSA_C], misc[:, t, 0:DSA_C], ACT.Square,
                               accum_out=stats[:, 0, t:t + 1]).then_inc(k_sq, 1)
            for t in range(TT):
                act.wait_ge(k_sq, TT + t)
                act.activation(relu_dot[0][:, 256:256 + IDX_D], misc[:, t, DSA_C:DSA_C + IDX_D], ACT.Square, scale=2.0,
                               accum_out=stats[:, 0, TT + t:TT + t + 1]).then_inc(k_sq, 1)
            root("kv", 8)
            dense("head_t", lambda i, m: act.activation(proj_t[:, bass.ds(i * 4 + m, 1) if not isinstance(i, int) else
                                                               slice(4 * i + m, 4 * i + m + 1), :], psd[m][:, :], ACT.Copy))
            act.wait_ge(k_turned, 1)
            act.activation(c_kv_t[:, 0, :], psx[0][:, :], ACT.Copy).then_inc(k_out_a, 1)
            act.wait_ge(k_turned, 3)
            act.activation(k_idx_t[:, :], psx[2][:, :], ACT.Copy).then_inc(k_out_a, 1)
            for b in range(4):
                act.wait_ge(uk_turned, b + 1)
                act.activation(w_uk_t[:, 2 * b:2 * b + 2, :], psx[b][:, :].rearrange("p (h c) -> p h c", h=2),
                               ACT.Copy).then_inc(uk_out, 1)
            for n in range(3 * IDX_H):
                i = 1 + n // IDX_H
                act.wait_ge(dot_done, n + 1)
                if n >= 2:
                    act.wait_ge(score_done, n - 1)
                act.activation(relu_dot[n % 2][:, 0:P * (i + 1)], psx[n % 4][:, 0:P * (i + 1)],
                               ACT.Relu).then_inc(relu_done, 1)

            def head_n_out(i, m):
                c = slice(512 * i, 512 * i + 512) if isinstance(i, int) else bass.ds(i * 512, 512)
                return act.activation(proj_n[:, m, c], psd[m][:, :], ACT.Copy)

            dense("head_n", head_n_out)
            for i in range(TT):
                for b in (0, 2):
                    act.wait_ge(qa_done, 4 * i + b + 1)
                    if i:
                        act.wait_ge(lg_done, 8 * i)
                    act.activation(q_abs[:, b // 2, 4 * (b % 2):4 * (b % 2) + 4, :],
                                   psx[b][:, :].rearrange("p (h q) -> p h q", h=4), ACT.Copy).then_inc(qa_out_a, 1)

                def exp(h):
                    n = 8 * i + h
                    act.wait_ge(lg_max, n + 1)
                    c = slice(n % 16, n % 16 + 1)
                    p = prob[h % 2][:, 0:P * (i + 1)]
                    act.activation(p, p, ACT.Exp, bias=head_neg[:, c], accum_out=head_sum[:, c]).then_inc(exp_done, 1)

                def turned(h):
                    n = 8 * i + h
                    act.wait_ge(pt_done, n + 1)
                    if h % 4 == 0 and n:
                        act.wait_ge(pv_done, 2 * (n // 4))
                    act.activation(prob_t[:, 0:i + 1, h % 4, :],
                                   psx[2 + h % 2][:, 0:P * (i + 1)].rearrange("p (k q) -> p k q", k=i + 1),
                                   ACT.Copy).then_inc(pt_out, 1)

                exp(0)
                for h in range(DSA_H):
                    if h + 1 < DSA_H:
                        exp(h + 1)
                    turned(h)
                    if h % 4 == 3:
                        g = h // 4
                        act.wait_ge(pv_done, 2 * (2 * i + g) + 1)
                        if i:
                            act.wait_ge(o_done, 2 * i)
                        act.activation(o_lat[:, 0, 4 * g:4 * g + 4, :], psd[0][:, :].rearrange("p (h q) -> p h q", h=4),
                                       ACT.Copy).then_inc(ol_out_a, 1)
                for g in range(2):
                    act.wait_ge(o_done, 2 * i + g + 1)
                    act.activation(act_hi[:, 4 * g:4 * g + 4, P * i:P * i + P],
                                   psd[2 + g][:, :].rearrange("p (h q) -> p h q", h=4), ACT.Copy).then_inc(o_hi, 1)

            act.wait_ge(g_abs, 1)
            act.activation(rows[2][:, :], rows[2][:, :], ACT.Exp).then_inc(act_own, 1)
            act.wait_ge(act_own, 1)
            act.activation(rows[2][:, :], rows[2][:, :], ACT.Ln, bias=1.0).then_inc(g_ln, 1)
            act.wait_ge(g_sumd, 1)
            act.activation(rows[6][:, :], rows[6][:, :], ACT.Exp, scale=-1.0).then_inc(g_em, 1)
            for f in range(8):
                act.wait_ge(conv_done, f + 1)
                act.activation(qk_t[:, f, :], qk_t[:, f, :], ACT.Silu).then_inc(silu_done, 1)
            act.activation(proj_n[:, :, 1024:2048], proj_n[:, :, 1024:2048], ACT.Sigmoid).then_inc(sig_done, 1)
            act.wait_ge(g_tok_out, 2)
            act.wait_ge(score_done, 3 * IDX_H)

            def decay(h):
                for j in range(TT):
                    n = 4 * h + j
                    act.wait_ge(m_row, h + 1)
                    if n >= 2:
                        act.wait_ge(m_p, n - 1)
                    act.activation(w_exp[n % 2][:, 0:T - P * j], psx[h % 2][:, P * j:T], ACT.Exp, scale=-1.0,
                                   bias=u_tok[:, j, h:h + 1]).then_inc(m_exp, 1)

            decay(0)
            for h in range(ML_H):
                if h + 1 < ML_H:
                    decay(h + 1)
                act.wait_ge(m_den, h + 1)
                for i in range(TT):
                    act.activation(hs[:, i, ML_V * h:ML_V * h + ML_V], psd[i // 2][:, 256 * (i % 2):256 * (i % 2) + 256],
                                   ACT.Copy, scale=den_inv[:, i, h:h + 1]).then_inc(m_hs, 1)
                for i in range(TT):
                    act.wait_ge(m_hs, 4 * h + i + 1)
                    if h or i:
                        act.wait_ge(m_sq, 4 * h + i)
                    act.activation(sq_junk[:, :], hs[:, i, ML_V * h:ML_V * h + ML_V], ACT.Square,
                                   accum_out=stats[:, 0, 4 * h + i:4 * h + i + 1]).then_inc(m_sq, 1)
            root("ml", 16)
            for f in range(8):
                act.wait_ge(m_turned, f + 1)
                act.activation(act_hi[:, 8 + f, :], psx[f % 4][:, :], ACT.Copy).then_inc(m_hi, 1)
            dense("out", None)
            norm("x", lambda t: x_res[:, t, :], ffn_junk, turned_to(act_hi))
            dense("cq", lambda i, m: act.activation(x_q[:, slice(4 * i + m, 4 * i + m + 1) if isinstance(i, int) else
                                                        bass.ds(i * 4 + m, 1), :], psd[m][:, :], ACT.Copy))
            act.wait_ge(mem_land, 16)
            norm("mem", lambda t: mem_in[:, t, :], mem_junk, turned_to(mem_hi))
            dense("k", lambda i, m: act.activation(x_k[:, slice(4 * i + m, 4 * i + m + 1) if isinstance(i, int) else
                                                       bass.ds(i * 4 + m, 1), :], psd[m][:, 0:N_MEM], ACT.Copy))

            def v_out(i, m):
                c = 256 * (m % 2)
                c = slice(512 * i + c, 512 * i + c + 256) if isinstance(i, int) else bass.ds(i * 512 + c, 256)
                return act.activation(x_v[:, m // 2, c], psd[m][:, 0:256], ACT.Copy)

            dense("v", v_out)

            def x_soft(n):
                act.wait_ge(xl_max, n + 1)
                if n >= 2:
                    act.wait_ge(xt_done, n - 1)
                act.activation(xp[n % 2][:, :], psx[n % 2][:, 0:N_MEM], ACT.Exp, scale=float(X_D) ** -0.5,
                               bias=head_neg[:, n:n + 1], accum_out=head_sum[:, n:n + 1]).then_inc(x_exp, 1)

            def x_turned(n):
                h, i = n // TT, n % TT
                act.wait_ge(xt_done, n + 1)
                if i == 0 and h >= 2:
                    act.wait_ge(xo_done, 4 * (h - 1))
                act.activation(xp_t[:, h % 2, :, P * i:P * i + P],
                               psx[2 + n % 2][:, 0:2 * P].rearrange("p (m q) -> p m q", m=2), ACT.Copy).then_inc(xt_out, 1)

            x_soft(0)
            for n in range(X_H * TT):
                if n + 1 < X_H * TT:
                    x_soft(n + 1)
                x_turned(n)
                if n % TT == TT - 1:
                    for d in range(4):
                        k = 4 * (n // TT) + d
                        act.wait_ge(xo_done, k + 1)
                        act.activation(act_hi[:, k, :], psd[d][:, :], ACT.Copy).then_inc(xo_hi, 1)
            dense("co", None)

            def h_out(t, g):
                if g % 2 == 0:
                    act.activation(h_t[:, 4 * g:4 * g + 4, P * t:P * t + P],
                                   psx[g][:, :].rearrange("p (k n) -> p k n", k=4), ACT.Copy).then_inc(n_hi, 1)

            norm("ffn", lambda t: x_res[:, t, :], ffn_junk, h_out)
            for t in range(TT):
                act.wait_ge(r_neg, 1)
                act.activation(g_exp[:, t, :], r_log[:, t, 0:G], ACT.Exp, bias=neg_m[:, 0, t:t + 1],
                               accum_out=g_sum[:, t:t + 1]).then_inc(r_exp, 1)
            for t in range(TT):
                act.wait_ge(r_neg, 2)
                act.activation(e_exp[:, t, :], e_log[:, t, :], ACT.Exp, bias=neg_m[:, 1, t:t + 1]).then_inc(r_exp, 1)

            def rows_out(b):
                act.wait_ge(xg_turned, b + 1)
                if not (isinstance(b, int) and b == 0):
                    act.wait_ge(e_used, b * 12 - 4)
                act.activation(xg_t[:, 0:8, :], psx[2][:, :].rearrange("p (k s) -> p k s", k=8), ACT.Copy).then_inc(xg_out, 1)

            def hidden(b):
                act.wait_ge(e_used, b * 12 + 8)
                act.activation(he_g[:, :, :], psx[0][:, 0:256].rearrange("p (f s) -> p f s", f=FT), ACT.Silu).then_inc(he_silu, 1)

            def y_out(b):
                act.wait_ge(put_copied, b + 1)
                act.wait_ge(e_used, b * 12 + 12)
                for m in (0, 2):
                    act.activation(y_sb[:, 512 * m:512 * m + 512], psd[m][0:BLOCK, :], ACT.Copy,
                                   scale=put_idx[:, 2:3].bitcast(F32)).then_inc(y_out_a, 1)

            rows_out(0)
            with act.Fori(0, NE - 1) as b:
                hidden(b)
                rows_out(b + 1)
                y_out(b)
            hidden(NE - 1)
            y_out(NE - 1)
            act.wait_ge(more_done, 1)
            n_more = act.value_load(more_i[0:1, MAX_MORE:MAX_MORE + 1], min_val=0, max_val=MAX_MORE)
            with act.Fori(0, MAX_MORE) as b:
                with act.If(n_more > b):
                    rows_out(b + NE)
                    hidden(b + NE)
                    y_out(b + NE)
            for t in range(TT):
                act.wait_ge(f_add, 2 * t + 2)
                if t:
                    act.wait_ge(f_sq, t)
                act.activation(xs_f[:, :], x_res[:, t, :], ACT.Square, accum_out=stats[:, 0, t:t + 1]).then_inc(f_sq, 1)
            root("fin", TT)

        @block.vector
        def _(dve):
            own = [0]

            def link(ins):
                own[0] += 1
                ins.then_inc(dve_own, 1)
                dve.wait_ge(dve_own, own[0])

            def split(name, i, j):
                b = first[name] + i
                w = SEG_W[name] if j < 8 else SEG_W[NEXT[name]] if SEG_N[name] == 1 or isinstance(i, int) else SEG_W[name]
                dve.wait_ge(hi_done, b * 8 + (j + 1))
                dve.tensor_tensor(w_lo[j % 2][:, :, 0:w], w_raw[j % 4][:, :, 0:w], w_hi[j % 2][:, :, 0:w].bitcast(F32),
                                  ALU.subtract).then_inc(lo_done, 1)

            def dense(name, evac, banks=(1, 3), beside=None):
                base, n = first[name], SEG_N[name]

                def one(i, top):
                    for j in range(2, top):
                        split(name, i, j)
                        if beside is not None:
                            beside(i, j - 2)
                    for m in banks:
                        dve.wait_ge(bank_done[m], base + i + 1)
                        evac(i, m).then_inc(bank_free[m], 1)

                if n > 1:
                    with dve.Fori(0, n - 1) as i:
                        one(i, 10)
                one(n - 1, 10 if name in NEXT else 8)
                dve.wait_ge(bank_done[3], base + n)
                for m in range(4):
                    dve.wait_ge(bank_free[m], base + n)

            def rstd(name, n, inv):
                k = RSTD_AT[name]
                var, r, t = stats[:, 1, 0:n], stats[:, 2, 0:n], stats[:, 3, 0:n]
                dve.tensor_scalar(var, stats[:, 0, 0:n], inv, EPS, ALU.mult, ALU.add).then_inc(n_var, 1)
                dve.wait_ge(n_sd, k + 1)
                link(dve.reciprocal(r, t))
                link(dve.tensor_tensor(t, r, r, ALU.mult))
                link(dve.tensor_tensor(t, t, var, ALU.mult))
                link(dve.tensor_scalar(t, t, -0.5, 1.5, ALU.mult, ALU.add))
                link(dve.tensor_tensor(r, r, t, ALU.mult))

            def norm(name, src, dst, g, lo, n_gain):
                n, base = NORM_N[name], NORM_AT[name]
                dve.wait_ge(n_sq, base + n)
                rstd(name, n, 1.0 / D)
                dve.wait_ge(gain_land, 16 * n_gain)

                def scale(t):
                    dve.scalar_tensor_tensor(dst[t % 2][:, :], src(t), stats[:, 2, t:t + 1], g[:, :], ALU.mult,
                                             ALU.mult).then_inc(n_xs, 1)

                scale(0)
                for t in range(n):
                    if t + 1 < n:
                        if t >= 1:
                            dve.wait_ge(n_turned, 4 * (base + t))
                            if name == "ffn":
                                dve.wait_ge(h_store[(t + 1) % 2], 16 * ((t + 1) // 2))
                        scale(t + 1)
                    for k in range(4):
                        q = 4 * (base + t) + k
                        if lo is not None:
                            hi_t, lo_t = lo
                            dve.wait_ge(n_hi, q + 1)
                            s = (slice(None), slice(4 * k, 4 * k + 4), slice(P * t, P * t + P))
                            dve.tensor_tensor(lo_t[s], psx[k][:, :].rearrange("p (k n) -> p k n", k=4),
                                              hi_t[s].bitcast(F32), ALU.subtract).then_inc(n_lo, 1)
                        elif k % 2:
                            dve.wait_ge(n_turned, q + 1)
                            dve.wait_ge(n_hi, 4 * base + 2 * t + k // 2 + 1)
                            dve.tensor_copy(h_t[:, 4 * k:4 * k + 4, P * t:P * t + P],
                                            psx[k][:, :].rearrange("p (k n) -> p k n", k=4)).then_inc(n_lo, 2)

            def one_of(i, m):
                return slice(4 * i + m, 4 * i + m + 1) if isinstance(i, int) else bass.ds(i * 4 + m, 1)

            for j in range(2):
                split("misc", 0, j)
            norm("mix", lambda t: x_in[:, t, :], xs, gain, (act_hi, act_lo), 1)
            dense("misc", lambda i, m: dve.tensor_copy(misc[:, m, :], psd[m][:, 0:MISC]))
            dve.wait_ge(k_sq, 8)
            rstd("kv", 8, 1.0 / DSA_C)
            dve.tensor_scalar(idx_w[:, :, :], misc[:, :, DSA_C + IDX_D:DSA_C + IDX_D + IDX_H],
                              float(IDX_H * IDX_D) ** -0.5, None, ALU.mult).then_inc(consts, 1)
            dve.wait_ge(kv_land, 32)
            for t in range(TT):
                dve.scalar_tensor_tensor(c_kv[:, t, :], misc[:, t, 0:DSA_C], stats[:, 2, t:t + 1], kv_gain[:, :],
                                         ALU.mult, ALU.mult).then_inc(k_norm, 1)
                for c in range(2):
                    dve.scalar_tensor_tensor(k_idx_n[:, t, IDX_D * c:IDX_D * c + IDX_D], misc[:, t, DSA_C:DSA_C + IDX_D],
                                             stats[:, 2, TT + t:TT + t + 1], ki_gain[:, :], ALU.mult,
                                             ALU.mult).then_inc(k_norm, 1)
            dense("head_t", lambda i, m: dve.tensor_copy(proj_t[:, one_of(i, m), :], psd[m][:, :]))
            dve.wait_ge(k_turned, 2)
            dve.tensor_copy(c_kv_t[:, 1, :], psx[1][:, :]).then_inc(k_out_d, 1)
            dve.wait_ge(consts, 3)
            for n in range(3 * IDX_H):
                i, h = 1 + n // IDX_H, n % IDX_H
                s = P * (i + 1)
                dve.wait_ge(relu_done, n + 1)
                if h == 0:
                    dve.tensor_scalar(chosen[i][:, :], relu_dot[n % 2][:, 0:s], idx_w[:, i, h:h + 1], None,
                                      ALU.mult).then_inc(score_done, 1)
                else:
                    dve.wait_ge(score_done, n)
                    dve.scalar_tensor_tensor(chosen[i][:, :], relu_dot[n % 2][:, 0:s], idx_w[:, i, h:h + 1],
                                             chosen[i][:, :], ALU.mult, ALU.add).then_inc(score_done, 1)
            dve.wait_ge(score_done, 3 * IDX_H)
            for i in (1, 2, 3):
                link(dve.memset(chosen[i][0:CHUNK, P * (i + 1) - CHUNK:P * (i + 1)], NEG))
            dve.sem_inc(round_done, 1)

            assert TOPK // 8 * 2 == SEG_N["head_n"] * 8

            def best_keys(i, k):
                n = i * 24 + (k // 2 * 6 + k % 2 * 2 + 1)
                for q, c in enumerate((2, 1) if k % 2 else (3,)):
                    wait_alone(dve, round_done, n + 2 * q, score_done, 3 * IDX_H)
                    dve.max(best[:, c, :], chosen[c][:, :]).then_inc(round_done, 1)
                    wait_alone(dve, round_done, n + 2 * q + 1, score_done, 3 * IDX_H)
                    dve.match_replace(out=chosen[c][:, :], in_to_replace=best[:, c, :], in_values=chosen[c][:, :],
                                      imm_value=TAKEN).then_inc(round_done, 1)

            dense("head_n", lambda i, m: dve.tensor_copy(
                proj_n[:, m, slice(512 * i, 512 * i + 512) if isinstance(i, int) else bass.ds(i * 512, 512)], psd[m][:, :]),
                beside=best_keys)
            dve.wait_ge(round_done, 6 * TOPK // 8 + 1)
            for c in (1, 2, 3):
                link(dve.tensor_scalar(chosen[c][:, :], chosen[c][:, :], TAKEN, HIDE, ALU.not_equal, ALU.mult))
            dve.wait_ge(bias_done, 1)
            for i in range(TT):
                for b in (1, 3):
                    dve.wait_ge(qa_done, 4 * i + b + 1)
                    if i:
                        dve.wait_ge(lg_done, 8 * i)
                    dve.tensor_copy(q_abs[:, b // 2, 4 * (b % 2):4 * (b % 2) + 4, :],
                                    psx[b][:, :].rearrange("p (h q) -> p h q", h=4)).then_inc(qa_out_d, 1)
                s = P * (i + 1)
                bias = bias0[:, :] if i < 1 else chosen[i][:, :]

                def masked(h):
                    n = 8 * i + h
                    c = slice(n % 16, n % 16 + 1)
                    dve.wait_ge(lg_done, n + 1)
                    if n >= 2:
                        dve.wait_ge(pt_done, n - 1)
                    dve.tensor_tensor_reduce(out=prob[h % 2][:, 0:s], in0=psx[h % 2][:, 0:s], in1=bias,
                                             scale=float(DSA_D) ** -0.5, scalar=-3.0e38, op0=ALU.add, op1=ALU.max,
                                             accum_out=head_max[:, c]).then_inc(lg_masked, 1)
                    dve.wait_ge(lg_masked, n + 1)
                    dve.tensor_scalar(head_neg[:, c], head_max[:, c], -1.0, None, ALU.mult).then_inc(lg_max, 1)

                def normed(h):
                    n = 8 * i + h
                    c = slice(n % 16, n % 16 + 1)
                    dve.wait_ge(exp_done, n + 1)
                    link(dve.reciprocal(head_inv[:, c], head_sum[:, c]))
                    dve.tensor_scalar(prob[h % 2][:, 0:s], prob[h % 2][:, 0:s], head_inv[:, c], None,
                                      ALU.mult).then_inc(prob_done, 1)

                masked(0)
                for h in range(DSA_H):
                    if h + 1 < DSA_H:
                        masked(h + 1)
                    normed(h)
                    if h % 4 == 3:
                        g = h // 4
                        dve.wait_ge(pv_done, 2 * (2 * i + g) + 2)
                        if i:
                            dve.wait_ge(o_done, 2 * i)
                        dve.tensor_copy(o_lat[:, 1, 4 * g:4 * g + 4, :],
                                        psd[1][:, :].rearrange("p (h q) -> p h q", h=4)).then_inc(ol_out_d, 1)
                for g in range(2):
                    dve.wait_ge(o_hi, 2 * i + g + 1)
                    a = (slice(None), slice(4 * g, 4 * g + 4), slice(P * i, P * i + P))
                    dve.tensor_tensor(act_lo[a], psd[2 + g][:, :].rearrange("p (h q) -> p h q", h=4),
                                      act_hi[a].bitcast(F32), ALU.subtract).then_inc(o_lo, 1)

            dve.wait_ge(g_turned, 2)
            dve.wait_ge(const_land, 5 * 16)
            link(dve.tensor_scalar(rows[0][:, :], psx[0][0:ML_H, :], gate_i[:, :], None, ALU.add))
            link(dve.tensor_scalar(rows[1][:, :], psx[1][0:ML_H, :], gate_f[:, :], None, ALU.add))
            link(dve.tensor_scalar(rows[2][:, :], rows[1][:, :], -1.0, None, ALU.mult))
            dve.tensor_tensor(rows[2][:, :], rows[1][:, :], rows[2][:, :], ALU.min).then_inc(g_abs, 1)
            link(dve.memset(r_ones[:, :], 1.0))
            dve.tensor_copy(pick_row[:, :, :], ident[0:ML_H, 0:ML_H].unsqueeze(2).to_broadcast([ML_H, ML_H, P])).then_inc(g_pick, 1)
            dve.wait_ge(c_turned, 1)
            dve.tensor_copy(conv_t[:, :], psx[3][:, 0:(CONV + 1) * 8]).then_inc(c_out, 1)
            dve.wait_ge(g_ln, 1)
            link(dve.scalar_tensor_tensor(rows[1][:, :], rows[1][:, :], 0.0, rows[2][:, :], ALU.min, ALU.subtract))
            link(dve.tensor_tensor_scan(rows[3][:, :], r_ones[:, :], rows[1][:, :], 0.0, ALU.mult, ALU.add))
            link(dve.tensor_tensor(rows[4][:, :], rows[0][:, :], rows[3][:, :], ALU.subtract))
            link(dve.tensor_tensor_scan(rows[5][:, :], r_ones[:, :], rows[4][:, :], 0.0, ALU.mult, ALU.max))
            dve.tensor_tensor(rows[6][:, :], rows[3][:, :], rows[5][:, :], ALU.add).then_inc(g_sumd, 1)
            dve.wait_ge(g_tok, 1)
            dve.tensor_copy(u_tok[:, :, :], psx[2][:, 0:16].rearrange("p (t h) -> p t h", t=TT)).then_inc(g_tok_out, 1)
            dve.tensor_copy(em_tok[:, :, :], psx[2][:, 16:32].rearrange("p (t h) -> p t h", t=TT)).then_inc(g_tok_out, 1)
            dve.wait_ge(c_out, 1)
            for f in range(8):
                src, dst = proj_t[:, 12 + f, :], qk_t[:, f, :]
                tap = lambda j: conv_t[:, 8 * j + f:8 * j + f + 1]
                link(dve.tensor_scalar(dst, src, tap(3), tap(4), ALU.mult, ALU.add))
                for j in (2, 1):
                    s = 3 - j
                    link(dve.scalar_tensor_tensor(dst[:, s:T], src[:, 0:T - s], tap(j), dst[:, s:T], ALU.mult, ALU.add))
                dve.scalar_tensor_tensor(dst[:, 3:T], src[:, 0:T - 3], tap(0), dst[:, 3:T], ALU.mult,
                                         ALU.add).then_inc(conv_done, 1)
            dve.wait_ge(g_tok_out, 2)

            def weigh(h):
                for j in range(TT):
                    n = 4 * h + j
                    dve.wait_ge(m_qk, n + 1)
                    dve.wait_ge(m_sel, n + 1)
                    if j == 0 and h:
                        dve.wait_ge(m_pv, 4 * h)
                    dve.scalar_tensor_tensor(p_ml[:, j, P * j:T], psx[2 + n % 2][:, 0:T - P * j], float(ML_K) ** -0.5,
                                             w_exp[n % 2][:, 0:T - P * j], ALU.mult, ALU.mult).then_inc(m_p, 1)

            for h in range(ML_H):
                weigh(h)
                dve.wait_ge(m_pv, 4 * h + 4)
                den = psd[2 + h % 2][:, 0:TT]
                link(dve.scalar_tensor_tensor(den_inv[:, :, h], den, -1.0, em_tok[:, :, h], ALU.mult, ALU.max))
                link(dve.tensor_tensor(den_inv[:, :, h], den, den_inv[:, :, h], ALU.max))
                dve.reciprocal(den_inv[:, :, h], den_inv[:, :, h]).then_inc(m_den, 1)
            dve.wait_ge(m_sq, 16)
            rstd("ml", 16, 1.0 / ML_V)
            dve.wait_ge(ml_land, 16)
            dve.wait_ge(sig_done, 1)
            for i in range(TT):
                for h in range(ML_H):
                    c = slice(ML_V * h, ML_V * h + ML_V)
                    link(dve.scalar_tensor_tensor(hs[:, i, c], hs[:, i, c], stats[:, 2, 4 * h + i:4 * h + i + 1],
                                                  ml_gain[:, c], ALU.mult, ALU.mult))
                dve.tensor_tensor(hs[:, i, :], hs[:, i, :], proj_n[:, i, 1024:2048], ALU.mult).then_inc(m_norm, 1)
            for f in range(8):
                dve.wait_ge(m_hi, f + 1)
                dve.tensor_tensor(act_lo[:, 8 + f, :], psx[f % 4][:, :], act_hi[:, 8 + f, :].bitcast(F32),
                                  ALU.subtract).then_inc(m_lo, 1)

            def add_res(i, m):
                c = slice(512 * i, 512 * i + 512) if isinstance(i, int) else bass.ds(i * 512, 512)
                return dve.tensor_tensor(x_res[:, m, c], psd[m][:, :], x_res[:, m, c], ALU.add)

            dve.wait_ge(res_land, 16)
            dense("out", add_res, banks=(0, 1, 2, 3))
            norm("x", lambda t: x_res[:, t, :], xs, gain, (act_hi, act_lo), 2)
            dense("cq", lambda i, m: dve.tensor_copy(x_q[:, one_of(i, m), :], psd[m][:, :]))
            dve.wait_ge(mem_land, 16)
            norm("mem", lambda t: mem_in[:, t, :], mem_xs, mem_gain, (mem_hi, mem_lo), 3)
            dense("k", lambda i, m: dve.tensor_copy(x_k[:, one_of(i, m), :], psd[m][:, 0:N_MEM]))

            def v_out(i, m):
                c = 256 * (m % 2)
                c = slice(512 * i + c, 512 * i + c + 256) if isinstance(i, int) else bass.ds(i * 512 + c, 256)
                return dve.tensor_copy(x_v[:, m // 2, c], psd[m][:, 0:256])

            dense("v", v_out)

            def x_max(n):
                dve.wait_ge(xl_done, n + 1)
                link(dve.tensor_reduce(head_max[:, n:n + 1], psx[n % 2][:, 0:N_MEM], AX.X, ALU.max))
                dve.tensor_scalar(head_neg[:, n:n + 1], head_max[:, n:n + 1], -float(X_D) ** -0.5, None,
                                  ALU.mult).then_inc(xl_max, 1)

            x_max(0)
            for n in range(X_H * TT):
                if n + 1 < X_H * TT:
                    x_max(n + 1)
                dve.wait_ge(x_exp, n + 1)
                link(dve.reciprocal(head_inv[:, n:n + 1], head_sum[:, n:n + 1]))
                dve.tensor_scalar(xp[n % 2][:, :], xp[n % 2][:, :], head_inv[:, n:n + 1], None,
                                  ALU.mult).then_inc(x_prob, 1)
                if n % TT == TT - 1:
                    for d in range(4):
                        k = 4 * (n // TT) + d
                        dve.wait_ge(xo_hi, k + 1)
                        dve.tensor_tensor(act_lo[:, k, :], psd[d][:, :], act_hi[:, k, :].bitcast(F32),
                                          ALU.subtract).then_inc(xo_lo, 1)
            dense("co", add_res, banks=(0, 1, 2, 3))
            norm("ffn", lambda t: x_res[:, t, :], ffn_xs, gain, None, 4)

            def spread(ap, shape, axis):
                return ap.unsqueeze(axis).to_broadcast(shape)

            dve.wait_ge(r_land, 64)
            dve.wait_ge(route_consts, 2)
            for t in range(TT):
                dve.wait_ge(r_done, t + 1)
                link(dve.tensor_tensor(r_log[:, t, :], psx[t][:, 0:G + NE], r_bias[:, :], ALU.add))
                link(dve.tensor_copy(g_log8[:, t, 0:G], r_log[:, t, 0:G]))
                link(dve.max(g_top[:, t, :], g_log8[:, t, :]))
                link(dve.max_index(g_idx[:, t, :], g_top[:, t, :], g_log8[:, t, :]))
            dve.tensor_scalar(neg_m[:, 0, :], g_top[:, :, 0], -1.0, None, ALU.mult).then_inc(r_neg, 1)
            link(dve.tensor_copy(g_sel[:, :], g_idx[:, :, 0]))
            link(dve.tensor_tensor(g_oh[:, :, :], spread(iota_e[:, 0:G], [P, TT, G], 1),
                                   spread(g_sel[:, :], [P, TT, G], 2), ALU.is_equal))
            for t in range(TT):
                link(dve.tensor_tensor(e_mul[:, t, :, :], r_log[:, t, G:G + NE].rearrange("p (g e) -> p g e", g=G),
                                       spread(g_oh[:, t, :], [P, G, EG], 2), ALU.mult))
            link(dve.tensor_reduce(e_log[:, :, :], e_mul[:, :, :, :].rearrange("p t g e -> p t e g"), AX.X, ALU.add))
            for t in range(TT):
                link(dve.max(e_top[:, t, :], e_log[:, t, :]))
            dve.tensor_scalar(neg_m[:, 1, :], e_top[:, :, 0], -1.0, None, ALU.mult).then_inc(r_neg, 1)
            dve.wait_ge(r_exp, 8)
            for t in range(TT):
                link(dve.max(e_best[:, t, :], e_exp[:, t, :]))
                link(dve.max_index(e_idx[:, t, :], e_best[:, t, :], e_exp[:, t, :]))
            link(dve.tensor_copy(e_id[:, :, :], e_idx[:, :, 0:2]))
            link(dve.scalar_tensor_tensor(e_id[:, :, :], spread(g_sel[:, :], [P, TT, 2], 2), float(EG), e_id[:, :, :],
                                          ALU.mult, ALU.add))
            link(dve.tensor_tensor(e_den[:, :], e_best[:, :, 0], e_best[:, :, 1], ALU.add))
            link(dve.tensor_tensor(e_den[:, :], e_den[:, :], g_sum[:, :], ALU.mult))
            link(dve.reciprocal(e_den[:, :], e_den[:, :]))
            link(dve.tensor_tensor(gate[:, :, :], e_best[:, :, 0:2], spread(e_den[:, :], [P, TT, 2], 2), ALU.mult))
            for t in range(TT):
                link(dve.tensor_tensor(one_hot[:, t, :, :], spread(iota_e[:, :], [P, 2, NE], 1),
                                       spread(e_id[:, t, :], [P, 2, NE], 2), ALU.is_equal))
            dve.tensor_tensor(chose[:, :, :], one_hot[:, :, 0, :], one_hot[:, :, 1, :], ALU.add).then_inc(r_chose, 1)
            dve.wait_ge(r_rank, 1)
            link(dve.tensor_copy(rank[:, :, :], psx[0][:, 0:TT * NE].rearrange("p (t e) -> p t e", t=TT)))
            link(dve.tensor_copy(count[:, :], psx[1][:, 0:NE]))
            link(dve.tensor_tensor(full[:, :, :], spread(count[:, :], [P, NE, 8], 2), spread(iota_m[:, :], [P, NE, 8], 1),
                                   ALU.is_gt))
            link(dve.tensor_reduce(more[:, :], full[:, :, :], AX.X, ALU.add))
            link(dve.tensor_tensor_scan(more_end[:, :], ones32[:, :], more[:, :], 0.0, ALU.mult, ALU.add))
            link(dve.tensor_tensor(more_at[:, :], more_end[:, :], more[:, :], ALU.subtract))
            link(dve.tensor_tensor(more_cmp[:, :, :], spread(iota_b[:, :], [1, MAX_MORE, NE], 2),
                                   spread(more_end[0:1, :], [1, MAX_MORE, NE], 1), ALU.is_ge))
            link(dve.tensor_reduce(more_f[:, 0:MAX_MORE], more_cmp[:, :, :], AX.X, ALU.add))
            link(dve.tensor_scalar(more_f[:, 0:MAX_MORE], more_f[:, 0:MAX_MORE], float(NE - 1), None, ALU.min))
            link(dve.tensor_copy(more_f[:, MAX_MORE:MAX_MORE + 1], more_end[0:1, NE - 1:NE]))
            dve.tensor_copy(more_i[:, :], more_f[:, :]).then_inc(more_done, 1)
            for src, dst in ((rank, pos), (more_at, pos_at)):
                for t in range(TT):
                    s = spread(src[:, t, :] if src is rank else src[:, :], [P, 2, NE], 1)
                    link(dve.tensor_tensor(picked[:, t, :, :], one_hot[:, t, :, :], s, ALU.mult))
                link(dve.tensor_reduce(dst[:, :, :], picked[:, :, :, :], AX.X, ALU.add))
            for t in range(TT):
                link(dve.tensor_tensor(pos_full[:, t, :, :], spread(pos[:, t, :], [P, 2, 8], 2),
                                       spread(iota_m[:, :], [P, 2, 8], 1), ALU.is_ge))
            link(dve.tensor_reduce(pos_q[:, :, :], pos_full[:, :, :, :], AX.X, ALU.add))
            link(dve.tensor_tensor(row_f[:, :, :], pos_at[:, :, :], pos_q[:, :, :], ALU.add))
            link(dve.tensor_scalar(row_f[:, :, :], row_f[:, :, :], float(NE - 1), None, ALU.add))
            link(dve.tensor_tensor(row_f[:, :, :], row_f[:, :, :], e_id[:, :, :], ALU.subtract))
            link(dve.tensor_scalar(row_t[:, :, :], pos_q[:, :, :], 0.0, None, ALU.is_gt))
            link(dve.tensor_tensor(row_f[:, :, :], row_f[:, :, :], row_t[:, :, :], ALU.mult))
            link(dve.tensor_tensor(row_f[:, :, :], row_f[:, :, :], e_id[:, :, :], ALU.add))
            link(dve.tensor_tensor(row_f[:, :, :], row_f[:, :, :], pos_q[:, :, :], ALU.subtract))
            link(dve.scalar_tensor_tensor(row_f[:, :, :], row_f[:, :, :], float(BLOCK), pos[:, :, :], ALU.mult, ALU.add))
            link(dve.tensor_copy(slot_new[:, :, :, 0:2], tok_f[:, :, :, :]))
            link(dve.tensor_copy(slot_new[:, :, :, 2].bitcast(F32), gate[:, :, :]))
            dve.tensor_copy(row_i[:, :, :], row_f[:, :, :]).then_inc(r_row, 1)

            def rows_out(b):
                dve.wait_ge(xg_turned, b + 1)
                if not (isinstance(b, int) and b == 0):
                    dve.wait_ge(e_used, b * 12 - 4)
                dve.tensor_copy(xg_t[:, 8:16, :], psx[3][:, :].rearrange("p (k s) -> p k s", k=8)).then_inc(xg_out, 1)

            def hidden(b):
                dve.wait_ge(he_silu, b + 1)
                dve.tensor_tensor(he[:, :, :], psx[0][:, 256:512].rearrange("p (f s) -> p f s", f=FT), he_g[:, :, :],
                                  ALU.mult).then_inc(he_done, 1)

            def y_out(b):
                dve.wait_ge(put_copied, b + 1)
                dve.wait_ge(e_used, b * 12 + 12)
                for m in (1, 3):
                    dve.tensor_scalar(y_sb[:, 512 * m:512 * m + 512], psd[m][0:BLOCK, :], put_idx[:, 2:3].bitcast(F32),
                                      None, ALU.mult).then_inc(y_out_d, 1)

            rows_out(0)
            with dve.Fori(0, NE - 1) as b:
                hidden(b)
                rows_out(b + 1)
                y_out(b)
            hidden(NE - 1)
            y_out(NE - 1)
            n_more = dve.value_load(more_i[0:1, MAX_MORE:MAX_MORE + 1], min_val=0, max_val=MAX_MORE)
            with dve.Fori(0, MAX_MORE) as b:
                with dve.If(n_more > b):
                    rows_out(b + NE)
                    hidden(b + NE)
                    y_out(b + NE)
            for t in range(TT):
                dve.wait_ge(back_land, 16 * (t + 1))
                for k in range(2):
                    dve.tensor_tensor(x_res[:, t, :], x_res[:, t, :], y_back[:, k, :], ALU.add).then_inc(f_add, 1)
                    dve.wait_ge(f_add, 2 * t + k + 1)
            dve.wait_ge(f_sq, TT)
            rstd("fin", TT, 1.0 / D)
            dve.wait_ge(fg_land, 16)
            for t in range(TT):
                if t >= 2:
                    dve.wait_ge(f_store[t % 2], 16 * (t // 2))
                dve.scalar_tensor_tensor(fin_o[t % 2][:, :], x_res[:, t, :], stats[:, 2, t:t + 1], fin_gain[:, :],
                                         ALU.mult, ALU.mult).then_inc(f_out, 1)


_INS = ["x", "mem", "norm_mix_g", "w_in", "kv_norm_g", "k_idx_norm_g", "w_uk", "w_uv", "conv_w", "conv_b", "gate_b",
        "ml_norm_g", "w_out", "norm_x_g", "mem_norm_g", "w_cq", "w_ckv", "w_co", "norm_ffn_g", "w_group", "b_group",
        "w_router", "b_router", "w_gate", "w_up", "w_down", "final_norm_g"]
_OUTS = [((1, T, D), "float32")]


def _w_in_columns(w):
    sizes = [DSA_H * DSA_D, DSA_C, IDX_H * IDX_D, IDX_D, IDX_H, ML_H * ML_K, ML_H * ML_K, ML_H * ML_V, ML_H, ML_H,
             ML_H * ML_V]
    dq, ckv, qi, ki, wi, mq, mk, mv, mi, mf, mo = np.split(np.asarray(w), np.cumsum(sizes)[:-1], axis=-1)
    return np.concatenate([ckv, ki, wi, mi, mf, dq, qi, mq, mk, mv, mo], axis=-1)


def kernel(**inputs):
    import concourse.bacc as _bacc
    from concourse import mybir as _mybir
    from concourse.bass_utils import run_bass_kernel_spmd as _run

    nc = _bacc.Bacc("TRN2", target_bir_lowering=False, num_devices=1)
    arrays, args = {}, []
    for name in _INS:
        a = _w_in_columns(inputs[name]) if name == "w_in" else inputs[name]
        a = np.ascontiguousarray(a)
        arrays[f"in_{name}_dram"] = a
        args.append(nc.dram_tensor(f"in_{name}_dram", a.shape, _mybir.dt.from_np(a.dtype), kind="ExternalInput").ap())
    for i, (shape, dtype) in enumerate(_OUTS):
        dt = _mybir.dt.from_np(np.dtype(dtype))
        args.append(nc.dram_tensor(f"out_{i}_dram", shape, dt, kind="ExternalOutput").ap())
    layer(nc, *args)
    r = _run(nc, [arrays], core_ids=[0])
    return r.results[0]["out_0_dram"]
```

```python
from contextlib import ExitStack

import numpy as np

import concourse.bass as bass
from concourse import mybir

F32 = mybir.dt.float32
F32R = mybir.dt.float32r
I32 = mybir.dt.int32
U32 = mybir.dt.uint32
ALU = mybir.AluOpType
ACT = mybir.ActivationFunctionType
AX = mybir.AxisListType

P = 128
EPS = 1e-6
T, D = 512, 2048
TT = T // P
KT = D // P
CHUNK = 64
N_MEM = 256
MT = N_MEM // P
DSA_H, DSA_D, DSA_C = 8, 128, 256
CT = DSA_C // P
IDX_H, IDX_D = 8, 64
TOPK = min(256, T // 4)
ML_H, ML_K, ML_V = 4, 128, 256
CONV = 4
X_H, X_D = 4, D // 4
G, EG = 4, 8
NE = G * EG
F = 512
FT = F // P
BLOCK = 64
MAX_MORE = (2 * T - 1) // BLOCK
NB = NE + MAX_MORE
OUT_OF_RANGE = 1 << 20
NEG = -1.0e38
TAKEN = -3.0e38
HIDE = -1.0e30
MISC = DSA_C + IDX_D + IDX_H + 2 * ML_H

KB = 1024
BASE = 16512


def layer(nc, x, mem, norm_mix_g, w_in, kv_norm_g, k_idx_norm_g, w_uk, w_uv, conv_w, conv_b, gate_b,
          ml_norm_g, w_out, norm_x_g, mem_norm_g, w_cq, w_ckv, w_co, norm_ffn_g, w_group, b_group,
          w_router, b_router, w_gate, w_up, w_down, final_norm_g, out):
    with ExitStack() as ctx:
        def at(name, shape, off_kb, dt=F32):
            return nc.alloc_sbuf_tensor_at(name, shape, dt, offset=BASE + int(off_kb * KB))

        def sem(name):
            return ctx.enter_context(nc.semaphore(name))

        w_raw = [at(f"w_raw{r}", [P, 2, 512], 4 * r) for r in range(4)]
        w_hi = [at(f"w_hi{r}", [P, 2, 512], 16 + 4 * r, F32R) for r in range(2)]
        w_lo = [at(f"w_lo{r}", [P, 2, 512], 24 + 4 * r, F32R) for r in range(2)]
        act_hi = at("act_hi", [P, KT, T], 32, F32R)
        act_lo = at("act_lo", [P, KT, T], 64, F32R)
        proj_t = at("proj_t", [P, 20, T], 96)
        proj_n = at("proj_n", [P, TT, 2048], 136)
        misc = at("misc", [P, TT, MISC], 168)
        gain = at("gain", [P, D], 174)
        x_in = at("x_in", [P, TT, D], 96)
        xs = [at(f"xs{r}", [P, D], 182 + 8 * r) for r in range(2)]
        junk = at("junk", [P, D], 136)

        w_uk_raw = at("w_uk_raw", [P, CT, 1024], 144)
        w_uk_t = at("w_uk_t", [P, DSA_H, DSA_C], 182)
        c_kv = at("c_kv", [P, TT, DSA_C], 190)
        c_kv_t = at("c_kv_t", [P, CT, T], 194)
        k_idx_t = at("k_idx_t", [P, T], 198)
        relu_dot = [at(f"relu_dot{r}", [P, T], 174 + 2 * r) for r in range(2)]
        k_idx_n = at("k_idx_n", [P, TT, 2 * IDX_D], 178)
        kv_gain = at("kv_gain", [P, DSA_C], 180)
        ki_gain = at("ki_gain", [P, IDX_D], 181)
        sq_junk = at("sq_junk", [P, ML_V], 200)
        w_uv_s = at("w_uv_s", [P, CT, 1024], 174)
        q_abs = at("q_abs", [P, CT, DSA_H, P], 48)
        prob = [at(f"prob{r}", [P, T], (56, 58, 61)[r]) for r in range(3)]
        bias0 = at("bias0", [P, P], 60)
        prob_t = at("prob_t", [P, TT, 4, P], 80)
        o_lat = at("o_lat", [P, CT, DSA_H, P], 88)

        w_exp = [at(f"w_exp{r}", [P, T], 112 + 2 * r) for r in range(2)]
        pick_row = at("pick_row", [ML_H, ML_H, P], 116)
        hs = at("hs", [P, TT, ML_H * ML_V], 96)
        p_ml = at("p_ml", [P, TT, T], 182)
        ml_gain = at("ml_gain", [P, ML_H * ML_V], 190)
        rows = [at(f"rows{r}", [ML_H, T], kb) for r, kb in enumerate((140, 142, 148, 150, 180, 198, 178))]
        r_ones = at("r_ones", [ML_H, T], 156)

        x_res = at("x_res", [P, TT, D], 136)
        x_q = at("x_q", [P, KT, T], 96)
        mem_in = at("mem_in", [P, MT, D], 184)
        mem_hi = at("mem_hi", [P, KT, N_MEM], 32, F32R)
        mem_lo = at("mem_lo", [P, KT, N_MEM], 48, F32R)
        mem_gain = at("mem_gain", [P, D], 168)
        mem_xs = [at(f"mem_xs{r}", [P, D], 128 + 48 * r) for r in range(2)]
        sq_part_junk = at("sq_part_junk", [P, 512], 134)
        x_k = at("x_k", [P, KT, N_MEM], 168)
        x_v = at("x_v", [P, MT, D], 184)
        xp = [at(f"xp{r}", [P, N_MEM], 200 + r) for r in range(3)]
        xp_t = at("xp_t", [P, 2, MT, T], 128)

        e_raw = [at(f"e_raw{r}", [P, 2048], 8 * r) for r in range(6)]
        e_hi = [at(f"e_hi{r}", [P, 2048], 48 + 8 * r, F32R) for r in range(3)]
        e_lo = [at(f"e_lo{r}", [P, 2048], 72 + 8 * r, F32R) for r in range(3)]
        h_t = at("h_t", [P, KT, T], 96)
        xg = at("xg", [BLOCK, D], 96)
        y_sb = at("y_sb", [BLOCK, D], 104)
        xt_hi = at("xt_hi", [P, KT, BLOCK], 112, F32R)
        xt_lo = at("xt_lo", [P, KT, BLOCK], 116, F32R)
        he_g = at("he_g", [BLOCK, F], 120)
        he = at("he", [BLOCK, F], 122)
        he_hi = at("he_hi", [P, FT, BLOCK], 124, F32R)
        he_lo = at("he_lo", [P, FT, BLOCK], 125, F32R)
        ffn_xs = [at(f"ffn_xs{r}", [P, D], 182 + 8 * r) for r in range(2)]
        w_r = at("w_r", [P, KT, 64], 168)
        r_log_t = at("r_log_t", [64, T], 172)
        fin_gain = at("fin_gain", [P, D], 174)
        y_back = [at(f"y_back{t}", [P, 2, D], 16 * t) for t in range(TT)]
        xs_f = at("xs_f", [P, D], 128)
        fin_o = [at(f"fin_o{r}", [P, D], 112 + 8 * r) for r in range(2)]

        low = [204.0]

        def small(name, shape, dt=F32):
            n = int(np.prod(shape[1:])) * 4
            t = at(name, shape, low[0], dt)
            low[0] += ((n + 31) // 32 * 32) / KB
            assert BASE + low[0] * KB <= nc.sbuf_usable_end, (name, low[0])
            return t

        ident = small("ident", [P, P])
        ones_col = small("ones_col", [P, 1])
        sq_part = small("sq_part", [P, TT, 4])
        stats = small("stats", [P, 4, 16])
        idx_w = small("idx_w", [P, TT, IDX_H])
        head_max = small("head_max", [P, 16])
        head_neg = small("head_neg", [P, 16])
        head_sum = small("head_sum", [P, 16])
        head_inv = small("head_inv", [P, 16])
        best = small("best", [P, TT, 8])
        chosen = [None, small("chosen1", [P, 2 * P]), at("chosen2", [P, 3 * P], 202), at("chosen3", [P, 4 * P], 200)]
        conv_t = small("conv_t", [P, (CONV + 1) * 8])
        conv_rows = small("conv_rows", [(CONV + 1) * 8, P])
        gate_i = small("gate_i", [ML_H, 1])
        gate_f = small("gate_f", [ML_H, 1])
        u_tok = small("u_tok", [P, TT, ML_H])
        em_tok = small("em_tok", [P, TT, ML_H])
        den_inv = small("den_inv", [P, TT, ML_H])
        assert low[0] < 207.8

        psd = [ctx.enter_context(nc.psum_tensor(f"psd{m}", [P, 512], F32)) for m in range(4)]
        psx = [ctx.enter_context(nc.psum_tensor(f"psx{m}", [P, 512], F32)) for m in range(4)]
        low[0] = 198.0
        before = small("before", [P, P])
        ones_sq = small("ones_sq", [P, P])
        slot_none = small("slot_none", [2 * NB, BLOCK // 2 * 4], I32)
        slot_new = small("slot_new", [P, TT, 2, 4], I32)
        slots = small("slots", [BLOCK, NB, 4], I32)
        take_idx = small("take_idx", [BLOCK, 4], I32)
        put_idx = small("put_idx", [BLOCK, 4], I32)
        tok_f = small("tok_f", [P, TT, 2, 2])
        ones32 = small("ones32", [P, NE])
        iota_e = small("iota_e", [P, NE])
        iota_m = small("iota_m", [P, 8])
        iota_b = small("iota_b", [1, MAX_MORE])
        r_bias = small("r_bias", [P, G + NE])
        more_i = small("more_i", [1, MAX_MORE + 1], I32)
        g_log8 = small("g_log8", [P, TT, 8])
        assert low[0] <= 204.0, low

        low[0] = 128.0
        r_log = small("r_log", [P, TT, G + NE])
        g_top = small("g_top", [P, TT, 8])
        g_idx = small("g_idx", [P, TT, 8], U32)
        g_sel = small("g_sel", [P, TT])
        g_oh = small("g_oh", [P, TT, G])
        g_exp = small("g_exp", [P, TT, G])
        g_sum = small("g_sum", [P, TT])
        e_mul = small("e_mul", [P, TT, G, EG])
        e_log = small("e_log", [P, TT, EG])
        e_top = small("e_top", [P, TT, 8])
        e_exp = small("e_exp", [P, TT, EG])
        e_best = small("e_best", [P, TT, 8])
        e_idx = small("e_idx", [P, TT, 8], U32)
        neg_m = small("neg_m", [P, 2, TT])
        e_id = small("e_id", [P, TT, 2])
        e_den = small("e_den", [P, TT])
        gate = small("gate", [P, TT, 2])
        one_hot = small("one_hot", [P, TT, 2, NE])
        chose = small("chose", [P, TT, NE])
        assert low[0] <= 136.0, low
        low[0] = 174.0
        rank = small("rank", [P, TT, NE])
        picked = small("picked", [P, TT, 2, NE])
        count = small("count", [P, NE])
        full = small("full", [P, NE, 8])
        more = small("more", [P, NE])
        more_end = small("more_end", [P, NE])
        more_at = small("more_at", [P, NE])
        pos = small("pos", [P, TT, 2])
        pos_at = small("pos_at", [P, TT, 2])
        pos_q = small("pos_q", [P, TT, 2])
        pos_full = small("pos_full", [P, TT, 2, 8])
        row_f = small("row_f", [P, TT, 2])
        row_t = small("row_t", [P, TT, 2])
        row_i = small("row_i", [P, TT, 2], I32)
        more_f = small("more_f", [1, MAX_MORE + 1])
        more_cmp = small("more_cmp", [1, MAX_MORE, NE])
        assert low[0] <= 182.0, low

        h_rows = nc.dram_tensor("h_rows", (T, D), F32, kind="Internal").ap()
        y_rows = nc.dram_tensor("y_rows", (2 * T, D), F32, kind="Internal").ap()
        slot_rows = nc.dram_tensor("slot_rows", (NB * BLOCK, 4), I32, kind="Internal").ap()

        x_land = [sem(f"x_land{t}") for t in range(TT)]
        gain_land = sem("gain_land")
        const_land = sem("const_land")
        kv_land = sem("kv_land")
        uv_land = sem("uv_land")
        ml_land = sem("ml_land")
        res_land = sem("res_land")
        mem_land = sem("mem_land")
        w_land = [sem(f"w_land{r}") for r in range(4)]
        hi_done = sem("hi_done")
        lo_done = sem("lo_done")
        w_used = sem("w_used")
        bank_done = [sem(f"bank_done{m}") for m in range(4)]
        bank_free = [sem(f"bank_free{m}") for m in range(4)]
        dve_own = sem("dve_own")
        act_own = sem("act_own")
        pool_own = sem("pool_own")
        consts = sem("consts")
        q_sq, n_sq, n_var, n_sd, n_xs = sem("q_sq"), sem("n_sq"), sem("n_var"), sem("n_sd"), sem("n_xs")
        n_turned, n_hi, n_lo = sem("n_turned"), sem("n_hi"), sem("n_lo")
        k_sq, k_norm, k_turned, k_out_a, k_out_d = (sem(s) for s in (
            "k_sq", "k_norm", "k_turned", "k_out_a", "k_out_d"))
        uk_turned, uk_out = sem("uk_turned"), sem("uk_out")
        dot_done, relu_done, score_done, round_done = (sem(s) for s in (
            "dot_done", "relu_done", "score_done", "round_done"))
        bias_done = sem("bias_done")
        qa_done, qa_out_a, qa_out_d = sem("qa_done"), sem("qa_out_a"), sem("qa_out_d")
        lg_done, lg_masked, lg_max, exp_done, prob_done = (sem(s) for s in (
            "lg_done", "lg_masked", "lg_max", "exp_done", "prob_done"))
        pt_done, pt_out, pv_done, ol_out_a, ol_out_d, o_done, o_hi, o_lo = (sem(s) for s in (
            "pt_done", "pt_out", "pv_done", "ol_out_a", "ol_out_d", "o_done", "o_hi", "o_lo"))
        g_turned, g_abs, g_ln, g_sumd, g_em, g_pick, g_tok, g_tok_out = (sem(s) for s in (
            "g_turned", "g_abs", "g_ln", "g_sumd", "g_em", "g_pick", "g_tok", "g_tok_out"))
        c_turned, c_out, conv_done, silu_done = (sem(s) for s in (
            "c_turned", "c_out", "conv_done", "silu_done"))
        m_row, m_exp, m_sel, m_qk, m_p, m_pv, m_den, m_hs, m_sq, m_norm, m_turned, m_hi, m_lo = (
            sem("m_" + s) for s in ("row", "exp", "sel", "qk", "p", "pv", "den", "hs", "sq", "norm",
                                    "turned", "hi", "lo"))
        xl_done, xl_max, x_exp, x_prob, xt_done, xt_out, xo_done, xo_hi, xo_lo = (
            sem(s) for s in ("xl_done", "xl_max", "x_exp", "x_prob", "xt_done", "xt_out", "xo_done",
                             "xo_hi", "xo_lo"))
        r_land, r_done, r_out, r_back, r_chose, r_neg, r_exp, r_rank, r_row, none_land, slot_store, slot_land = (
            sem(s) for s in ("r_land", "r_done", "r_out", "r_back", "r_chose", "r_neg", "r_exp", "r_rank",
                             "r_row", "none_land", "slot_store", "slot_land"))
        more_done, route_consts = sem("more_done"), sem("route_consts")
        e_land = [sem(f"e_land{r}") for r in range(6)]
        e_hi_done, e_lo_done, e_used = sem("e_hi_done"), sem("e_lo_done"), sem("e_used")
        xg_zero, xg_land, xg_turned, xt_high, xg_out = (sem(s) for s in (
            "xg_zero", "xg_land", "xg_turned", "xt_high", "xg_out"))
        he_silu, he_done, he_turned, he_split_a, he_split_d, y_out_a, y_out_d, y_store = (sem(s) for s in (
            "he_silu", "he_done", "he_turned", "he_split_a", "he_split_d", "y_out_a", "y_out_d", "y_store"))
        take_copied, put_copied, put_used, experts_done = (sem(s) for s in (
            "take_copied", "put_copied", "put_used", "experts_done"))
        back_land = [sem(f"back_land{t}") for t in range(TT)]
        f_add, f_sq, f_out = (sem(s) for s in ("f_add", "f_sq", "f_out"))
        h_store = [sem(f"h_store{r}") for r in range(2)]
        f_store = [sem(f"f_store{r}") for r in range(2)]
        fg_land = sem("fg_land")

        SEGS = [("misc", 1, MISC), ("head_t", 5, 512), ("head_n", 4, 512), ("out", 4, 512),
                ("cq", 4, 512), ("k", 4, 512), ("v", 4, 512), ("co", 4, 512)]
        first = {}
        blocks = 0
        for name, n, _ in SEGS:
            first[name] = blocks
            blocks += n
        SEG_N = {name: n for name, n, _ in SEGS}
        SEG_W = {name: w for name, _, w in SEGS}
        NEXT = {a[0]: b[0] for a, b in zip(SEGS, SEGS[1:])}
        w_in_v = w_in[0].rearrange("(k p) n -> p k n", p=P)
        ckv_v = w_ckv[0].rearrange("(k p) n -> p k n", p=P)
        SEG_SRC = {
            "misc": (w_in_v, 0), "head_t": (w_in_v, MISC), "head_n": (w_in_v, MISC + 5 * 512),
            "out": (w_out[0].rearrange("(k p) n -> p k n", p=P), 0),
            "cq": (w_cq[0].rearrange("(k p) n -> p k n", p=P), 0),
            "k": (ckv_v, 0), "v": (ckv_v, D),
            "co": (w_co[0].rearrange("(k p) n -> p k n", p=P), 0),
        }
        NORM_AT = {"mix": 0, "x": 4, "mem": 8, "ffn": 10}
        SQ_AT = {"out": 1, "x": 1, "co": 1 + 4 * TT, "ffn": 1 + 4 * TT}
        NORM_N = {"mix": 4, "x": 4, "mem": 2, "ffn": 4}
        block = ctx.enter_context(nc.Block())

        def wait_alone(eng, sem_, value, base_sem, base_value):
            if not isinstance(value, int):
                eng.compute_val(value)
            eng.wait_ge(base_sem, base_value)
            eng.wait_ge(sem_, value)

        @block.sync
        def _(sp):
            def piece(name, i, j, wait=True):
                src, c0 = SEG_SRC[name]
                w = SEG_W[name]
                if wait:
                    sp.wait_ge(lo_done, (first[name] + i) * 8 + (j - 3))
                col = i * 512 + c0
                cols = slice(col, col + w) if isinstance(col, int) else bass.ds(col, w)
                sp.dma_start(w_raw[j % 4][:, :, 0:w], src[:, 2 * j:2 * j + 2, cols]).then_inc(w_land[j % 4], 16)

            def stream(name):
                n = SEG_N[name]
                if n > 1:
                    with sp.Fori(0, n - 1) as i:
                        for j in range(4, 8):
                            piece(name, i, j)
                        for j in range(4):
                            piece(name, i + 1, j)
                for j in range(4, 8):
                    piece(name, n - 1, j)
                if name in NEXT:
                    for j in range(4):
                        piece(NEXT[name], 0, j)

            sp.dma_start(gain[:, :], norm_mix_g[0:1, :].to_broadcast([P, D])).then_inc(gain_land, 16)
            for t in range(TT):
                sp.dma_start(x_in[:, t, :], x[0, t * P:(t + 1) * P, :]).then_inc(x_land[t], 16)
            for j in range(4):
                piece("misc", 0, j, wait=False)
            sp.dma_start(w_uk_raw[:, :, :], w_uk[0].rearrange("(c p) h d -> p c (h d)", p=P)).then_inc(const_land, 16)
            sp.dma_start(conv_rows[0:CONV * 8, :], conv_w[0].rearrange("j (f p) -> (j f) p", p=P)).then_inc(const_land, 16)
            sp.dma_start(conv_rows[CONV * 8:(CONV + 1) * 8, :],
                         conv_b[0].rearrange("(f p) -> f p", p=P)).then_inc(const_land, 16)
            gb = gate_b.rearrange("a (k g) -> g (a k)", k=2)
            sp.dma_start(gate_i[:, :], gb[:, 0:1]).then_inc(const_land, 16)
            sp.dma_start(gate_f[:, :], gb[:, 1:2]).then_inc(const_land, 16)
            sp.wait_ge(n_xs, 4)
            sp.dma_start(kv_gain[:, :], kv_norm_g[0:1, :].to_broadcast([P, DSA_C])).then_inc(kv_land, 16)
            sp.dma_start(ki_gain[:, :], k_idx_norm_g[0:1, :].to_broadcast([P, IDX_D])).then_inc(kv_land, 16)
            stream("misc")
            stream("head_t")
            stream("head_n")
            sp.wait_ge(bias_done, 1)
            sp.wait_ge(g_tok_out, 2)
            sp.wait_ge(silu_done, 8)
            sp.dma_start(w_uv_s[:, :, :], w_uv[0].rearrange("(c p) h d -> p c (h d)", p=P)).then_inc(uv_land, 16)
            sp.wait_ge(o_done, 2 * TT)
            sp.dma_start(ml_gain[:, :], ml_norm_g[0:1, :].to_broadcast([P, ML_H * ML_V])).then_inc(ml_land, 16)
            sp.wait_ge(m_norm, TT)
            sp.dma_start(x_res[:, :, :], x[0].rearrange("(t p) d -> p t d", p=P)).then_inc(res_land, 16)
            sp.dma_start(gain[:, :], norm_x_g[0:1, :].to_broadcast([P, D])).then_inc(gain_land, 16)
            stream("out")
            sp.wait_ge(n_turned, 4 * NORM_AT["mem"])
            sp.dma_start(mem_gain[:, :], mem_norm_g[0:1, :].to_broadcast([P, D])).then_inc(gain_land, 16)
            sp.dma_start(mem_in[:, :, :], mem[0].rearrange("(t p) d -> p t d", p=P)).then_inc(mem_land, 16)
            stream("cq")
            stream("k")
            stream("v")
            sp.wait_ge(xl_done, 16)
            for m in (0, 2):
                sp.wait_ge(bank_free[m], first["co"])
            sp.wait_ge(xo_done, 16)
            sp.dma_start(gain[:, :], norm_ffn_g[0:1, :].to_broadcast([P, D])).then_inc(gain_land, 16)
            sp.dma_start(w_r[:, :, 0:G], w_group[0].rearrange("(k p) g -> p k g", p=P)).then_inc(r_land, 16)
            sp.dma_start(w_r[:, :, G:G + NE], w_router[0].rearrange("(k p) g -> p k g", p=P)).then_inc(r_land, 16)
            sp.dma_start(r_bias[:, 0:G], b_group[0:1, :].to_broadcast([P, G])).then_inc(r_land, 16)
            sp.dma_start(r_bias[:, G:G + NE], b_router[0:1, :].to_broadcast([P, NE])).then_inc(r_land, 16)
            sp.wait_ge(route_consts, 1)
            sp.dma_start(slot_rows.rearrange("(p n) c -> p (n c)", p=2 * NB), slot_none[:, :]).then_inc(none_land, 16)
            stream("co")
            sp.wait_ge(bank_done[3], blocks)

            def expert_piece(e, r):
                one_e = slice(e, e + 1) if isinstance(e, int) else bass.ds(e, 1)
                if r < 8:
                    w, q = (w_gate, w_up)[r // 4][0], r % 4
                    src = w[one_e].rearrange("e (p k) f -> p (e k) f", k=KT)[:, 4 * q:4 * q + 4, :]
                    dst = e_raw[r % 6][:, :].rearrange("p (k f) -> p k f", k=4)
                else:
                    src = w_down[0][one_e].rearrange("e f d -> (e f) d")[P * (r - 8):P * (r - 7), :]
                    dst = e_raw[r % 6][:, :]
                sp.dma_start(dst, src).then_inc(e_land[r % 6], 16)

            def expert(b, e):
                for r in range(12):
                    sp.wait_ge(e_lo_done, b * 12 + (r - 5))
                    expert_piece(e, r)

            def store_rows(t):
                sp.wait_ge(n_xs, NORM_AT["ffn"] + t + 1)
                sp.dma_start(h_rows[t * P:(t + 1) * P, :], ffn_xs[t % 2][:, :]).then_inc(h_store[t % 2], 16)

            for r in range(6):
                expert_piece(0, r)
                if r < TT:
                    store_rows(r)
            for r in range(6, 9):
                sp.wait_ge(e_lo_done, r - 5)
                expert_piece(0, r)
            sp.wait_ge(slot_store, 16 * 2 * TT)
            sp.dma_start(slots[:, :, :], slot_rows.rearrange("(b s) c -> s b c", s=BLOCK)).then_inc(slot_land, 16)
            sp.dma_start(fin_gain[:, :], final_norm_g.rearrange("(a d) -> a d", a=1).to_broadcast([P, D])).then_inc(fg_land, 16)
            for r in range(9, 12):
                sp.wait_ge(e_lo_done, r - 5)
                expert_piece(0, r)
            with sp.Fori(1, NE) as e:
                expert(e, e)
            sp.wait_ge(more_done, 1)
            n_more = sp.value_load(more_i[0:1, MAX_MORE:MAX_MORE + 1], min_val=0, max_val=MAX_MORE)
            with sp.If(n_more > 0):
                with sp.Fori(0, MAX_MORE) as b:
                    with sp.If(n_more > b):
                        expert(b + NE, sp.value_load(more_i[0:1, bass.ds(b, 1)], min_val=0, max_val=NE - 1))
            sp.wait_ge(experts_done, 1)
            for t in range(TT):
                sp.dma_start(y_back[t][:, :, :],
                             y_rows.rearrange("(k t p) d -> t p k d", k=2, p=P)[t]).then_inc(back_land[t], 16)
            for t in range(TT):
                sp.wait_ge(f_out, t + 1)
                sp.dma_start(out[0, t * P:(t + 1) * P, :], fin_o[t % 2][:, :]).then_inc(f_store[t % 2], 16)
            for r in range(2):
                sp.wait_ge(f_store[r], 16 * TT // 2)

        @block.gpsimd
        def _(pool):
            pool.memset(ident[:, :], 0.0).then_inc(pool_own, 1)
            pool.memset(ones_col[:, :], 1.0).then_inc(consts, 1)
            pool.wait_ge(pool_own, 1)
            pool.affine_select(out=ident[:, :], in_=ident[:, :], compare_op=ALU.not_equal, fill=1.0, base=0,
                               pattern=[[-1, P]], channel_multiplier=1).then_inc(consts, 1)
            pool.wait_ge(bank_done[3], first["out"])
            pool.memset(bias0[:, :], 0.0).then_inc(pool_own, 1)
            pool.wait_ge(pool_own, 2)
            pool.memset(bias0[0:CHUNK, CHUNK:P], HIDE).then_inc(bias_done, 1)
            for n in range(4 * ML_H):
                pool.wait_ge(m_exp, n + 1)
                w = w_exp[n % 2][:, 0:P]
                pool.affine_select(out=w, in_=w, compare_op=ALU.is_ge, fill=0.0, base=0,
                                   pattern=[[1, P]], channel_multiplier=-1).then_inc(m_sel, 1)
            pool.wait_ge(xo_done, 16)
            pool.wait_ge(x_prob, 16)
            pool.memset(slot_none[:, :], OUT_OF_RANGE).then_inc(route_consts, 1)
            pool.memset(before[:, :], 1.0).then_inc(pool_own, 1)
            pool.memset(w_r[:, :, G + NE:64], 0.0).then_inc(pool_own, 1)
            pool.memset(ones_sq[:, :], 1.0).then_inc(pool_own, 1)
            pool.memset(ones32[:, :], 1.0).then_inc(pool_own, 1)
            pool.memset(slot_new[:, :, :, :], 0).then_inc(pool_own, 1)
            pool.iota(iota_e[:, :], [[1, NE]], base=0, channel_multiplier=0,
                      allow_small_or_imprecise_dtypes=True).then_inc(pool_own, 1)
            pool.iota(iota_m[:, :], [[BLOCK, 8]], base=BLOCK, channel_multiplier=0,
                      allow_small_or_imprecise_dtypes=True).then_inc(pool_own, 1)
            pool.iota(iota_b[:, :], [[1, MAX_MORE]], base=0, channel_multiplier=0,
                      allow_small_or_imprecise_dtypes=True).then_inc(pool_own, 1)
            pool.iota(tok_f[:, :, :, 0], [[P, TT], [0, 2]], base=0, channel_multiplier=1,
                      allow_small_or_imprecise_dtypes=True).then_inc(pool_own, 1)
            pool.iota(tok_f[:, :, :, 1], [[P, TT], [T, 2]], base=0, channel_multiplier=1,
                      allow_small_or_imprecise_dtypes=True).then_inc(pool_own, 1)
            pool.memset(g_log8[:, :, :], NEG).then_inc(pool_own, 1)
            pool.wait_ge(pool_own, 13)
            pool.affine_select(out=before[:, :], in_=before[:, :], compare_op=ALU.is_gt, fill=0.0, base=0,
                               pattern=[[1, P]], channel_multiplier=-1).then_inc(route_consts, 1)
            pool.wait_ge(r_done, TT)
            pool.memset(xg[:, :], 0.0).then_inc(xg_zero, 1)
            pool.wait_ge(none_land, 16)
            pool.wait_ge(r_row, 1)
            for t in range(TT):
                for k in range(2):
                    pool.indirect_dma_start(
                        out=slot_rows[:, :], out_offset=bass.IndirectOffsetOnAxis(ap=row_i[:, t, k:k + 1], axis=0),
                        in_=slot_new[:, t, k, :], in_offset=None,
                        bounds_check=NB * BLOCK - 1, oob_is_err=False).then_inc(slot_store, 16)
            pool.wait_ge(slot_land, 16)
            for r in range(2):
                pool.wait_ge(h_store[r], 16 * TT // 2)
            col = lambda b: bass.ds(b, 1) if not isinstance(b, int) else slice(b, b + 1)

            def take(b):
                if not (isinstance(b, int) and b == 0):
                    pool.wait_ge(xg_turned, b)
                pool.tensor_copy(take_idx[:, :], slots[:, col(b), :].rearrange("s b c -> s (b c)")).then_inc(take_copied, 1)
                wait_alone(pool, take_copied, b + 1, slot_land, 16)
                pool.indirect_dma_start(
                    out=xg[:, :], out_offset=None, in_=h_rows[:, :],
                    in_offset=bass.IndirectOffsetOnAxis(ap=take_idx[:, 0:1], axis=0),
                    bounds_check=T - 1, oob_is_err=False).then_inc(xg_land, 16)

            def put(b):
                if not (isinstance(b, int) and b == 0):
                    wait_alone(pool, y_store, b * 16, slot_land, 16)
                pool.tensor_copy(put_idx[:, :], slots[:, col(b), :].rearrange("s b c -> s (b c)")).then_inc(put_copied, 1)
                pool.wait_ge(put_copied, b + 1)
                wait_alone(pool, y_out_a, b * 2 + 2, slot_land, 16)
                pool.wait_ge(y_out_d, b * 2 + 2)
                pool.indirect_dma_start(
                    out=y_rows[:, :], out_offset=bass.IndirectOffsetOnAxis(ap=put_idx[:, 1:2], axis=0),
                    in_=y_sb[:, :], in_offset=None,
                    bounds_check=2 * T - 1, oob_is_err=False).then_inc(y_store, 16)

            pool.wait_ge(xg_zero, 1)
            take(0)
            take(1)
            put(0)
            with pool.Fori(1, NE - 1) as b:
                take(b + 1)
                put(b)
            put(NE - 1)
            pool.wait_ge(more_done, 1)
            n_more = pool.value_load(more_i[0:1, MAX_MORE:MAX_MORE + 1], min_val=0, max_val=MAX_MORE)
            with pool.If(n_more > 0):
                with pool.Fori(0, MAX_MORE) as b:
                    with pool.If(n_more > b):
                        take(b + NE)
                        put(b + NE)
            pool.wait_ge(y_store, n_more * 16 + 16 * NE)
            pool.sem_inc(experts_done, 1)

        @block.tensor
        def _(pe):
            def dense(name, mode, n_tok=512):
                base, n, w = first[name], SEG_N[name], SEG_W[name]
                hi, lo = (mem_hi, mem_lo) if name in ("k", "v") else (act_hi, act_lo)

                def one(i):
                    b = base + i
                    for j in range(8):
                        pe.wait_ge(lo_done, b * 8 + (j + 1))
                        for m in range(4):
                            for kk in range(2):
                                kt = 2 * j + kk
                                if kt == 0 and not (isinstance(b, int) and b == 0):
                                    pe.wait_ge(bank_free[m], b)
                                wh, wl = w_hi[j % 2][:, kk, :], w_lo[j % 2][:, kk, :]
                                if mode == "features":
                                    o = psd[m][:, 0:n_tok]
                                    c = slice(P * m, P * m + P)
                                    pairs = [(wh[:, c], hi[:, kt, 0:n_tok]), (wh[:, c], lo[:, kt, 0:n_tok]),
                                             (wl[:, c], hi[:, kt, 0:n_tok])]
                                elif mode == "tokens":
                                    o = psd[m][:, 0:w]
                                    c = slice(P * m, P * m + P)
                                    pairs = [(hi[:, kt, c], wh[:, 0:w]), (hi[:, kt, c], wl[:, 0:w]),
                                             (lo[:, kt, c], wh[:, 0:w])]
                                else:
                                    o = psd[m][:, 0:256]
                                    c = slice(P * (m // 2), P * (m // 2) + P)
                                    v = slice(256 * (m % 2), 256 * (m % 2) + 256)
                                    pairs = [(hi[:, kt, c], wh[:, v]), (hi[:, kt, c], wl[:, v]),
                                             (lo[:, kt, c], wh[:, v])]
                                for q, (a, c) in enumerate(pairs):
                                    ins = pe.matmul(o, a, c, start=(kt == 0 and q == 0), stop=(kt == KT - 1 and q == 2))
                                if kt == KT - 1:
                                    ins.then_inc(bank_done[m], 1)
                        if j < 7:
                            ins.then_inc(w_used, 1)

                if n == 1:
                    one(0)
                else:
                    with pe.Fori(0, n) as i:
                        one(i)

            def turn_norm(name, src, tiles=None):
                for t in tiles or range(NORM_N[name]):
                    pe.wait_ge(n_xs, NORM_AT[name] + t + 1)
                    for g in range(4):
                        q = 4 * (NORM_AT[name] + t) + g
                        if q >= 4:
                            pe.wait_ge(n_lo, q - 3)
                        for k in range(4):
                            kt = 4 * g + k
                            ins = pe.transpose(psx[g][:, P * k:P * k + P], src[t % 2][:, kt * P:kt * P + P], ident[:, :])
                        ins.then_inc(n_turned, 1)

            pe.wait_ge(consts, 2)
            turn_norm("mix", xs)
            pe.wait_ge(n_lo, 16)
            dense("misc", "tokens")
            dense("head_t", "features")

            pe.wait_ge(k_norm, 3 * TT)
            for c in range(CT):
                for t in range(TT):
                    ins = pe.transpose(psx[c][:, P * t:P * t + P], c_kv[:, t, P * c:P * c + P], ident[:, :])
                ins.then_inc(k_turned, 1)
            for t in range(TT):
                ins = pe.transpose(psx[2][:, P * t:P * t + P], k_idx_n[:, t, :], ident[:, :])
            ins.then_inc(k_turned, 1)
            pe.wait_ge(const_land, 5 * 16)
            nr = (CONV + 1) * 8
            pe.transpose(psx[3][:, 0:nr], conv_rows[:, :], ident[0:nr, 0:nr]).then_inc(c_turned, 1)
            for b in range(4):
                if b == 0:
                    pe.wait_ge(k_out_a, 2)
                if b == 1:
                    pe.wait_ge(k_out_d, 1)
                if b == 3:
                    pe.wait_ge(c_out, 1)
                for h in range(2):
                    for c in range(CT):
                        d0 = (2 * b + h) * DSA_D
                        ins = pe.transpose(psx[b][:, DSA_C * h + P * c:DSA_C * h + P * c + P],
                                           w_uk_raw[:, c, d0:d0 + DSA_D], ident[:, :])
                ins.then_inc(uk_turned, 1)
            for m in range(4):
                pe.wait_ge(bank_free[m], first["head_n"])
            for n in range(3 * IDX_H):
                i, h = 1 + n // IDX_H, n % IDX_H
                if n < 4:
                    pe.wait_ge(uk_out, n + 1)
                else:
                    pe.wait_ge(relu_done, n - 3)
                r = slice(IDX_D * (h % 2), IDX_D * (h % 2) + IDX_D)
                pe.matmul(psx[n % 4][:, 0:P * (i + 1)], proj_t[r, 8 + h // 2, P * i:P * i + P],
                          k_idx_t[r, 0:P * (i + 1)], start=True, stop=True).then_inc(dot_done, 1)
            pe.wait_ge(relu_done, 3 * IDX_H)
            for g in range(2):
                for t in range(TT):
                    ins = pe.transpose(psx[g][0:ML_H, P * t:P * t + P],
                                       misc[:, t, MISC - 8 + 4 * g:MISC - 4 + 4 * g], ident[:, :])
                ins.then_inc(g_turned, 1)
            dense("head_n", "tokens")
            pe.wait_ge(g_sumd, 1)
            pe.wait_ge(g_em, 1)
            for t in range(TT):
                pe.transpose(psx[2][:, 4 * t:4 * t + 4], rows[4][:, P * t:P * t + P], ident[0:ML_H, 0:ML_H])
                ins = pe.transpose(psx[2][:, 16 + 4 * t:20 + 4 * t], rows[6][:, P * t:P * t + P], ident[0:ML_H, 0:ML_H])
            ins.then_inc(g_tok, 1)
            pe.wait_ge(g_tok_out, 2)

            pe.wait_ge(g_abs, 1)
            pe.wait_ge(silu_done, 8)
            for m in range(4):
                pe.wait_ge(bank_free[m], first["out"])
            def q_latent(i):
                if i:
                    pe.wait_ge(lg_masked, 8 * i)
                for b in range(4):
                    c, g = b // 2, b % 2
                    for h in range(4):
                        ins = pe.matmul(psx[b][:, P * h:P * h + P], w_uk_t[:, 4 * g + h, P * c:P * c + P],
                                        proj_t[:, 4 * g + h, P * i:P * i + P], start=True, stop=True)
                    ins.then_inc(qa_done, 1)

            def logits(i, h):
                n = 8 * i + h
                if h == 0:
                    pe.wait_ge(qa_out_a, 2 * i + 2)
                    pe.wait_ge(qa_out_d, 2 * i + 2)
                if h >= 4:
                    pe.wait_ge(lg_masked, n - 3)
                for c in range(CT):
                    ins = pe.matmul(psx[h % 4][:, 0:P * (i + 1)], q_abs[:, c, h, :], c_kv_t[:, c, 0:P * (i + 1)],
                                    start=(c == 0), stop=(c == CT - 1))
                ins.then_inc(lg_done, 1)

            def turn(i, h):
                n = 8 * i + h
                pe.wait_ge(prob_done, n + 1)
                if n >= 2:
                    pe.wait_ge(pt_out, n - 1)
                if i and h < 2:
                    pe.wait_ge(o_lo, 2 * (i - 1) + h + 1)
                for k in range(i + 1):
                    ins = pe.transpose(psd[2 + h % 2][:, P * k:P * k + P], prob[n % 3][:, P * k:P * k + P], ident[:, :])
                ins.then_inc(pt_done, 1)

            def values(i, g):
                pe.wait_ge(pt_out, 8 * i + 4 * g + 4)
                if 2 * i + g:
                    pe.wait_ge(ol_out_a, 2 * i + g)
                    pe.wait_ge(ol_out_d, 2 * i + g)
                for c in range(CT):
                    for k in range(i + 1):
                        ins = pe.matmul(psd[c][:, :], c_kv[:, k, P * c:P * c + P],
                                        prob_t[:, k, :, :].rearrange("p h q -> p (h q)"),
                                        start=(k == 0), stop=(k == i))
                    ins.then_inc(pv_done, 1)

            def outputs(i):
                if i == 0:
                    pe.wait_ge(uv_land, 16)
                pe.wait_ge(ol_out_a, 2 * i + 2)
                pe.wait_ge(ol_out_d, 2 * i + 2)
                for g in range(2):
                    for h in range(4):
                        for c in range(CT):
                            hh = 4 * g + h
                            ins = pe.matmul(psd[2 + g][:, P * h:P * h + P], w_uv_s[:, c, DSA_D * hh:DSA_D * hh + DSA_D],
                                            o_lat[:, c, hh, :], start=(c == 0), stop=(c == CT - 1))
                    ins.then_inc(o_done, 1)

            q_latent(0)
            for i in range(TT):
                logits(i, 0)
                logits(i, 1)
                for h in range(DSA_H):
                    if h + 2 < DSA_H:
                        logits(i, h + 2)
                    turn(i, h)
                    if h == 4:
                        values(i, 0)
                if i + 1 < TT:
                    q_latent(i + 1)
                values(i, 1)
                outputs(i)

            pe.wait_ge(o_lo, 2 * TT)
            pe.wait_ge(g_pick, 1)
            for h in range(ML_H):
                if h >= 2:
                    pe.wait_ge(m_exp, 4 * (h - 1))
                pe.matmul(psx[h % 2][:, :], pick_row[:, h, :], rows[5][:, :], start=True, stop=True).then_inc(m_row, 1)
                for j in range(TT):
                    n = 4 * h + j
                    if n >= 2:
                        pe.wait_ge(m_p, n - 1)
                    pe.matmul(psx[2 + n % 2][:, 0:T - P * j], proj_t[:, 16 + h, P * j:P * j + P], proj_t[:, 12 + h, P * j:T],
                              start=True, stop=True).then_inc(m_qk, 1)
                pe.wait_ge(m_p, 4 * h + 4)
                if h:
                    pe.wait_ge(m_hs, 4 * h)
                if h >= 2:
                    pe.wait_ge(m_den, h - 1)
                for i in range(TT):
                    o = psd[i // 2][:, 256 * (i % 2):256 * (i % 2) + 256]
                    for j in range(i + 1):
                        pe.matmul(o, p_ml[:, j, P * i:P * i + P], proj_n[:, j, ML_V * h:ML_V * h + ML_V],
                                  start=(j == 0), stop=(j == i))
                    for j in range(i + 1):
                        ins = pe.matmul(psd[2 + h % 2][:, i:i + 1], p_ml[:, j, P * i:P * i + P], ones_col[:, :],
                                        start=(j == 0), stop=(j == i))
                    ins.then_inc(m_pv, 1)
            for t in range(TT):
                pe.wait_ge(m_norm, t + 1)
            for f in range(8):
                if f >= 4:
                    pe.wait_ge(m_lo, f - 3)
                for t in range(TT):
                    ins = pe.transpose(psx[f % 4][:, P * t:P * t + P], hs[:, t, P * f:P * f + P], ident[:, :])
                ins.then_inc(m_turned, 1)
            pe.wait_ge(m_lo, 8)
            dense("out", "tokens")
            turn_norm("x", xs)
            pe.wait_ge(n_lo, 4 * NORM_AT["mem"])
            dense("cq", "features")
            turn_norm("mem", mem_xs)
            pe.wait_ge(n_lo, 4 * NORM_AT["ffn"])
            dense("k", "features", N_MEM)
            dense("v", "halves")

            for m in range(4):
                pe.wait_ge(bank_free[m], first["co"])

            def x_logits(n):
                h, i = n // TT, n % TT
                if n >= 3:
                    pe.wait_ge(x_exp, n - 2)
                for d in range(4):
                    ins = pe.matmul(psx[n % 3][:, 0:N_MEM], x_q[:, 4 * h + d, P * i:P * i + P], x_k[:, 4 * h + d, :],
                                    start=(d == 0), stop=(d == 3))
                ins.then_inc(xl_done, 1)

            def x_turn(n):
                pe.wait_ge(x_prob, n + 1)
                if n >= 1:
                    pe.wait_ge(xt_out, n)
                for m in range(MT):
                    ins = pe.transpose(psx[3][:, P * m:P * m + P], xp[n % 3][:, P * m:P * m + P], ident[:, :])
                ins.then_inc(xt_done, 1)

            def x_values(h):
                pe.wait_ge(xt_out, TT * h + TT)
                for d in range(4):
                    if h:
                        pe.wait_ge(xo_lo, 4 * (h - 1) + d + 1)
                    for m in range(MT):
                        c = X_D * h + P * d
                        ins = pe.matmul(psd[d][:, :], x_v[:, m, c:c + P], xp_t[:, h % 2, m, :],
                                        start=(m == 0), stop=(m == MT - 1))
                    ins.then_inc(xo_done, 1)

            x_logits(0)
            x_logits(1)
            for n in range(X_H * TT):
                if n + 2 < X_H * TT:
                    x_logits(n + 2)
                x_turn(n)
                if n and n % TT == 0:
                    x_values(n // TT - 1)
            x_values(X_H - 1)
            pe.wait_ge(xo_lo, 16)
            dense("co", "tokens")

            def route(t):
                pe.wait_ge(n_lo, 4 * (NORM_AT["ffn"] + t + 1))
                for kt in range(KT):
                    ins = pe.matmul(psd[t][0:64, 0:P], w_r[:, kt, :], h_t[:, kt, P * t:P * t + P],
                                    start=(kt == 0), stop=(kt == KT - 1))
                ins.then_inc(r_done, 1)

            turn_norm("ffn", ffn_xs, (0, 1))
            pe.wait_ge(r_land, 4 * 16)
            pe.wait_ge(route_consts, 2)
            for t in range(TT):
                route(t)
                if t + 2 < TT:
                    turn_norm("ffn", ffn_xs, (t + 2,))
            for t in range(TT):
                pe.wait_ge(r_out, t + 1)
                pe.transpose(psd[t][:, 256:320], r_log_t[:, P * t:P * t + P], ident[0:64, 0:64]).then_inc(r_back, 1)
            pe.wait_ge(r_chose, 1)
            for t in range(TT):
                for s in range(t + 1):
                    ins = pe.matmul(psx[0][:, NE * t:NE * t + NE], before[:, :] if s == t else ones_sq[:, :],
                                    chose[:, s, :], start=(s == 0), stop=(s == t))
            for s in range(TT):
                ins = pe.matmul(psx[1][:, 0:NE], ones_sq[:, :], chose[:, s, :], start=(s == 0), stop=(s == TT - 1))
            ins.then_inc(r_rank, 1)

            def turn_rows(b):
                wait_alone(pe, xg_land, b * 16 + 16, consts, 2)
                for k in range(KT):
                    ins = pe.transpose(psx[2 + k // 8][:, BLOCK * (k % 8):BLOCK * (k % 8) + BLOCK],
                                       xg[:, k:D:KT], ident[0:BLOCK, 0:BLOCK])
                ins.then_inc(xg_turned, 1)

            def passes(o, x_hi, x_lo, w_hi_, w_lo_, start, stop):
                pe.matmul(o, x_hi, w_hi_, start=start, stop=False)
                pe.matmul(o, x_hi, w_lo_, start=False, stop=False)
                return pe.matmul(o, x_lo, w_hi_, start=False, stop=stop)

            def gate_up(b):
                pe.wait_ge(xg_out, b * 2 + 2)
                for r in range(8):
                    u, q = r // 4, r % 4
                    pe.wait_ge(e_lo_done, b * 12 + (r + 1))
                    for k in range(4):
                        c = slice(512 * k, 512 * k + 512)
                        ins = passes(psx[u][0:BLOCK, :], xt_hi[:, 4 * q + k, :], xt_lo[:, 4 * q + k, :],
                                     e_hi[r % 3][:, c], e_lo[r % 3][:, c], q == 0 and k == 0, q == 3 and k == 3)
                    ins.then_inc(e_used, 1)

            def down(b):
                wait_alone(pe, he_done, b + 1, consts, 2)
                for f in range(FT):
                    ins = pe.transpose(psx[0][:, BLOCK * f:BLOCK * f + BLOCK], he[:, P * f:P * f + P], ident[0:BLOCK, 0:BLOCK])
                ins.then_inc(he_turned, 1)
                if not (isinstance(b, int) and b == 0):
                    pe.wait_ge(y_out_a, b * 2)
                    pe.wait_ge(y_out_d, b * 2)
                pe.wait_ge(he_split_a, b + 1)
                pe.wait_ge(he_split_d, b + 1)
                for f in range(FT):
                    r = 8 + f
                    pe.wait_ge(e_lo_done, b * 12 + (r + 1))
                    for m in range(4):
                        c = slice(512 * m, 512 * m + 512)
                        ins = passes(psd[m][0:BLOCK, :], he_hi[:, f, :], he_lo[:, f, :], e_hi[r % 3][:, c],
                                     e_lo[r % 3][:, c], f == 0, f == FT - 1)
                    ins.then_inc(e_used, 1)

            turn_rows(0)
            gate_up(0)
            turn_rows(1)
            down(0)
            with pe.Fori(1, NE - 1) as b:
                gate_up(b)
                turn_rows(b + 1)
                down(b)
            gate_up(NE - 1)
            down(NE - 1)
            pe.wait_ge(more_done, 1)
            n_more = pe.value_load(more_i[0:1, MAX_MORE:MAX_MORE + 1], min_val=0, max_val=MAX_MORE)
            with pe.If(n_more > 0):
                with pe.Fori(0, MAX_MORE) as b:
                    with pe.If(n_more > b):
                        turn_rows(b + NE)
                        gate_up(b + NE)
                        down(b + NE)

        @block.scalar
        def _(act):
            def split(name, i, j):
                b = first[name] + i
                w = SEG_W[name] if j < 8 else SEG_W[NEXT[name]] if SEG_N[name] == 1 or isinstance(i, int) else SEG_W[name]
                act.wait_ge(w_land[j % 4], (b * 2 + (j // 4 + 1)) * 16)
                if j == 9:
                    act.wait_ge(bank_done[3], b + 1)
                elif j >= 2:
                    act.wait_ge(w_used, b * 7 + min(j - 1, 7))
                act.activation(w_hi[j % 2][:, :, 0:w], w_raw[j % 4][:, :, 0:w], ACT.Copy).then_inc(hi_done, 1)

            def dense(name, evac, behind=None, before_last=None, beside=None, banks=lambda i: (0, 2)):
                base, n = first[name], SEG_N[name]

                def one(i, top):
                    for j in range(2, min(top, 9)):
                        split(name, i, j)
                        if beside is not None:
                            beside(i, j - 2)
                    if evac is not None:
                        for m in banks(i):
                            act.wait_ge(bank_done[m], base + i + 1)
                            evac(i, m).then_inc(bank_free[m], 1)
                    if top > 9:
                        split(name, i, 9)
                        if beside is not None:
                            beside(i, 7)
                    if behind is not None:
                        behind(i)

                if beside is not None:
                    for i in range(n - 1):
                        one(i, 10)
                elif n > 1:
                    with act.Fori(0, n - 1) as i:
                        one(i, 10)
                if before_last is not None:
                    before_last()
                one(n - 1, 10 if name in NEXT else 8)
                act.wait_ge(bank_done[3], base + n)
                for m in range(4):
                    act.wait_ge(bank_free[m], base + n)

            roots = [0]

            def root(c0, n):
                roots[0] += 1
                act.wait_ge(n_var, roots[0])
                act.activation(stats[:, 3, c0:c0 + n], stats[:, 1, c0:c0 + n], ACT.Sqrt).then_inc(n_sd, 1)

            squares = [0]

            def square(src, junk_, t):
                if squares[0]:
                    act.wait_ge(n_sq, squares[0])
                squares[0] += 1
                act.activation(junk_, src, ACT.Square, accum_out=stats[:, 0, t:t + 1]).then_inc(n_sq, 1)

            def turned_tile(name, t, turned_out):
                for g in range(4):
                    act.wait_ge(n_turned, 4 * (NORM_AT[name] + t) + g + 1)
                    turned_out(t, g)

            def part_squares(name):
                def go(i):
                    for m in range(TT):
                        act.wait_ge(bank_free[m], i + (first[name] + 1))
                        c = slice(512 * i, 512 * i + 512) if isinstance(i, int) else bass.ds(i * 512, 512)
                        part = sq_part[:, m, i:i + 1] if isinstance(i, int) else sq_part[:, m, bass.ds(i, 1)]
                        act.wait_ge(q_sq, i * TT + (SQ_AT[name] + m))
                        act.activation(sq_part_junk[:, :], x_res[:, m, c], ACT.Square, accum_out=part).then_inc(q_sq, 1)
                return go

            def turned_to(hi):
                def go(t, g):
                    act.activation(hi[:, 4 * g:4 * g + 4, P * t:P * t + P],
                                   psx[g][:, :].rearrange("p (k n) -> p k n", k=4), ACT.Copy).then_inc(n_hi, 1)
                return go

            for t in range(TT):
                act.wait_ge(x_land[t], 16)
                square(x_in[:, t, :], junk[:, :], t)
                root(t, 1)
                if t:
                    turned_tile("mix", t - 1, turned_to(act_hi))
            for j in range(2):
                split("misc", 0, j)
            turned_tile("mix", TT - 1, turned_to(act_hi))

            dense("misc", lambda i, m: act.activation(misc[:, m, :], psd[m][:, 0:MISC], ACT.Copy))
            act.wait_ge(n_xs, 4)
            for t in range(TT):
                if t:
                    act.wait_ge(k_sq, t)
                act.activation(relu_dot[0][:, 0:DSA_C], misc[:, t, 0:DSA_C], ACT.Square,
                               accum_out=stats[:, 0, t:t + 1]).then_inc(k_sq, 1)
            for t in range(TT):
                act.wait_ge(k_sq, TT + t)
                act.activation(relu_dot[0][:, 256:256 + IDX_D], misc[:, t, DSA_C:DSA_C + IDX_D], ACT.Square, scale=2.0,
                               accum_out=stats[:, 0, TT + t:TT + t + 1]).then_inc(k_sq, 1)
            root(0, 8)
            dense("head_t", lambda i, m: act.activation(proj_t[:, bass.ds(i * 4 + m, 1) if not isinstance(i, int) else
                                                               slice(4 * i + m, 4 * i + m + 1), :], psd[m][:, :], ACT.Copy))
            act.wait_ge(k_turned, 1)
            act.activation(c_kv_t[:, 0, :], psx[0][:, :], ACT.Copy).then_inc(k_out_a, 1)
            act.wait_ge(k_turned, 3)
            act.activation(k_idx_t[:, :], psx[2][:, :], ACT.Copy).then_inc(k_out_a, 1)
            for b in range(4):
                act.wait_ge(uk_turned, b + 1)
                act.activation(w_uk_t[:, 2 * b:2 * b + 2, :], psx[b][:, :].rearrange("p (h c) -> p h c", h=2),
                               ACT.Copy).then_inc(uk_out, 1)
            for n in range(3 * IDX_H):
                i = 1 + n // IDX_H
                act.wait_ge(dot_done, n + 1)
                if n >= 2:
                    act.wait_ge(score_done, n - 1)
                act.activation(relu_dot[n % 2][:, 0:P * (i + 1)], psx[n % 4][:, 0:P * (i + 1)],
                               ACT.Relu).then_inc(relu_done, 1)

            def head_n_out(i, m):
                return act.activation(proj_n[:, m, 512 * i:512 * i + 512], psd[m][:, :], ACT.Copy if i < 2 else ACT.Sigmoid)

            def gates_and_silu(i, k):
                if (i, k) == (0, 2):
                    act.wait_ge(g_abs, 1)
                    act.activation(rows[2][:, :], rows[2][:, :], ACT.Exp).then_inc(act_own, 1)
                    act.wait_ge(act_own, 1)
                    act.activation(rows[2][:, :], rows[2][:, :], ACT.Ln, bias=1.0).then_inc(g_ln, 1)
                if (i, k) == (0, 4):
                    act.wait_ge(g_sumd, 1)
                    act.activation(rows[6][:, :], rows[6][:, :], ACT.Exp, scale=-1.0).then_inc(g_em, 1)
                f = 2 * i + k // 4
                if k % 4 == 3:
                    act.wait_ge(conv_done, f + 1)
                    act.activation(proj_t[:, 12 + f, :], relu_dot[f % 2][:, :], ACT.Silu).then_inc(silu_done, 1)

            dense("head_n", head_n_out, beside=gates_and_silu, banks=lambda i: (0, 2) if i < 2 else (0, 1, 2, 3))
            def q_out(i):
                for b in (0, 2):
                    act.wait_ge(qa_done, 4 * i + b + 1)
                    if i:
                        act.wait_ge(lg_done, 8 * i)
                    act.activation(q_abs[:, b // 2, 4 * (b % 2):4 * (b % 2) + 4, :],
                                   psx[b][:, :].rearrange("p (h q) -> p h q", h=4), ACT.Copy).then_inc(qa_out_a, 1)

            def exp(i, h):
                n = 8 * i + h
                act.wait_ge(lg_max, n + 1)
                c = slice(n % 16, n % 16 + 1)
                p = prob[n % 3][:, 0:P * (i + 1)]
                act.activation(p, p, ACT.Exp, bias=head_neg[:, c], accum_out=head_sum[:, c]).then_inc(exp_done, 1)

            def turned(i, h):
                n = 8 * i + h
                act.wait_ge(pt_done, n + 1)
                if h % 4 == 0 and n:
                    act.wait_ge(pv_done, 2 * (n // 4))
                act.activation(prob_t[:, 0:i + 1, h % 4, :],
                               psd[2 + h % 2][:, 0:P * (i + 1)].rearrange("p (k q) -> p k q", k=i + 1),
                               ACT.Copy).then_inc(pt_out, 1)

            def latent_out(i, g):
                act.wait_ge(pv_done, 2 * (2 * i + g) + 1)
                if i:
                    act.wait_ge(o_done, 2 * i)
                act.activation(o_lat[:, 0, 4 * g:4 * g + 4, :], psd[0][:, :].rearrange("p (h q) -> p h q", h=4),
                               ACT.Copy).then_inc(ol_out_a, 1)

            q_out(0)
            for i in range(TT):
                exp(i, 0)
                exp(i, 1)
                for h in range(DSA_H):
                    turned(i, h)
                    if h + 2 < DSA_H:
                        exp(i, h + 2)
                    if h == 4:
                        latent_out(i, 0)
                if i + 1 < TT:
                    q_out(i + 1)
                latent_out(i, 1)
                for g in range(2):
                    act.wait_ge(o_done, 2 * i + g + 1)
                    act.activation(act_hi[:, 4 * g:4 * g + 4, P * i:P * i + P],
                                   psd[2 + g][:, :].rearrange("p (h q) -> p h q", h=4), ACT.Copy).then_inc(o_hi, 1)

            act.wait_ge(g_tok_out, 2)
            act.wait_ge(score_done, 3 * IDX_H)

            def decay(h):
                for j in range(TT):
                    n = 4 * h + j
                    act.wait_ge(m_row, h + 1)
                    if n >= 2:
                        act.wait_ge(m_p, n - 1)
                    act.activation(w_exp[n % 2][:, 0:T - P * j], psx[h % 2][:, P * j:T], ACT.Exp, scale=-1.0,
                                   bias=u_tok[:, j, h:h + 1]).then_inc(m_exp, 1)

            decay(0)
            for h in range(ML_H):
                if h + 1 < ML_H:
                    decay(h + 1)
                act.wait_ge(m_den, h + 1)
                for i in range(TT):
                    act.activation(hs[:, i, ML_V * h:ML_V * h + ML_V], psd[i // 2][:, 256 * (i % 2):256 * (i % 2) + 256],
                                   ACT.Copy, scale=den_inv[:, i, h:h + 1]).then_inc(m_hs, 1)
                for i in range(TT):
                    act.wait_ge(m_hs, 4 * h + i + 1)
                    if h or i:
                        act.wait_ge(m_sq, 4 * h + i)
                    act.activation(sq_junk[:, :], hs[:, i, ML_V * h:ML_V * h + ML_V], ACT.Square,
                                   accum_out=stats[:, 0, 4 * h + i:4 * h + i + 1]).then_inc(m_sq, 1)
            root(0, 16)
            for f in range(8):
                act.wait_ge(m_turned, f + 1)
                act.activation(act_hi[:, 8 + f, :], psx[f % 4][:, :], ACT.Copy).then_inc(m_hi, 1)
            dense("out", None, behind=part_squares("out"))
            root(0, TT)
            for t in range(TT):
                turned_tile("x", t, turned_to(act_hi))

            def mem_squares():
                act.wait_ge(mem_land, 16)
                for t in range(MT):
                    square(mem_in[:, t, :], mem_xs[t][:, :], t)
                root(0, MT)

            dense("cq", lambda i, m: act.activation(x_q[:, slice(4 * i + m, 4 * i + m + 1) if isinstance(i, int) else
                                                        bass.ds(i * 4 + m, 1), :], psd[m][:, :], ACT.Copy),
                  before_last=mem_squares)
            for t in range(MT):
                turned_tile("mem", t, turned_to(mem_hi))
            dense("k", lambda i, m: act.activation(x_k[:, slice(4 * i + m, 4 * i + m + 1) if isinstance(i, int) else
                                                       bass.ds(i * 4 + m, 1), :], psd[m][:, 0:N_MEM], ACT.Copy))

            def v_out(i, m):
                c = 256 * (m % 2)
                c = slice(512 * i + c, 512 * i + c + 256) if isinstance(i, int) else bass.ds(i * 512 + c, 256)
                return act.activation(x_v[:, m // 2, c], psd[m][:, 0:256], ACT.Copy)

            dense("v", v_out)

            def x_soft(n):
                act.wait_ge(xl_max, n + 1)
                if n >= 3:
                    act.wait_ge(xt_done, n - 2)
                act.activation(xp[n % 3][:, :], psx[n % 3][:, 0:N_MEM], ACT.Exp, scale=float(X_D) ** -0.5,
                               bias=head_neg[:, n:n + 1], accum_out=head_sum[:, n:n + 1]).then_inc(x_exp, 1)

            def x_turned(n):
                h, i = n // TT, n % TT
                act.wait_ge(xt_done, n + 1)
                if i == 0 and h >= 2:
                    act.wait_ge(xo_done, 4 * (h - 1))
                act.activation(xp_t[:, h % 2, :, P * i:P * i + P],
                               psx[3][:, 0:2 * P].rearrange("p (m q) -> p m q", m=2), ACT.Copy).then_inc(xt_out, 1)

            def x_out(h):
                for d in range(4):
                    k = 4 * h + d
                    act.wait_ge(xo_done, k + 1)
                    act.activation(act_hi[:, k, :], psd[d][:, :], ACT.Copy).then_inc(xo_hi, 1)

            x_soft(0)
            x_soft(1)
            for n in range(X_H * TT):
                x_turned(n)
                if n + 2 < X_H * TT:
                    x_soft(n + 2)
                if n > TT and n % TT == 1:
                    x_out(n // TT - 1)
            x_out(X_H - 1)
            dense("co", None, behind=part_squares("co"))

            def h_out(t, g):
                if g % 2 == 0:
                    act.activation(h_t[:, 4 * g:4 * g + 4, P * t:P * t + P],
                                   psx[g][:, :].rearrange("p (k n) -> p k n", k=4), ACT.Copy).then_inc(n_hi, 1)

            root(0, TT)
            for t in range(TT):
                turned_tile("ffn", t, h_out)
            def e_split(b, r):
                act.wait_ge(e_land[r % 6], b * 32 + (r // 6 + 1) * 16)
                if not (isinstance(b, int) and b == 0 and r < 3):
                    act.wait_ge(e_used, b * 12 + (r - 2))
                act.activation(e_hi[r % 3][:, :], e_raw[r % 6][:, :], ACT.Copy).then_inc(e_hi_done, 1)

            for t in range(TT):
                act.wait_ge(r_done, t + 1)
                act.activation(r_log_t[:, P * t:P * t + P], psd[t][0:64, 0:P], ACT.Copy).then_inc(r_out, 1)
            for t in range(TT):
                act.wait_ge(r_neg, 1)
                act.activation(g_exp[:, t, :], r_log[:, t, 0:G], ACT.Exp, bias=neg_m[:, 0, t:t + 1],
                               accum_out=g_sum[:, t:t + 1]).then_inc(r_exp, 1)
            for t in range(TT):
                act.wait_ge(r_neg, 2)
                act.activation(e_exp[:, t, :], e_log[:, t, :], ACT.Exp, bias=neg_m[:, 1, t:t + 1]).then_inc(r_exp, 1)
            for r in range(3):
                e_split(0, r)

            def rows_out(b):
                act.wait_ge(xg_turned, b + 1)
                for k in range(2):
                    act.activation(xt_hi[:, 8 * k:8 * k + 8, :], psx[2 + k][:, :].rearrange("p (k s) -> p k s", k=8),
                                   ACT.Copy).then_inc(xt_high, 1)

            def expert(b, ahead):
                for r in range(3, 7):
                    e_split(b, r)
                act.wait_ge(e_used, b * 12 + 4)
                act.activation(he_g[:, :], psx[0][0:BLOCK, :], ACT.Silu).then_inc(he_silu, 1)
                for r in range(7, 10):
                    e_split(b, r)
                act.wait_ge(he_turned, b + 1)
                act.activation(he_hi[:, :, :], psx[0][:, 0:FT * BLOCK].rearrange("p (f s) -> p f s", f=FT),
                               ACT.Copy).then_inc(he_split_a, 1)
                e_split(b, 10)
                if ahead:
                    rows_out(b + 1)
                for r in range(11, 15 if ahead else 12):
                    e_split(b, r)
                act.wait_ge(put_copied, b + 1)
                act.wait_ge(e_used, b * 12 + 12)
                for m in (0, 2):
                    act.activation(y_sb[:, 512 * m:512 * m + 512], psd[m][0:BLOCK, :], ACT.Copy,
                                   scale=put_idx[:, 2:3].bitcast(F32)).then_inc(y_out_a, 1)

            rows_out(0)
            with act.Fori(0, NE - 1) as b:
                expert(b, True)
            expert(NE - 1, False)
            act.wait_ge(more_done, 1)
            n_more = act.value_load(more_i[0:1, MAX_MORE:MAX_MORE + 1], min_val=0, max_val=MAX_MORE)
            with act.If(n_more > 0):
                with act.Fori(0, MAX_MORE) as b:
                    with act.If(n_more > b):
                        for r in range(3):
                            e_split(b + NE, r)
                        rows_out(b + NE)
                        expert(b + NE, False)
            for t in range(TT):
                act.wait_ge(f_add, 2 * t + 2)
                if t:
                    act.wait_ge(f_sq, t)
                act.activation(xs_f[:, :], x_res[:, t, :], ACT.Square, accum_out=stats[:, 0, t:t + 1]).then_inc(f_sq, 1)
                root(t, 1)

        @block.vector
        def _(dve):
            own = [0]

            def link(ins):
                own[0] += 1
                ins.then_inc(dve_own, 1)
                dve.wait_ge(dve_own, own[0])

            def split(name, i, j):
                b = first[name] + i
                w = SEG_W[name] if j < 8 else SEG_W[NEXT[name]] if SEG_N[name] == 1 or isinstance(i, int) else SEG_W[name]
                dve.wait_ge(hi_done, b * 8 + (j + 1))
                dve.tensor_tensor(w_lo[j % 2][:, :, 0:w], w_raw[j % 4][:, :, 0:w], w_hi[j % 2][:, :, 0:w].bitcast(F32),
                                  ALU.subtract).then_inc(lo_done, 1)

            def dense(name, evac, banks=lambda i: (1, 3), beside=None, before_last=None):
                base, n = first[name], SEG_N[name]

                def one(i, top):
                    for j in range(2, min(top, 9)):
                        split(name, i, j)
                        if beside is not None:
                            beside(i, j - 2)
                    for m in banks(i):
                        dve.wait_ge(bank_done[m], base + i + 1)
                        evac(i, m).then_inc(bank_free[m], 1)
                    if top > 9:
                        split(name, i, 9)
                        if beside is not None:
                            beside(i, 7)

                if beside is not None:
                    for i in range(n - 1):
                        one(i, 10)
                elif n > 1:
                    with dve.Fori(0, n - 1) as i:
                        one(i, 10)
                if before_last is not None:
                    before_last()
                one(n - 1, 10 if name in NEXT else 8)
                dve.wait_ge(bank_done[3], base + n)
                for m in range(4):
                    dve.wait_ge(bank_free[m], base + n)

            roots = [0]

            def rstd(c0, n, inv):
                roots[0] += 1
                var, r, t = stats[:, 1, c0:c0 + n], stats[:, 2, c0:c0 + n], stats[:, 3, c0:c0 + n]
                dve.tensor_scalar(var, stats[:, 0, c0:c0 + n], inv, EPS, ALU.mult, ALU.add).then_inc(n_var, 1)
                dve.wait_ge(n_sd, roots[0])
                link(dve.reciprocal(r, t))
                link(dve.tensor_tensor(t, r, r, ALU.mult))
                link(dve.tensor_tensor(t, t, var, ALU.mult))
                link(dve.tensor_scalar(t, t, -0.5, 1.5, ALU.mult, ALU.add))
                link(dve.tensor_tensor(r, r, t, ALU.mult))

            def scale(src, dst, g, t):
                dve.scalar_tensor_tensor(dst[t % 2][:, :], src, stats[:, 2, t:t + 1], g[:, :], ALU.mult,
                                         ALU.mult).then_inc(n_xs, 1)

            def turned_tile(name, t, lo):
                base = NORM_AT[name]
                for k in range(4):
                    q = 4 * (base + t) + k
                    if lo is not None:
                        hi_t, lo_t = lo
                        dve.wait_ge(n_hi, q + 1)
                        s = (slice(None), slice(4 * k, 4 * k + 4), slice(P * t, P * t + P))
                        dve.tensor_tensor(lo_t[s], psx[k][:, :].rearrange("p (k n) -> p k n", k=4),
                                          hi_t[s].bitcast(F32), ALU.subtract).then_inc(n_lo, 1)
                    elif k % 2:
                        dve.wait_ge(n_turned, q + 1)
                        dve.wait_ge(n_hi, 4 * base + 2 * t + k // 2 + 1)
                        dve.tensor_copy(h_t[:, 4 * k:4 * k + 4, P * t:P * t + P],
                                        psx[k][:, :].rearrange("p (k n) -> p k n", k=4)).then_inc(n_lo, 2)

            def norm(name, dst, g, lo, n_gain):
                base = NORM_AT[name]
                dve.wait_ge(q_sq, SQ_AT[name] + 4 * TT)
                link(dve.tensor_reduce(stats[:, 0, 0:TT], sq_part[:, :, :], AX.X, ALU.add))
                rstd(0, TT, 1.0 / D)
                dve.wait_ge(gain_land, 16 * n_gain)
                scale(x_res[:, 0, :], dst, g, 0)
                for t in range(TT):
                    if t + 1 < TT:
                        if t >= 1:
                            dve.wait_ge(n_turned, 4 * (base + t))
                            if name == "ffn":
                                dve.wait_ge(h_store[(t + 1) % 2], 16 * ((t + 1) // 2))
                        scale(x_res[:, t + 1, :], dst, g, t + 1)
                    turned_tile(name, t, lo)

            def one_of(i, m):
                return slice(4 * i + m, 4 * i + m + 1) if isinstance(i, int) else bass.ds(i * 4 + m, 1)

            dve.wait_ge(gain_land, 16)
            for t in range(TT):
                dve.wait_ge(n_sq, t + 1)
                rstd(t, 1, 1.0 / D)
                if t >= 2:
                    dve.wait_ge(n_turned, 4 * (t - 1))
                scale(x_in[:, t, :], xs, gain, t)
                if t:
                    turned_tile("mix", t - 1, (act_hi, act_lo))
            for j in range(2):
                split("misc", 0, j)
            turned_tile("mix", TT - 1, (act_hi, act_lo))
            dense("misc", lambda i, m: dve.tensor_copy(misc[:, m, :], psd[m][:, 0:MISC]))
            dve.wait_ge(k_sq, 8)
            rstd(0, 8, 1.0 / DSA_C)
            dve.tensor_scalar(idx_w[:, :, :], misc[:, :, DSA_C + IDX_D:DSA_C + IDX_D + IDX_H],
                              float(IDX_H * IDX_D) ** -0.5, None, ALU.mult).then_inc(consts, 1)
            dve.wait_ge(kv_land, 32)
            for t in range(TT):
                dve.scalar_tensor_tensor(c_kv[:, t, :], misc[:, t, 0:DSA_C], stats[:, 2, t:t + 1], kv_gain[:, :],
                                         ALU.mult, ALU.mult).then_inc(k_norm, 1)
                for c in range(2):
                    dve.scalar_tensor_tensor(k_idx_n[:, t, IDX_D * c:IDX_D * c + IDX_D], misc[:, t, DSA_C:DSA_C + IDX_D],
                                             stats[:, 2, TT + t:TT + t + 1], ki_gain[:, :], ALU.mult,
                                             ALU.mult).then_inc(k_norm, 1)
            dense("head_t", lambda i, m: dve.tensor_copy(proj_t[:, one_of(i, m), :], psd[m][:, :]))
            dve.wait_ge(k_turned, 2)
            dve.tensor_copy(c_kv_t[:, 1, :], psx[1][:, :]).then_inc(k_out_d, 1)
            dve.wait_ge(c_turned, 1)
            dve.tensor_copy(conv_t[:, :], psx[3][:, 0:(CONV + 1) * 8]).then_inc(c_out, 1)
            dve.wait_ge(c_out, 1)
            dve.wait_ge(consts, 3)
            for n in range(3 * IDX_H):
                i, h = 1 + n // IDX_H, n % IDX_H
                s = P * (i + 1)
                dve.wait_ge(relu_done, n + 1)
                if h == 0:
                    dve.tensor_scalar(chosen[i][:, :], relu_dot[n % 2][:, 0:s], idx_w[:, i, h:h + 1], None,
                                      ALU.mult).then_inc(score_done, 1)
                else:
                    dve.wait_ge(score_done, n)
                    dve.scalar_tensor_tensor(chosen[i][:, :], relu_dot[n % 2][:, 0:s], idx_w[:, i, h:h + 1],
                                             chosen[i][:, :], ALU.mult, ALU.add).then_inc(score_done, 1)
            dve.wait_ge(score_done, 3 * IDX_H)
            for i in (1, 2, 3):
                link(dve.memset(chosen[i][0:CHUNK, P * (i + 1) - CHUNK:P * (i + 1)], NEG))
            dve.sem_inc(round_done, 1)

            assert TOPK // 8 * 2 == SEG_N["head_n"] * 8

            def best_keys(i, k):
                n = 24 * i + 6 * (k // 2) + 2 * (k % 2) + 1
                for q, c in enumerate((2, 1) if k % 2 else (3,)):
                    dve.wait_ge(round_done, n + 2 * q)
                    dve.max(best[:, c, :], chosen[c][:, :]).then_inc(round_done, 1)
                    dve.wait_ge(round_done, n + 2 * q + 1)
                    dve.match_replace(out=chosen[c][:, :], in_to_replace=best[:, c, :], in_values=chosen[c][:, :],
                                      imm_value=TAKEN).then_inc(round_done, 1)

            def gates_in():
                dve.wait_ge(g_turned, 2)
                dve.wait_ge(const_land, 5 * 16)
                link(dve.tensor_scalar(rows[0][:, :], psx[0][0:ML_H, :], gate_i[:, :], None, ALU.add))
                link(dve.tensor_scalar(rows[1][:, :], psx[1][0:ML_H, :], gate_f[:, :], None, ALU.add))
                link(dve.tensor_scalar(rows[2][:, :], rows[1][:, :], -1.0, None, ALU.mult))
                dve.tensor_tensor(rows[2][:, :], rows[1][:, :], rows[2][:, :], ALU.min).then_inc(g_abs, 1)
                link(dve.memset(r_ones[:, :], 1.0))

            def gates_summed():
                dve.wait_ge(g_ln, 1)
                link(dve.scalar_tensor_tensor(rows[1][:, :], rows[1][:, :], 0.0, rows[2][:, :], ALU.min, ALU.subtract))
                link(dve.tensor_tensor_scan(rows[3][:, :], r_ones[:, :], rows[1][:, :], 0.0, ALU.mult, ALU.add))
                link(dve.tensor_tensor(rows[4][:, :], rows[0][:, :], rows[3][:, :], ALU.subtract))
                link(dve.tensor_tensor_scan(rows[5][:, :], r_ones[:, :], rows[4][:, :], 0.0, ALU.mult, ALU.max))
                dve.tensor_tensor(rows[6][:, :], rows[3][:, :], rows[5][:, :], ALU.add).then_inc(g_sumd, 1)

            def convolved(f):
                src, dst = proj_t[:, 12 + f, :], relu_dot[f % 2][:, :]
                tap = lambda j: conv_t[:, 8 * j + f:8 * j + f + 1]
                if f >= 2:
                    dve.wait_ge(silu_done, f - 1)
                link(dve.tensor_scalar(dst, src, tap(3), tap(4), ALU.mult, ALU.add))
                for j in (2, 1):
                    s = 3 - j
                    link(dve.scalar_tensor_tensor(dst[:, s:T], src[:, 0:T - s], tap(j), dst[:, s:T], ALU.mult, ALU.add))
                dve.scalar_tensor_tensor(dst[:, 3:T], src[:, 0:T - 3], tap(0), dst[:, 3:T], ALU.mult,
                                         ALU.add).then_inc(conv_done, 1)

            def keys_gates_conv(i, k):
                best_keys(i, k)
                if (i, k) == (0, 0):
                    gates_in()
                if (i, k) == (0, 3):
                    gates_summed()
                if k % 4 == 1:
                    convolved(2 * i + k // 4)

            dense("head_n", lambda i, m: dve.tensor_copy(proj_n[:, m, 512 * i:512 * i + 512], psd[m][:, :]),
                  banks=lambda i: (1, 3) if i < 2 else (), beside=keys_gates_conv)
            dve.wait_ge(g_tok, 1)
            dve.tensor_copy(u_tok[:, :, :], psx[2][:, 0:16].rearrange("p (t h) -> p t h", t=TT)).then_inc(g_tok_out, 1)
            dve.tensor_copy(em_tok[:, :, :], psx[2][:, 16:32].rearrange("p (t h) -> p t h", t=TT)).then_inc(g_tok_out, 1)
            dve.wait_ge(round_done, 6 * TOPK // 8 + 1)
            for c in (1, 2, 3):
                link(dve.tensor_scalar(chosen[c][:, :], chosen[c][:, :], TAKEN, HIDE, ALU.not_equal, ALU.mult))
            dve.wait_ge(bias_done, 1)
            def q_out(i):
                for b in (1, 3):
                    dve.wait_ge(qa_done, 4 * i + b + 1)
                    if i:
                        dve.wait_ge(lg_done, 8 * i)
                    dve.tensor_copy(q_abs[:, b // 2, 4 * (b % 2):4 * (b % 2) + 4, :],
                                    psx[b][:, :].rearrange("p (h q) -> p h q", h=4)).then_inc(qa_out_d, 1)

            def masked(i, h):
                n, s = 8 * i + h, P * (i + 1)
                c = slice(n % 16, n % 16 + 1)
                dve.wait_ge(lg_done, n + 1)
                if n >= 3:
                    dve.wait_ge(pt_done, n - 2)
                dve.tensor_tensor_reduce(out=prob[n % 3][:, 0:s], in0=psx[h % 4][:, 0:s],
                                         in1=bias0[:, :] if i == 0 else chosen[i][:, :], scale=float(DSA_D) ** -0.5,
                                         scalar=-3.0e38, op0=ALU.add, op1=ALU.max,
                                         accum_out=head_max[:, c]).then_inc(lg_masked, 1)
                dve.wait_ge(lg_masked, n + 1)
                dve.tensor_scalar(head_neg[:, c], head_max[:, c], -1.0, None, ALU.mult).then_inc(lg_max, 1)

            def normed(i, h):
                n, s = 8 * i + h, P * (i + 1)
                c = slice(n % 16, n % 16 + 1)
                dve.wait_ge(exp_done, n + 1)
                link(dve.reciprocal(head_inv[:, c], head_sum[:, c]))
                dve.tensor_scalar(prob[n % 3][:, 0:s], prob[n % 3][:, 0:s], head_inv[:, c], None,
                                  ALU.mult).then_inc(prob_done, 1)

            def latent_out(i, g):
                dve.wait_ge(pv_done, 2 * (2 * i + g) + 2)
                if i:
                    dve.wait_ge(o_done, 2 * i)
                dve.tensor_copy(o_lat[:, 1, 4 * g:4 * g + 4, :],
                                psd[1][:, :].rearrange("p (h q) -> p h q", h=4)).then_inc(ol_out_d, 1)

            q_out(0)
            for i in range(TT):
                masked(i, 0)
                masked(i, 1)
                for h in range(DSA_H):
                    normed(i, h)
                    if h + 2 < DSA_H:
                        masked(i, h + 2)
                    if h == 5:
                        latent_out(i, 0)
                if i + 1 < TT:
                    q_out(i + 1)
                latent_out(i, 1)
                for g in range(2):
                    dve.wait_ge(o_hi, 2 * i + g + 1)
                    a = (slice(None), slice(4 * g, 4 * g + 4), slice(P * i, P * i + P))
                    dve.tensor_tensor(act_lo[a], psd[2 + g][:, :].rearrange("p (h q) -> p h q", h=4),
                                      act_hi[a].bitcast(F32), ALU.subtract).then_inc(o_lo, 1)

            dve.tensor_copy(pick_row[:, :, :], ident[0:ML_H, 0:ML_H].unsqueeze(2).to_broadcast([ML_H, ML_H, P])).then_inc(g_pick, 1)
            dve.wait_ge(g_tok_out, 2)

            def weigh(h):
                for j in range(TT):
                    n = 4 * h + j
                    dve.wait_ge(m_qk, n + 1)
                    dve.wait_ge(m_sel, n + 1)
                    if j == 0 and h:
                        dve.wait_ge(m_pv, 4 * h)
                    dve.scalar_tensor_tensor(p_ml[:, j, P * j:T], psx[2 + n % 2][:, 0:T - P * j], float(ML_K) ** -0.5,
                                             w_exp[n % 2][:, 0:T - P * j], ALU.mult, ALU.mult).then_inc(m_p, 1)

            for h in range(ML_H):
                weigh(h)
                dve.wait_ge(m_pv, 4 * h + 4)
                den = psd[2 + h % 2][:, 0:TT]
                link(dve.scalar_tensor_tensor(den_inv[:, :, h], den, -1.0, em_tok[:, :, h], ALU.mult, ALU.max))
                link(dve.tensor_tensor(den_inv[:, :, h], den, den_inv[:, :, h], ALU.max))
                dve.reciprocal(den_inv[:, :, h], den_inv[:, :, h]).then_inc(m_den, 1)
            dve.wait_ge(m_sq, 16)
            rstd(0, 16, 1.0 / ML_V)
            dve.wait_ge(ml_land, 16)
            for i in range(TT):
                for h in range(ML_H):
                    c = slice(ML_V * h, ML_V * h + ML_V)
                    link(dve.scalar_tensor_tensor(hs[:, i, c], hs[:, i, c], stats[:, 2, 4 * h + i:4 * h + i + 1],
                                                  ml_gain[:, c], ALU.mult, ALU.mult))
                dve.tensor_tensor(hs[:, i, :], hs[:, i, :], proj_n[:, i, 1024:2048], ALU.mult).then_inc(m_norm, 1)
            for f in range(8):
                dve.wait_ge(m_hi, f + 1)
                dve.tensor_tensor(act_lo[:, 8 + f, :], psx[f % 4][:, :], act_hi[:, 8 + f, :].bitcast(F32),
                                  ALU.subtract).then_inc(m_lo, 1)

            def add_res(i, m):
                c = slice(512 * i, 512 * i + 512) if isinstance(i, int) else bass.ds(i * 512, 512)
                return dve.tensor_tensor(x_res[:, m, c], psd[m][:, :], x_res[:, m, c], ALU.add)

            dve.sem_inc(q_sq, 1)
            dve.wait_ge(res_land, 16)
            dense("out", add_res, banks=lambda i: (0, 1, 2, 3))
            norm("x", xs, gain, (act_hi, act_lo), 2)

            def mem_normed():
                dve.wait_ge(n_sq, NORM_N["mix"] + MT)
                rstd(0, MT, 1.0 / D)
                dve.wait_ge(gain_land, 16 * 3)
                for t in range(MT):
                    scale(mem_in[:, t, :], mem_xs, mem_gain, t)

            dense("cq", lambda i, m: dve.tensor_copy(x_q[:, one_of(i, m), :], psd[m][:, :]), before_last=mem_normed)
            for t in range(MT):
                turned_tile("mem", t, (mem_hi, mem_lo))
            dense("k", lambda i, m: dve.tensor_copy(x_k[:, one_of(i, m), :], psd[m][:, 0:N_MEM]))

            def v_out(i, m):
                c = 256 * (m % 2)
                c = slice(512 * i + c, 512 * i + c + 256) if isinstance(i, int) else bass.ds(i * 512 + c, 256)
                return dve.tensor_copy(x_v[:, m // 2, c], psd[m][:, 0:256])

            dense("v", v_out)

            def x_max(n):
                dve.wait_ge(xl_done, n + 1)
                link(dve.tensor_reduce(head_max[:, n:n + 1], psx[n % 3][:, 0:N_MEM], AX.X, ALU.max))
                dve.tensor_scalar(head_neg[:, n:n + 1], head_max[:, n:n + 1], -float(X_D) ** -0.5, None,
                                  ALU.mult).then_inc(xl_max, 1)

            def x_out(h):
                for d in range(4):
                    k = 4 * h + d
                    dve.wait_ge(xo_hi, k + 1)
                    dve.tensor_tensor(act_lo[:, k, :], psd[d][:, :], act_hi[:, k, :].bitcast(F32),
                                      ALU.subtract).then_inc(xo_lo, 1)

            x_max(0)
            x_max(1)
            for n in range(X_H * TT):
                dve.wait_ge(x_exp, n + 1)
                link(dve.reciprocal(head_inv[:, n:n + 1], head_sum[:, n:n + 1]))
                dve.tensor_scalar(xp[n % 3][:, :], xp[n % 3][:, :], head_inv[:, n:n + 1], None,
                                  ALU.mult).then_inc(x_prob, 1)
                if n + 2 < X_H * TT:
                    x_max(n + 2)
                if n > TT and n % TT == 1:
                    x_out(n // TT - 1)
            x_out(X_H - 1)
            dense("co", add_res, banks=lambda i: (0, 1, 2, 3))
            norm("ffn", ffn_xs, gain, None, 4)

            def spread(ap, shape, axis):
                return ap.unsqueeze(axis).to_broadcast(shape)

            def e_split(b, r):
                dve.wait_ge(e_hi_done, b * 12 + (r + 1))
                dve.tensor_tensor(e_lo[r % 3][:, :], e_raw[r % 6][:, :], e_hi[r % 3][:, :].bitcast(F32),
                                  ALU.subtract).then_inc(e_lo_done, 1)

            dve.wait_ge(r_land, 64)
            dve.wait_ge(route_consts, 2)
            for t in range(TT):
                dve.wait_ge(r_back, t + 1)
                link(dve.tensor_tensor(r_log[:, t, :], psd[t][:, 256:256 + G + NE], r_bias[:, :], ALU.add))
                link(dve.tensor_copy(g_log8[:, t, 0:G], r_log[:, t, 0:G]))
                link(dve.max(g_top[:, t, :], g_log8[:, t, :]))
                link(dve.max_index(g_idx[:, t, :], g_top[:, t, :], g_log8[:, t, :]))
            dve.tensor_scalar(neg_m[:, 0, :], g_top[:, :, 0], -1.0, None, ALU.mult).then_inc(r_neg, 1)
            link(dve.tensor_copy(g_sel[:, :], g_idx[:, :, 0]))
            link(dve.tensor_tensor(g_oh[:, :, :], spread(iota_e[:, 0:G], [P, TT, G], 1),
                                   spread(g_sel[:, :], [P, TT, G], 2), ALU.is_equal))
            for t in range(TT):
                link(dve.tensor_tensor(e_mul[:, t, :, :], r_log[:, t, G:G + NE].rearrange("p (g e) -> p g e", g=G),
                                       spread(g_oh[:, t, :], [P, G, EG], 2), ALU.mult))
            link(dve.tensor_reduce(e_log[:, :, :], e_mul[:, :, :, :].rearrange("p t g e -> p t e g"), AX.X, ALU.add))
            for t in range(TT):
                link(dve.max(e_top[:, t, :], e_log[:, t, :]))
            dve.tensor_scalar(neg_m[:, 1, :], e_top[:, :, 0], -1.0, None, ALU.mult).then_inc(r_neg, 1)
            dve.wait_ge(r_exp, 8)
            for t in range(TT):
                link(dve.max(e_best[:, t, :], e_exp[:, t, :]))
                link(dve.max_index(e_idx[:, t, :], e_best[:, t, :], e_exp[:, t, :]))
            link(dve.tensor_copy(e_id[:, :, :], e_idx[:, :, 0:2]))
            link(dve.scalar_tensor_tensor(e_id[:, :, :], spread(g_sel[:, :], [P, TT, 2], 2), float(EG), e_id[:, :, :],
                                          ALU.mult, ALU.add))
            link(dve.tensor_tensor(e_den[:, :], e_best[:, :, 0], e_best[:, :, 1], ALU.add))
            link(dve.tensor_tensor(e_den[:, :], e_den[:, :], g_sum[:, :], ALU.mult))
            link(dve.reciprocal(e_den[:, :], e_den[:, :]))
            link(dve.tensor_tensor(gate[:, :, :], e_best[:, :, 0:2], spread(e_den[:, :], [P, TT, 2], 2), ALU.mult))
            for t in range(TT):
                link(dve.tensor_tensor(one_hot[:, t, :, :], spread(iota_e[:, :], [P, 2, NE], 1),
                                       spread(e_id[:, t, :], [P, 2, NE], 2), ALU.is_equal))
            dve.tensor_tensor(chose[:, :, :], one_hot[:, :, 0, :], one_hot[:, :, 1, :], ALU.add).then_inc(r_chose, 1)
            for r in range(3):
                e_split(0, r)
            dve.wait_ge(r_rank, 1)
            link(dve.tensor_copy(rank[:, :, :], psx[0][:, 0:TT * NE].rearrange("p (t e) -> p t e", t=TT)))
            link(dve.tensor_copy(count[:, :], psx[1][:, 0:NE]))
            link(dve.tensor_tensor(full[:, :, :], spread(count[:, :], [P, NE, 8], 2), spread(iota_m[:, :], [P, NE, 8], 1),
                                   ALU.is_gt))
            link(dve.tensor_reduce(more[:, :], full[:, :, :], AX.X, ALU.add))
            link(dve.tensor_tensor_scan(more_end[:, :], ones32[:, :], more[:, :], 0.0, ALU.mult, ALU.add))
            link(dve.tensor_tensor(more_at[:, :], more_end[:, :], more[:, :], ALU.subtract))
            link(dve.tensor_tensor(more_cmp[:, :, :], spread(iota_b[:, :], [1, MAX_MORE, NE], 2),
                                   spread(more_end[0:1, :], [1, MAX_MORE, NE], 1), ALU.is_ge))
            link(dve.tensor_reduce(more_f[:, 0:MAX_MORE], more_cmp[:, :, :], AX.X, ALU.add))
            link(dve.tensor_scalar(more_f[:, 0:MAX_MORE], more_f[:, 0:MAX_MORE], float(NE - 1), None, ALU.min))
            link(dve.tensor_copy(more_f[:, MAX_MORE:MAX_MORE + 1], more_end[0:1, NE - 1:NE]))
            dve.tensor_copy(more_i[:, :], more_f[:, :]).then_inc(more_done, 1)
            for src, dst in ((rank, pos), (more_at, pos_at)):
                for t in range(TT):
                    s = spread(src[:, t, :] if src is rank else src[:, :], [P, 2, NE], 1)
                    link(dve.tensor_tensor(picked[:, t, :, :], one_hot[:, t, :, :], s, ALU.mult))
                link(dve.tensor_reduce(dst[:, :, :], picked[:, :, :, :], AX.X, ALU.add))
            for t in range(TT):
                link(dve.tensor_tensor(pos_full[:, t, :, :], spread(pos[:, t, :], [P, 2, 8], 2),
                                       spread(iota_m[:, :], [P, 2, 8], 1), ALU.is_ge))
            link(dve.tensor_reduce(pos_q[:, :, :], pos_full[:, :, :, :], AX.X, ALU.add))
            link(dve.tensor_tensor(row_f[:, :, :], pos_at[:, :, :], pos_q[:, :, :], ALU.add))
            link(dve.tensor_scalar(row_f[:, :, :], row_f[:, :, :], float(NE - 1), None, ALU.add))
            link(dve.tensor_tensor(row_f[:, :, :], row_f[:, :, :], e_id[:, :, :], ALU.subtract))
            link(dve.tensor_scalar(row_t[:, :, :], pos_q[:, :, :], 0.0, None, ALU.is_gt))
            link(dve.tensor_tensor(row_f[:, :, :], row_f[:, :, :], row_t[:, :, :], ALU.mult))
            link(dve.tensor_tensor(row_f[:, :, :], row_f[:, :, :], e_id[:, :, :], ALU.add))
            link(dve.tensor_tensor(row_f[:, :, :], row_f[:, :, :], pos_q[:, :, :], ALU.subtract))
            link(dve.scalar_tensor_tensor(row_f[:, :, :], row_f[:, :, :], float(BLOCK), pos[:, :, :], ALU.mult, ALU.add))
            link(dve.tensor_copy(slot_new[:, :, :, 0:2], tok_f[:, :, :, :]))
            link(dve.tensor_copy(slot_new[:, :, :, 2].bitcast(F32), gate[:, :, :]))
            dve.tensor_copy(row_i[:, :, :], row_f[:, :, :]).then_inc(r_row, 1)

            def rows_out(b):
                for k in range(2):
                    dve.wait_ge(xt_high, b * 2 + (k + 1))
                    dve.tensor_tensor(xt_lo[:, 8 * k:8 * k + 8, :], psx[2 + k][:, :].rearrange("p (k s) -> p k s", k=8),
                                      xt_hi[:, 8 * k:8 * k + 8, :].bitcast(F32), ALU.subtract).then_inc(xg_out, 1)

            def expert(b, ahead):
                for r in range(3, 10):
                    e_split(b, r)
                dve.wait_ge(he_silu, b + 1)
                dve.wait_ge(e_used, b * 12 + 8)
                dve.tensor_tensor(he[:, :], psx[1][0:BLOCK, :], he_g[:, :], ALU.mult).then_inc(he_done, 1)
                dve.wait_ge(he_split_a, b + 1)
                dve.tensor_tensor(he_lo[:, :, :], psx[0][:, 0:FT * BLOCK].rearrange("p (f s) -> p f s", f=FT),
                                  he_hi[:, :, :].bitcast(F32), ALU.subtract).then_inc(he_split_d, 1)
                e_split(b, 10)
                if ahead:
                    rows_out(b + 1)
                for r in range(11, 15 if ahead else 12):
                    e_split(b, r)
                dve.wait_ge(put_copied, b + 1)
                dve.wait_ge(e_used, b * 12 + 12)
                for m in (1, 3):
                    dve.tensor_scalar(y_sb[:, 512 * m:512 * m + 512], psd[m][0:BLOCK, :], put_idx[:, 2:3].bitcast(F32),
                                      None, ALU.mult).then_inc(y_out_d, 1)

            rows_out(0)
            with dve.Fori(0, NE - 1) as b:
                expert(b, True)
            expert(NE - 1, False)
            n_more = dve.value_load(more_i[0:1, MAX_MORE:MAX_MORE + 1], min_val=0, max_val=MAX_MORE)
            with dve.If(n_more > 0):
                with dve.Fori(0, MAX_MORE) as b:
                    with dve.If(n_more > b):
                        for r in range(3):
                            e_split(b + NE, r)
                        rows_out(b + NE)
                        expert(b + NE, False)
            dve.wait_ge(fg_land, 16)

            def finish(t):
                dve.wait_ge(f_sq, t + 1)
                rstd(t, 1, 1.0 / D)
                if t >= 2:
                    dve.wait_ge(f_store[t % 2], 16 * (t // 2))
                dve.scalar_tensor_tensor(fin_o[t % 2][:, :], x_res[:, t, :], stats[:, 2, t:t + 1], fin_gain[:, :],
                                         ALU.mult, ALU.mult).then_inc(f_out, 1)

            for t in range(TT):
                dve.wait_ge(back_land[t], 16)
                for k in range(2):
                    dve.tensor_tensor(x_res[:, t, :], x_res[:, t, :], y_back[t][:, k, :], ALU.add).then_inc(f_add, 1)
                    dve.wait_ge(f_add, 2 * t + k + 1)
                if t:
                    finish(t - 1)
            finish(TT - 1)


_INS = ["x", "mem", "norm_mix_g", "w_in", "kv_norm_g", "k_idx_norm_g", "w_uk", "w_uv", "conv_w", "conv_b", "gate_b",
        "ml_norm_g", "w_out", "norm_x_g", "mem_norm_g", "w_cq", "w_ckv", "w_co", "norm_ffn_g", "w_group", "b_group",
        "w_router", "b_router", "w_gate", "w_up", "w_down", "final_norm_g"]
_OUTS = [((1, T, D), "float32")]


def _w_in_columns(w):
    sizes = [DSA_H * DSA_D, DSA_C, IDX_H * IDX_D, IDX_D, IDX_H, ML_H * ML_K, ML_H * ML_K, ML_H * ML_V, ML_H, ML_H,
             ML_H * ML_V]
    dq, ckv, qi, ki, wi, mq, mk, mv, mi, mf, mo = np.split(np.asarray(w), np.cumsum(sizes)[:-1], axis=-1)
    return np.concatenate([ckv, ki, wi, mi, mf, dq, qi, mq, mk, mv, mo], axis=-1)


def kernel(**inputs):
    import concourse.bacc as _bacc
    from concourse import mybir as _mybir
    from concourse.bass_utils import run_bass_kernel_spmd as _run

    nc = _bacc.Bacc("TRN2", target_bir_lowering=False, num_devices=1)
    arrays, args = {}, []
    for name in _INS:
        a = _w_in_columns(inputs[name]) if name == "w_in" else inputs[name]
        a = np.ascontiguousarray(a)
        arrays[f"in_{name}_dram"] = a
        args.append(nc.dram_tensor(f"in_{name}_dram", a.shape, _mybir.dt.from_np(a.dtype), kind="ExternalInput").ap())
    for i, (shape, dtype) in enumerate(_OUTS):
        dt = _mybir.dt.from_np(np.dtype(dtype))
        args.append(nc.dram_tensor(f"out_{i}_dram", shape, dt, kind="ExternalOutput").ap())
    layer(nc, *args)
    r = _run(nc, [arrays], core_ids=[0])
    return r.results[0]["out_0_dram"]
```

```python
from contextlib import ExitStack

import numpy as np

import concourse.bass as bass
from concourse import mybir

F32 = mybir.dt.float32
F32R = mybir.dt.float32r
I32 = mybir.dt.int32
U32 = mybir.dt.uint32
ALU = mybir.AluOpType
ACT = mybir.ActivationFunctionType
AX = mybir.AxisListType

P = 128
EPS = 1e-6
T, D = 512, 2048
TT = T // P
KT = D // P
CHUNK = 64
N_MEM = 256
MT = N_MEM // P
DSA_H, DSA_D, DSA_C = 8, 128, 256
CT = DSA_C // P
IDX_H, IDX_D = 8, 64
TOPK = min(256, T // 4)
ML_H, ML_K, ML_V = 4, 128, 256
CONV = 4
X_H, X_D = 4, D // 4
G, EG = 4, 8
NE = G * EG
F = 512
FT = F // P
BLOCK = 64
MAX_MORE = (2 * T - 1) // BLOCK
NB = NE + MAX_MORE
OUT_OF_RANGE = 1 << 20
NEG = -1.0e38
TAKEN = -3.0e38
HIDE = -1.0e30
MISC = DSA_C + IDX_D + IDX_H + 2 * ML_H

KB = 1024
BASE = 16512


def span(start, n):
    return slice(start, start + n) if isinstance(start, int) else bass.ds(start, n)


def layer(nc, x, mem, norm_mix_g, w_in, kv_norm_g, k_idx_norm_g, w_uk, w_uv, conv_w, conv_b, gate_b,
          ml_norm_g, w_out, norm_x_g, mem_norm_g, w_cq, w_ckv, w_co, norm_ffn_g, w_group, b_group,
          w_router, b_router, w_gate, w_up, w_down, final_norm_g, out):
    with ExitStack() as ctx:
        def at(name, shape, off_kb, dt=F32):
            return nc.alloc_sbuf_tensor_at(name, shape, dt, offset=BASE + int(off_kb * KB))

        def sem(name):
            return ctx.enter_context(nc.semaphore(name))

        w_raw = [at(f"w_raw{r}", [P, 2, 512], 4 * r) for r in range(4)]
        w_hi = [at(f"w_hi{r}", [P, 2, 512], 16 + 4 * r, F32R) for r in range(2)]
        w_lo = [at(f"w_lo{r}", [P, 2, 512], 24 + 4 * r, F32R) for r in range(2)]
        act_hi = at("act_hi", [P, KT, T], 32, F32R)
        act_lo = at("act_lo", [P, KT, T], 64, F32R)
        proj_t = at("proj_t", [P, 20, T], 96)
        proj_n = at("proj_n", [P, TT, 2048], 136)
        misc = at("misc", [P, TT, MISC], 168)
        gain = at("gain", [P, D], 174)
        x_in = at("x_in", [P, TT, D], 96)
        xs = [at(f"xs{r}", [P, D], 182 + 8 * r) for r in range(2)]
        junk = at("junk", [P, D], 136)

        w_uk_raw = at("w_uk_raw", [P, CT, 1024], 144)
        k_t = at("k_t", [P, DSA_H, T], 178)
        c_kv = at("c_kv", [P, TT, DSA_C], 190)
        c_kv_t = at("c_kv_t", [P, CT, T], 194)
        k_idx_t = at("k_idx_t", [P, T], 198)
        relu_dot = [at(f"relu_dot{r}", [P, T], 174 + 2 * r) for r in range(2)]
        k_idx_n = at("k_idx_n", [P, TT, 2 * IDX_D], 178)
        kv_gain = at("kv_gain", [P, DSA_C], 180)
        ki_gain = at("ki_gain", [P, IDX_D], 181)
        sq_junk = at("sq_junk", [P, ML_V], 200)
        w_uv_s = at("w_uv_s", [P, CT, 1024], 64)
        v_n = at("v_n", [P, TT, 1024], 80)
        conv_out = [at(f"conv_out{r}", [P, T], (116, 198)[r]) for r in range(2)]
        prob = [at(f"prob{r}", [P, T], 54 + 2 * r) for r in range(3)]
        bias0 = at("bias0", [P, P], 60)
        prob_t = [at(f"prob_t{r}", [P, TT, P], 48 + 2 * r) for r in range(3)]

        w_exp = [at(f"w_exp{r}", [P, T], 112 + 2 * r) for r in range(2)]
        pick_row = at("pick_row", [ML_H, ML_H, P], 116)
        hs = at("hs", [P, TT, ML_H * ML_V], 96)
        p_ml = [at(f"p_ml{r}", [P, TT, T], 178 + 8 * r) for r in range(2)]
        ml_gain = at("ml_gain", [P, ML_H * ML_V], 174)
        rows = [at(f"rows{r}", [ML_H, T], kb) for r, kb in enumerate((140, 142, 148, 150, 112, 118, 114))]
        r_ones = at("r_ones", [ML_H, T], 156)

        x_res = at("x_res", [P, TT, D], 136)
        x_q = at("x_q", [P, KT, T], 96)
        mem_in = at("mem_in", [P, MT, D], 184)
        mem_hi = at("mem_hi", [P, KT, N_MEM], 32, F32R)
        mem_lo = at("mem_lo", [P, KT, N_MEM], 48, F32R)
        mem_gain = at("mem_gain", [P, D], 168)
        mem_xs = [at(f"mem_xs{r}", [P, D], 128 + 48 * r) for r in range(2)]
        sq_part_junk = at("sq_part_junk", [P, 512], 134)
        x_k = at("x_k", [P, KT, N_MEM], 168)
        x_v = at("x_v", [P, MT, D], 184)
        xp = [at(f"xp{r}", [P, N_MEM], 200 + r) for r in range(3)]
        xp_t = at("xp_t", [P, 2, MT, T], 128)

        e_raw = [at(f"e_raw{r}", [P, 2048], 8 * r) for r in range(6)]
        e_hi = [at(f"e_hi{r}", [P, 2048], 48 + 8 * r, F32R) for r in range(3)]
        e_lo = [at(f"e_lo{r}", [P, 2048], 72 + 8 * r, F32R) for r in range(3)]
        h_t = at("h_t", [P, KT, T], 96)
        xg = at("xg", [BLOCK, D], 96)
        y_sb = at("y_sb", [BLOCK, D], 104)
        xt_hi = at("xt_hi", [P, KT, BLOCK], 112, F32R)
        xt_lo = at("xt_lo", [P, KT, BLOCK], 116, F32R)
        he_g = at("he_g", [BLOCK, F], 120)
        he = at("he", [BLOCK, F], 122)
        he_hi = at("he_hi", [P, FT, BLOCK], 124, F32R)
        he_lo = at("he_lo", [P, FT, BLOCK], 125, F32R)
        ffn_xs = [at(f"ffn_xs{r}", [P, D], 182 + 8 * r) for r in range(2)]
        w_r = at("w_r", [P, KT, 64], 168)
        r_log_t = at("r_log_t", [64, T], 172)
        fin_gain = at("fin_gain", [P, D], 174)
        y_back = [at(f"y_back{t}", [P, 2, D], 16 * t) for t in range(TT)]
        xs_f = at("xs_f", [P, D], 128)
        fin_o = [at(f"fin_o{r}", [P, D], 112 + 8 * r) for r in range(2)]

        low = [204.0]

        def small(name, shape, dt=F32):
            n = int(np.prod(shape[1:])) * 4
            t = at(name, shape, low[0], dt)
            low[0] += ((n + 31) // 32 * 32) / KB
            assert BASE + low[0] * KB <= nc.sbuf_usable_end, (name, low[0])
            return t

        ident = small("ident", [P, P])
        ones_col = small("ones_col", [P, 1])
        sq_part = small("sq_part", [P, TT, 4])
        stats = small("stats", [P, 4, 16])
        idx_w = small("idx_w", [P, TT, IDX_H])
        head_max = small("head_max", [P, 16])
        head_neg = small("head_neg", [P, 16])
        head_sum = small("head_sum", [P, 16])
        head_inv = small("head_inv", [P, 16])
        best = small("best", [P, TT, 8])
        chosen = [None, small("chosen1", [P, 2 * P]), at("chosen2", [P, 3 * P], 202), at("chosen3", [P, 4 * P], 200)]
        conv_t = small("conv_t", [P, (CONV + 1) * 8])
        conv_rows = small("conv_rows", [(CONV + 1) * 8, P])
        gate_i = small("gate_i", [ML_H, 1])
        gate_f = small("gate_f", [ML_H, 1])
        u_tok = small("u_tok", [P, TT, ML_H])
        em_tok = small("em_tok", [P, TT, ML_H])
        den_inv = small("den_inv", [P, TT, ML_H])
        assert low[0] < 207.8

        psd = [ctx.enter_context(nc.psum_tensor(f"psd{m}", [P, 512], F32)) for m in range(4)]
        psx = [ctx.enter_context(nc.psum_tensor(f"psx{m}", [P, 512], F32)) for m in range(4)]
        low[0] = 198.0
        before = small("before", [P, P])
        ones_sq = small("ones_sq", [P, P])
        slot_none = small("slot_none", [2 * NB, BLOCK // 2 * 4], I32)
        slot_new = small("slot_new", [P, TT, 2, 4], I32)
        slots = small("slots", [BLOCK, NB, 4], I32)
        take_idx = small("take_idx", [BLOCK, 4], I32)
        put_idx = small("put_idx", [BLOCK, 4], I32)
        tok_f = small("tok_f", [P, TT, 2, 2])
        ones32 = small("ones32", [P, NE])
        iota_e = small("iota_e", [P, NE])
        iota_m = small("iota_m", [P, 8])
        iota_b = small("iota_b", [1, MAX_MORE])
        r_bias = small("r_bias", [P, G + NE])
        more_i = small("more_i", [1, MAX_MORE + 1], I32)
        g_log8 = small("g_log8", [P, TT, 8])
        assert low[0] <= 204.0, low

        low[0] = 128.0
        r_log = small("r_log", [P, TT, G + NE])
        g_top = small("g_top", [P, TT, 8])
        g_idx = small("g_idx", [P, TT, 8], U32)
        g_sel = small("g_sel", [P, TT])
        g_oh = small("g_oh", [P, TT, G])
        g_exp = small("g_exp", [P, TT, G])
        g_sum = small("g_sum", [P, TT])
        e_mul = small("e_mul", [P, TT, G, EG])
        e_log = small("e_log", [P, TT, EG])
        e_top = small("e_top", [P, TT, 8])
        e_exp = small("e_exp", [P, TT, EG])
        e_best = small("e_best", [P, TT, 8])
        e_idx = small("e_idx", [P, TT, 8], U32)
        neg_m = small("neg_m", [P, 2, TT])
        e_id = small("e_id", [P, TT, 2])
        e_den = small("e_den", [P, TT])
        gate = small("gate", [P, TT, 2])
        one_hot = small("one_hot", [P, TT, 2, NE])
        chose = small("chose", [P, TT, NE])
        assert low[0] <= 136.0, low
        low[0] = 174.0
        rank = small("rank", [P, TT, NE])
        picked = small("picked", [P, TT, 2, NE])
        count = small("count", [P, NE])
        full = small("full", [P, NE, 8])
        more = small("more", [P, NE])
        more_end = small("more_end", [P, NE])
        more_at = small("more_at", [P, NE])
        pos = small("pos", [P, TT, 2])
        pos_at = small("pos_at", [P, TT, 2])
        pos_q = small("pos_q", [P, TT, 2])
        pos_full = small("pos_full", [P, TT, 2, 8])
        row_f = small("row_f", [P, TT, 2])
        row_t = small("row_t", [P, TT, 2])
        row_i = small("row_i", [P, TT, 2], I32)
        more_f = small("more_f", [1, MAX_MORE + 1])
        more_cmp = small("more_cmp", [1, MAX_MORE, NE])
        assert low[0] <= 182.0, low

        h_rows = nc.dram_tensor("h_rows", (T, D), F32, kind="Internal").ap()
        y_rows = nc.dram_tensor("y_rows", (2 * T, D), F32, kind="Internal").ap()
        slot_rows = nc.dram_tensor("slot_rows", (NB * BLOCK, 4), I32, kind="Internal").ap()

        x_land = [sem(f"x_land{t}") for t in range(TT)]
        gain_land = sem("gain_land")
        const_land = sem("const_land")
        kv_land = sem("kv_land")
        uv_land = sem("uv_land")
        ml_land = sem("ml_land")
        res_land = sem("res_land")
        mem_land = sem("mem_land")
        w_land = [sem(f"w_land{r}") for r in range(4)]
        hi_done = sem("hi_done")
        lo_done = sem("lo_done")
        w_used = sem("w_used")
        bank_done = [sem(f"bank_done{m}") for m in range(4)]
        bank_free = [sem(f"bank_free{m}") for m in range(4)]
        dve_own = sem("dve_own")
        act_own = sem("act_own")
        pool_own = sem("pool_own")
        consts = sem("consts")
        q_sq, n_sq, n_var, n_sd, n_xs = sem("q_sq"), sem("n_sq"), sem("n_var"), sem("n_sd"), sem("n_xs")
        n_turned, n_hi, n_lo = sem("n_turned"), sem("n_hi"), sem("n_lo")
        k_sq, k_norm, k_turned, k_out_a, k_out_d = (sem(s) for s in (
            "k_sq", "k_norm", "k_turned", "k_out_a", "k_out_d"))
        kh_done, kh_out_a, kh_out_d = sem("kh_done"), sem("kh_out_a"), sem("kh_out_d")
        vh_done, vh_out_a, vh_out_d = sem("vh_done"), sem("vh_out_a"), sem("vh_out_d")
        dot_done, relu_done, score_done, round_done = (sem(s) for s in (
            "dot_done", "relu_done", "score_done", "round_done"))
        bias_done = sem("bias_done")
        lg_done, lg_masked, lg_max, exp_done, prob_done = (sem(s) for s in (
            "lg_done", "lg_masked", "lg_max", "exp_done", "prob_done"))
        pt_done, pt_out, pv_done, o_hi, o_lo = (sem(s) for s in ("pt_done", "pt_out", "pv_done", "o_hi", "o_lo"))
        g_turned, g_abs, g_ln, g_sumd, g_em, g_pick, g_tok, g_tok_out = (sem(s) for s in (
            "g_turned", "g_abs", "g_ln", "g_sumd", "g_em", "g_pick", "g_tok", "g_tok_out"))
        c_turned, c_out, conv_done, silu_done = (sem(s) for s in (
            "c_turned", "c_out", "conv_done", "silu_done"))
        m_row, m_exp, m_sel, m_qk, m_p, m_pv, m_den, m_hs, m_sq, m_norm, m_turned, m_hi, m_lo = (
            sem("m_" + s) for s in ("row", "exp", "sel", "qk", "p", "pv", "den", "hs", "sq", "norm",
                                    "turned", "hi", "lo"))
        xl_done, xl_max, x_exp, x_prob, xt_done, xt_out, xo_done, xo_hi, xo_lo = (
            sem(s) for s in ("xl_done", "xl_max", "x_exp", "x_prob", "xt_done", "xt_out", "xo_done",
                             "xo_hi", "xo_lo"))
        r_land, r_done, r_out, r_back, r_chose, r_neg, r_exp, r_rank, r_row, none_land, slot_store, slot_land = (
            sem(s) for s in ("r_land", "r_done", "r_out", "r_back", "r_chose", "r_neg", "r_exp", "r_rank",
                             "r_row", "none_land", "slot_store", "slot_land"))
        more_done, route_consts = sem("more_done"), sem("route_consts")
        e_land = [sem(f"e_land{r}") for r in range(6)]
        e_hi_done, e_lo_done, e_used = sem("e_hi_done"), sem("e_lo_done"), sem("e_used")
        xg_zero, xg_land, xg_turned, xt_high, xg_out = (sem(s) for s in (
            "xg_zero", "xg_land", "xg_turned", "xt_high", "xg_out"))
        he_silu, he_done, he_turned, he_split_a, he_split_d, y_out_a, y_out_d, y_store = (sem(s) for s in (
            "he_silu", "he_done", "he_turned", "he_split_a", "he_split_d", "y_out_a", "y_out_d", "y_store"))
        take_copied, put_copied, experts_done = (sem(s) for s in (
            "take_copied", "put_copied", "experts_done"))
        back_land = [sem(f"back_land{t}") for t in range(TT)]
        f_pair, f_add, f_sq, f_out = (sem(s) for s in ("f_pair", "f_add", "f_sq", "f_out"))
        h_store = [sem(f"h_store{r}") for r in range(2)]
        f_store = [sem(f"f_store{r}") for r in range(2)]
        fg_land = sem("fg_land")

        SEGS = [("misc", 1, MISC), ("head_t", 5, 512), ("head_n", 4, 512), ("out", 4, 512),
                ("cq", 4, 512), ("k", 4, 512), ("v", 4, 512), ("co", 4, 512)]
        first = {}
        blocks = 0
        for name, n, _ in SEGS:
            first[name] = blocks
            blocks += n
        SEG_N = {name: n for name, n, _ in SEGS}
        SEG_W = {name: w for name, _, w in SEGS}
        NEXT = {a[0]: b[0] for a, b in zip(SEGS, SEGS[1:])}
        w_in_v = w_in[0].rearrange("(k p) n -> p k n", p=P)
        ckv_v = w_ckv[0].rearrange("(k p) n -> p k n", p=P)
        SEG_SRC = {
            "misc": (w_in_v, 0), "head_t": (w_in_v, MISC), "head_n": (w_in_v, MISC + 5 * 512),
            "out": (w_out[0].rearrange("(k p) n -> p k n", p=P), 0),
            "cq": (w_cq[0].rearrange("(k p) n -> p k n", p=P), 0),
            "k": (ckv_v, 0), "v": (ckv_v, D),
            "co": (w_co[0].rearrange("(k p) n -> p k n", p=P), 0),
        }
        NORM_AT = {"mix": 0, "x": 4, "mem": 8, "ffn": 10}
        SQ_AT = {"out": 1, "x": 1, "co": 1 + 4 * TT, "ffn": 1 + 4 * TT}
        NORM_N = {"mix": 4, "x": 4, "mem": 2, "ffn": 4}
        block = ctx.enter_context(nc.Block())

        def piece_width(name, i, j):
            last = isinstance(i, int) and i == SEG_N[name] - 1
            return SEG_W[NEXT[name]] if j >= 8 and last else SEG_W[name]

        def wait_alone(eng, sem_, value, base_sem, base_value):
            if not isinstance(value, int):
                eng.compute_val(value)
            eng.wait_ge(base_sem, base_value)
            eng.wait_ge(sem_, value)

        @block.sync
        def _(sp):
            def piece(name, i, j, wait=True):
                src, c0 = SEG_SRC[name]
                w = SEG_W[name]
                if wait:
                    sp.wait_ge(lo_done, (first[name] + i) * 8 + (j - 3))
                col = i * 512 + c0
                cols = span(col, w)
                sp.dma_start(w_raw[j % 4][:, :, 0:w], src[:, 2 * j:2 * j + 2, cols]).then_inc(w_land[j % 4], 16)

            def stream(name, ahead=False):
                n = SEG_N[name]
                if ahead:
                    for j in range(4):
                        piece(name, 1, j)
                if n > 1:
                    with sp.Fori(1 if ahead else 0, n - 1) as i:
                        for j in range(4, 8):
                            piece(name, i, j)
                        for j in range(4):
                            piece(name, i + 1, j)
                for j in range(4, 8):
                    piece(name, n - 1, j)
                if name in NEXT:
                    for j in range(4):
                        piece(NEXT[name], 0, j)

            for t in range(TT):
                sp.dma_start(x_in[:, t, :], x[0, t * P:(t + 1) * P, :]).then_inc(x_land[t], 16)
                if t == 0:
                    sp.dma_start(gain[:, :], norm_mix_g[0:1, :].to_broadcast([P, D])).then_inc(gain_land, 16)
            for j in range(4):
                piece("misc", 0, j, wait=False)
            sp.dma_start(w_uk_raw[:, :, :], w_uk[0].rearrange("(c p) h d -> p c (h d)", p=P)).then_inc(const_land, 16)
            sp.dma_start(conv_rows[0:CONV * 8, :], conv_w[0].rearrange("j (f p) -> (j f) p", p=P)).then_inc(const_land, 16)
            sp.dma_start(conv_rows[CONV * 8:(CONV + 1) * 8, :],
                         conv_b[0].rearrange("(f p) -> f p", p=P)).then_inc(const_land, 16)
            gb = gate_b.rearrange("a (k g) -> g (a k)", k=2)
            sp.dma_start(gate_i[:, :], gb[:, 0:1]).then_inc(const_land, 16)
            sp.dma_start(gate_f[:, :], gb[:, 1:2]).then_inc(const_land, 16)
            sp.wait_ge(n_xs, 4)
            sp.dma_start(kv_gain[:, :], kv_norm_g[0:1, :].to_broadcast([P, DSA_C])).then_inc(kv_land, 16)
            sp.dma_start(ki_gain[:, :], k_idx_norm_g[0:1, :].to_broadcast([P, IDX_D])).then_inc(kv_land, 16)
            stream("misc")
            stream("head_t")
            stream("head_n")
            sp.wait_ge(bank_done[3], first["out"])
            sp.dma_start(w_uv_s[:, :, :], w_uv[0].rearrange("(c p) h d -> p c (h d)", p=P)).then_inc(uv_land, 16)
            sp.wait_ge(pv_done, TT * DSA_H)
            sp.dma_start(ml_gain[:, :], ml_norm_g[0:1, :].to_broadcast([P, ML_H * ML_V])).then_inc(ml_land, 16)
            for j in range(4, 8):
                piece("out", 0, j)
            sp.wait_ge(m_norm, TT)
            sp.dma_start(x_res[:, :, :], x[0].rearrange("(t p) d -> p t d", p=P)).then_inc(res_land, 16)
            sp.dma_start(gain[:, :], norm_x_g[0:1, :].to_broadcast([P, D])).then_inc(gain_land, 16)
            stream("out", ahead=True)
            sp.wait_ge(n_turned, 4 * NORM_AT["mem"])
            sp.dma_start(mem_gain[:, :], mem_norm_g[0:1, :].to_broadcast([P, D])).then_inc(gain_land, 16)
            sp.dma_start(mem_in[:, :, :], mem[0].rearrange("(t p) d -> p t d", p=P)).then_inc(mem_land, 16)
            stream("cq")
            stream("k")
            stream("v")
            sp.wait_ge(xl_done, 16)
            for m in (0, 2):
                sp.wait_ge(bank_free[m], first["co"])
            sp.wait_ge(xo_done, 16)
            sp.dma_start(gain[:, :], norm_ffn_g[0:1, :].to_broadcast([P, D])).then_inc(gain_land, 16)
            sp.dma_start(w_r[:, :, 0:G], w_group[0].rearrange("(k p) g -> p k g", p=P)).then_inc(r_land, 16)
            sp.dma_start(w_r[:, :, G:G + NE], w_router[0].rearrange("(k p) g -> p k g", p=P)).then_inc(r_land, 16)
            sp.dma_start(r_bias[:, 0:G], b_group[0:1, :].to_broadcast([P, G])).then_inc(r_land, 16)
            sp.dma_start(r_bias[:, G:G + NE], b_router[0:1, :].to_broadcast([P, NE])).then_inc(r_land, 16)
            sp.wait_ge(route_consts, 1)
            sp.dma_start(slot_rows.rearrange("(p n) c -> p (n c)", p=2 * NB), slot_none[:, :]).then_inc(none_land, 16)
            stream("co")
            sp.wait_ge(bank_done[3], blocks)

            def expert_piece(e, r):
                one_e = span(e, 1)
                if r < 8:
                    w, q = (w_gate, w_up)[r // 4][0], r % 4
                    src = w[one_e].rearrange("e (p k) f -> p (e k) f", k=KT)[:, 4 * q:4 * q + 4, :]
                    dst = e_raw[r % 6][:, :].rearrange("p (k f) -> p k f", k=4)
                else:
                    src = w_down[0][one_e].rearrange("e f d -> (e f) d")[P * (r - 8):P * (r - 7), :]
                    dst = e_raw[r % 6][:, :]
                sp.dma_start(dst, src).then_inc(e_land[r % 6], 16)

            def expert(b, e):
                for r in range(12):
                    sp.wait_ge(e_lo_done, b * 12 + (r - 5))
                    expert_piece(e, r)

            def store_rows(t):
                sp.wait_ge(n_xs, NORM_AT["ffn"] + t + 1)
                sp.dma_start(h_rows[t * P:(t + 1) * P, :], ffn_xs[t % 2][:, :]).then_inc(h_store[t % 2], 16)

            for r in range(6):
                expert_piece(0, r)
                if r < TT:
                    store_rows(r)
            for r in range(6, 9):
                sp.wait_ge(e_lo_done, r - 5)
                expert_piece(0, r)
            sp.wait_ge(slot_store, 16 * 2 * TT)
            sp.dma_start(slots[:, :, :], slot_rows.rearrange("(b s) c -> s b c", s=BLOCK)).then_inc(slot_land, 16)
            sp.wait_ge(more_done, 1)
            sp.dma_start(fin_gain[:, :], final_norm_g.rearrange("(a d) -> a d", a=1).to_broadcast([P, D])).then_inc(fg_land, 16)
            for r in range(9, 12):
                sp.wait_ge(e_lo_done, r - 5)
                expert_piece(0, r)
            with sp.Fori(1, NE) as e:
                expert(e, e)
            sp.wait_ge(more_done, 1)
            n_more = sp.value_load(more_i[0:1, MAX_MORE:MAX_MORE + 1], min_val=0, max_val=MAX_MORE)
            with sp.If(n_more > 0):
                with sp.Fori(0, MAX_MORE) as b:
                    with sp.If(n_more > b):
                        expert(b + NE, sp.value_load(more_i[0:1, bass.ds(b, 1)], min_val=0, max_val=NE - 1))
            sp.wait_ge(experts_done, 1)
            for t in range(TT):
                sp.dma_start(y_back[t][:, :, :],
                             y_rows.rearrange("(k t p) d -> t p k d", k=2, p=P)[t]).then_inc(back_land[t], 16)
            for t in range(TT):
                sp.wait_ge(f_out, t + 1)
                sp.dma_start(out[0, t * P:(t + 1) * P, :], fin_o[t % 2][:, :]).then_inc(f_store[t % 2], 16)
            for r in range(2):
                sp.wait_ge(f_store[r], 16 * TT // 2)

        @block.gpsimd
        def _(pool):
            pool.memset(ident[:, :], 0.0).then_inc(pool_own, 1)
            pool.memset(ones_col[:, :], 1.0).then_inc(consts, 1)
            pool.wait_ge(pool_own, 1)
            pool.affine_select(out=ident[:, :], in_=ident[:, :], compare_op=ALU.not_equal, fill=1.0, base=0,
                               pattern=[[-1, P]], channel_multiplier=1).then_inc(consts, 1)
            pool.wait_ge(bank_done[3], first["out"])
            pool.memset(bias0[:, :], 0.0).then_inc(pool_own, 1)
            pool.wait_ge(pool_own, 2)
            pool.memset(bias0[0:CHUNK, CHUNK:P], HIDE).then_inc(bias_done, 1)
            for n in range(4 * ML_H):
                pool.wait_ge(m_exp, n + 1)
                w = w_exp[n % 2][:, 0:P]
                pool.affine_select(out=w, in_=w, compare_op=ALU.is_ge, fill=0.0, base=0,
                                   pattern=[[1, P]], channel_multiplier=-1).then_inc(m_sel, 1)
            pool.wait_ge(xo_done, 16)
            pool.wait_ge(x_prob, 16)
            pool.memset(slot_none[:, :], OUT_OF_RANGE).then_inc(route_consts, 1)
            pool.memset(before[:, :], 1.0).then_inc(pool_own, 1)
            pool.memset(w_r[:, :, G + NE:64], 0.0).then_inc(pool_own, 1)
            pool.memset(ones_sq[:, :], 1.0).then_inc(pool_own, 1)
            pool.memset(ones32[:, :], 1.0).then_inc(pool_own, 1)
            pool.memset(slot_new[:, :, :, :], 0).then_inc(pool_own, 1)
            pool.iota(iota_e[:, :], [[1, NE]], base=0, channel_multiplier=0,
                      allow_small_or_imprecise_dtypes=True).then_inc(pool_own, 1)
            pool.iota(iota_m[:, :], [[BLOCK, 8]], base=BLOCK, channel_multiplier=0,
                      allow_small_or_imprecise_dtypes=True).then_inc(pool_own, 1)
            pool.iota(iota_b[:, :], [[1, MAX_MORE]], base=0, channel_multiplier=0,
                      allow_small_or_imprecise_dtypes=True).then_inc(pool_own, 1)
            pool.iota(tok_f[:, :, :, 0], [[P, TT], [0, 2]], base=0, channel_multiplier=1,
                      allow_small_or_imprecise_dtypes=True).then_inc(pool_own, 1)
            pool.iota(tok_f[:, :, :, 1], [[P, TT], [T, 2]], base=0, channel_multiplier=1,
                      allow_small_or_imprecise_dtypes=True).then_inc(pool_own, 1)
            pool.memset(g_log8[:, :, :], NEG).then_inc(pool_own, 1)
            pool.wait_ge(pool_own, 13)
            pool.affine_select(out=before[:, :], in_=before[:, :], compare_op=ALU.is_gt, fill=0.0, base=0,
                               pattern=[[1, P]], channel_multiplier=-1).then_inc(route_consts, 1)
            pool.wait_ge(r_done, TT)
            pool.memset(xg[:, :], 0.0).then_inc(xg_zero, 1)
            pool.wait_ge(none_land, 16)
            pool.wait_ge(r_row, 1)
            for t in range(TT):
                for k in range(2):
                    pool.indirect_dma_start(
                        out=slot_rows[:, :], out_offset=bass.IndirectOffsetOnAxis(ap=row_i[:, t, k:k + 1], axis=0),
                        in_=slot_new[:, t, k, :], in_offset=None,
                        bounds_check=NB * BLOCK - 1, oob_is_err=False).then_inc(slot_store, 16)
            pool.wait_ge(slot_land, 16)
            for r in range(2):
                pool.wait_ge(h_store[r], 16 * TT // 2)
            col = lambda b: span(b, 1)

            def take(b):
                if not (isinstance(b, int) and b == 0):
                    pool.wait_ge(xg_turned, b)
                pool.tensor_copy(take_idx[:, :], slots[:, col(b), :].rearrange("s b c -> s (b c)")).then_inc(take_copied, 1)
                wait_alone(pool, take_copied, b + 1, slot_land, 16)
                pool.indirect_dma_start(
                    out=xg[:, :], out_offset=None, in_=h_rows[:, :],
                    in_offset=bass.IndirectOffsetOnAxis(ap=take_idx[:, 0:1], axis=0),
                    bounds_check=T - 1, oob_is_err=False).then_inc(xg_land, 16)

            def put(b):
                if not (isinstance(b, int) and b == 0):
                    wait_alone(pool, y_store, b * 16, slot_land, 16)
                pool.tensor_copy(put_idx[:, :], slots[:, col(b), :].rearrange("s b c -> s (b c)")).then_inc(put_copied, 1)
                pool.wait_ge(put_copied, b + 1)
                wait_alone(pool, y_out_a, b * 2 + 2, slot_land, 16)
                pool.wait_ge(y_out_d, b * 2 + 2)
                pool.indirect_dma_start(
                    out=y_rows[:, :], out_offset=bass.IndirectOffsetOnAxis(ap=put_idx[:, 1:2], axis=0),
                    in_=y_sb[:, :], in_offset=None,
                    bounds_check=2 * T - 1, oob_is_err=False).then_inc(y_store, 16)

            pool.wait_ge(xg_zero, 1)
            take(0)
            take(1)
            put(0)
            with pool.Fori(1, NE - 1) as b:
                take(b + 1)
                put(b)
            put(NE - 1)
            pool.wait_ge(more_done, 1)
            n_more = pool.value_load(more_i[0:1, MAX_MORE:MAX_MORE + 1], min_val=0, max_val=MAX_MORE)
            with pool.If(n_more > 0):
                with pool.Fori(0, MAX_MORE) as b:
                    with pool.If(n_more > b):
                        take(b + NE)
                        put(b + NE)
            pool.wait_ge(y_store, n_more * 16 + 16 * NE)
            pool.sem_inc(experts_done, 1)
            for t in range(1, TT):
                pool.wait_ge(back_land[t], 16)
                pool.tensor_tensor(y_back[t][:, 0, :], y_back[t][:, 0, :], y_back[t][:, 1, :], ALU.add).then_inc(f_pair, 1)

        @block.tensor
        def _(pe):
            def dense(name, mode, n_tok=512, half_way=None):
                base, n, w = first[name], SEG_N[name], SEG_W[name]
                hi, lo = (mem_hi, mem_lo) if name in ("k", "v") else (act_hi, act_lo)

                def one(i, pieces=range(8), free=None):
                    b = base + i
                    for j in pieces:
                        pe.wait_ge(lo_done, b * 8 + (j + 1))
                        for m in range(4):
                            for kk in range(2):
                                kt = 2 * j + kk
                                if kt == 0 and free is not None:
                                    free(m)
                                if kt == 0 and not (isinstance(b, int) and b == 0):
                                    pe.wait_ge(bank_free[m], b)
                                wh, wl = w_hi[j % 2][:, kk, :], w_lo[j % 2][:, kk, :]
                                if mode == "features":
                                    o = psd[m][:, 0:n_tok]
                                    c = slice(P * m, P * m + P)
                                    pairs = [(wh[:, c], hi[:, kt, 0:n_tok]), (wh[:, c], lo[:, kt, 0:n_tok]),
                                             (wl[:, c], hi[:, kt, 0:n_tok])]
                                elif mode == "tokens":
                                    o = psd[m][:, 0:w]
                                    c = slice(P * m, P * m + P)
                                    pairs = [(hi[:, kt, c], wh[:, 0:w]), (hi[:, kt, c], wl[:, 0:w]),
                                             (lo[:, kt, c], wh[:, 0:w])]
                                else:
                                    o = psd[m][:, 0:256]
                                    c = slice(P * (m // 2), P * (m // 2) + P)
                                    v = slice(256 * (m % 2), 256 * (m % 2) + 256)
                                    pairs = [(hi[:, kt, c], wh[:, v]), (hi[:, kt, c], wl[:, v]),
                                             (lo[:, kt, c], wh[:, v])]
                                for q, (a, c) in enumerate(pairs):
                                    ins = pe.matmul(o, a, c, start=(kt == 0 and q == 0), stop=(kt == KT - 1 and q == 2))
                                if kt == KT - 1:
                                    ins.then_inc(bank_done[m], 1)
                        if j < 7:
                            ins.then_inc(w_used, 1)

                if half_way is not None:
                    free, turn = half_way
                    one(0, range(4), free)
                    turn()
                    one(0, range(4, 8))
                    with pe.Fori(1, n) as i:
                        one(i)
                elif n == 1:
                    one(0)
                else:
                    with pe.Fori(0, n) as i:
                        one(i)

            def turn_norm(name, src, tiles=None):
                for t in tiles or range(NORM_N[name]):
                    pe.wait_ge(n_xs, NORM_AT[name] + t + 1)
                    for g in range(4):
                        q = 4 * (NORM_AT[name] + t) + g
                        if q >= 4:
                            pe.wait_ge(n_lo, q - 3)
                        for k in range(4):
                            kt = 4 * g + k
                            ins = pe.transpose(psx[g][:, P * k:P * k + P], src[t % 2][:, kt * P:kt * P + P], ident[:, :])
                        ins.then_inc(n_turned, 1)

            pe.wait_ge(consts, 2)
            turn_norm("mix", xs)
            pe.wait_ge(n_lo, 16)
            dense("misc", "tokens")
            dense("head_t", "features")

            pe.wait_ge(k_norm, 3 * TT)
            for c in range(CT):
                for t in range(TT):
                    ins = pe.transpose(psx[c][:, P * t:P * t + P], c_kv[:, t, P * c:P * c + P], ident[:, :])
                ins.then_inc(k_turned, 1)
            for t in range(TT):
                ins = pe.transpose(psx[2][:, P * t:P * t + P], k_idx_n[:, t, :], ident[:, :])
            ins.then_inc(k_turned, 1)
            pe.wait_ge(const_land, 5 * 16)
            nr = (CONV + 1) * 8
            pe.transpose(psx[3][:, 0:nr], conv_rows[:, :], ident[0:nr, 0:nr]).then_inc(c_turned, 1)
            pe.wait_ge(k_out_a, 2)
            pe.wait_ge(k_out_d, 1)
            pe.wait_ge(c_out, 1)

            def keys_read(h):
                pe.wait_ge(kh_out_d if h % 2 else kh_out_a, h // 2 + 1)

            for h in range(DSA_H):
                if h >= 4:
                    keys_read(h - 4)
                for c in range(CT):
                    ins = pe.matmul(psx[h % 4][:, :], w_uk_raw[:, c, DSA_D * h:DSA_D * h + DSA_D], c_kv_t[:, c, :],
                                    start=(c == 0), stop=(c == CT - 1))
                ins.then_inc(kh_done, 1)
            for m in range(4):
                pe.wait_ge(bank_free[m], first["head_n"])
            for n in range(3 * IDX_H):
                i, h = 1 + n // IDX_H, n % IDX_H
                if n < 4:
                    keys_read(4 + n)
                else:
                    pe.wait_ge(relu_done, n - 3)
                r = slice(IDX_D * (h % 2), IDX_D * (h % 2) + IDX_D)
                pe.matmul(psx[n % 4][:, 0:P * (i + 1)], proj_t[r, 8 + h // 2, P * i:P * i + P],
                          k_idx_t[r, 0:P * (i + 1)], start=True, stop=True).then_inc(dot_done, 1)
            pe.wait_ge(relu_done, 3 * IDX_H)
            for g in range(2):
                for t in range(TT):
                    ins = pe.transpose(psx[g][0:ML_H, P * t:P * t + P],
                                       misc[:, t, MISC - 8 + 4 * g:MISC - 4 + 4 * g], ident[:, :])
                ins.then_inc(g_turned, 1)
            dense("head_n", "tokens")
            pe.wait_ge(g_sumd, 1)
            pe.wait_ge(g_em, 1)
            for t in range(TT):
                pe.transpose(psx[2][:, 4 * t:4 * t + 4], rows[4][:, P * t:P * t + P], ident[0:ML_H, 0:ML_H])
                ins = pe.transpose(psx[2][:, 16 + 4 * t:20 + 4 * t], rows[6][:, P * t:P * t + P], ident[0:ML_H, 0:ML_H])
            ins.then_inc(g_tok, 1)
            pe.wait_ge(g_tok_out, 2)

            pe.wait_ge(g_abs, 1)
            pe.wait_ge(silu_done, 8)
            for m in range(4):
                pe.wait_ge(bank_free[m], first["out"])
            def logits(n):
                i, h = n // DSA_H, n % DSA_H
                if n >= 4:
                    pe.wait_ge(lg_masked, n - 3)
                pe.matmul(psx[n % 4][:, 0:P * (i + 1)], proj_t[:, h, P * i:P * i + P], k_t[:, h, 0:P * (i + 1)],
                          start=True, stop=True).then_inc(lg_done, 1)

            def turn(n):
                i = n // DSA_H
                pe.wait_ge(prob_done, n + 1)
                if n >= 2:
                    pe.wait_ge(pt_out, n - 1)
                for k in range(i + 1):
                    ins = pe.transpose(psd[2 + n % 2][:, P * k:P * k + P], prob[n % 3][:, P * k:P * k + P], ident[:, :])
                ins.then_inc(pt_done, 1)

            def values(n):
                i, h = n // DSA_H, n % DSA_H
                pe.wait_ge(pt_out, n + 1)
                if h % 4 == 0 and n >= 8:
                    pe.wait_ge(o_lo, n // 4 - 1)
                for k in range(i + 1):
                    ins = pe.matmul(psd[n // 4 % 2][:, P * (h % 4):P * (h % 4) + P], v_n[:, k, DSA_D * h:DSA_D * h + DSA_D],
                                    prob_t[n % 3][:, k, :], start=(k == 0), stop=(k == i))
                ins.then_inc(pv_done, 1)

            logits(0)
            logits(1)
            pe.wait_ge(uv_land, 16)
            for t in range(TT):
                for m in range(2):
                    if t:
                        pe.wait_ge(vh_out_d if m else vh_out_a, t)
                    for c in range(CT):
                        ins = pe.matmul(psd[m][:, :], c_kv_t[:, c, P * t:P * t + P], w_uv_s[:, c, 512 * m:512 * m + 512],
                                        start=(c == 0), stop=(c == CT - 1))
                    ins.then_inc(vh_done, 1)
            pe.wait_ge(vh_out_a, TT)
            pe.wait_ge(vh_out_d, TT)
            for n in range(TT * DSA_H):
                if n + 2 < TT * DSA_H:
                    logits(n + 2)
                turn(n)
                if n:
                    values(n - 1)
            values(TT * DSA_H - 1)

            pe.wait_ge(o_lo, 2 * TT)
            pe.wait_ge(g_pick, 1)
            def max_row(h):
                if h >= 2:
                    pe.wait_ge(m_exp, 4 * (h - 1))
                    pe.wait_ge(m_den, h - 1)
                pe.matmul(psx[h % 2][:, :], pick_row[:, h, :], rows[5][:, :], start=True, stop=True).then_inc(m_row, 1)

            def key_query(h, j):
                n = 4 * h + j
                if n >= 2:
                    pe.wait_ge(m_p, n - 1)
                pe.matmul(psx[2 + n % 2][:, 0:T - P * j], proj_t[:, 16 + h, P * j:P * j + P], proj_t[:, 12 + h, P * j:T],
                          start=True, stop=True).then_inc(m_qk, 1)

            def memory_read(h, i):
                pe.wait_ge(m_p, 4 * h + i + 1)
                if h >= 2 and i == 0:
                    pe.wait_ge(m_hs, 4 * (h - 1))
                o = psd[2 * (h % 2) + i // 2][:, 256 * (i % 2):256 * (i % 2) + 256]
                for j in range(i + 1):
                    pe.matmul(o, p_ml[h % 2][:, j, P * i:P * i + P], proj_n[:, j, ML_V * h:ML_V * h + ML_V],
                              start=(j == 0), stop=(j == i))
                for j in range(i + 1):
                    ins = pe.matmul(psx[h % 2][:, i:i + 1], p_ml[h % 2][:, j, P * i:P * i + P], ones_col[:, :],
                                    start=(j == 0), stop=(j == i))
                ins.then_inc(m_pv, 1)

            max_row(0)
            for j in range(TT):
                key_query(0, j)
            for h in range(ML_H):
                if h + 1 < ML_H:
                    max_row(h + 1)
                pe.wait_ge(m_exp, 4 * h + 4)
                for j in range(TT):
                    if h + 1 < ML_H:
                        key_query(h + 1, j)
                    memory_read(h, j)

            def numerators_read(m):
                pe.wait_ge(m_hs, 12 + 2 * max(m - 1, 0))

            def turn_memory():
                for t in range(TT):
                    pe.wait_ge(m_norm, t + 1)
                for f in range(8):
                    if f >= 4:
                        pe.wait_ge(m_lo, f - 3)
                    for t in range(TT):
                        ins = pe.transpose(psx[f % 4][:, P * t:P * t + P], hs[:, t, P * f:P * f + P], ident[:, :])
                    ins.then_inc(m_turned, 1)
                pe.wait_ge(m_lo, 8)

            dense("out", "tokens", half_way=(numerators_read, turn_memory))
            turn_norm("x", xs)
            pe.wait_ge(n_lo, 4 * NORM_AT["mem"])
            dense("cq", "features")
            turn_norm("mem", mem_xs)
            pe.wait_ge(n_lo, 4 * NORM_AT["ffn"])
            dense("k", "features", N_MEM)
            dense("v", "halves")

            for m in range(4):
                pe.wait_ge(bank_free[m], first["co"])

            def x_logits(n):
                h, i = n // TT, n % TT
                if n >= 3:
                    pe.wait_ge(x_exp, n - 2)
                for d in range(4):
                    ins = pe.matmul(psx[n % 3][:, 0:N_MEM], x_q[:, 4 * h + d, P * i:P * i + P], x_k[:, 4 * h + d, :],
                                    start=(d == 0), stop=(d == 3))
                ins.then_inc(xl_done, 1)

            def x_turn(n):
                pe.wait_ge(x_prob, n + 1)
                if n >= 1:
                    pe.wait_ge(xt_out, n)
                for m in range(MT):
                    ins = pe.transpose(psx[3][:, P * m:P * m + P], xp[n % 3][:, P * m:P * m + P], ident[:, :])
                ins.then_inc(xt_done, 1)

            def x_values(h):
                pe.wait_ge(xt_out, TT * h + TT)
                for d in range(4):
                    if h:
                        pe.wait_ge(xo_lo, 4 * (h - 1) + d + 1)
                    for m in range(MT):
                        c = X_D * h + P * d
                        ins = pe.matmul(psd[d][:, :], x_v[:, m, c:c + P], xp_t[:, h % 2, m, :],
                                        start=(m == 0), stop=(m == MT - 1))
                    ins.then_inc(xo_done, 1)

            x_logits(0)
            x_logits(1)
            for n in range(X_H * TT):
                if n + 2 < X_H * TT:
                    x_logits(n + 2)
                x_turn(n)
                if n and n % TT == 0:
                    x_values(n // TT - 1)
            x_values(X_H - 1)
            pe.wait_ge(xo_lo, 16)
            dense("co", "tokens")

            def route(t):
                pe.wait_ge(n_lo, 4 * (NORM_AT["ffn"] + t + 1))
                for kt in range(KT):
                    ins = pe.matmul(psd[t][0:64, 0:P], w_r[:, kt, :], h_t[:, kt, P * t:P * t + P],
                                    start=(kt == 0), stop=(kt == KT - 1))
                ins.then_inc(r_done, 1)

            turn_norm("ffn", ffn_xs, (0, 1))
            pe.wait_ge(r_land, 4 * 16)
            pe.wait_ge(route_consts, 2)
            for t in range(TT):
                route(t)
                if t + 2 < TT:
                    turn_norm("ffn", ffn_xs, (t + 2,))
            for t in range(TT):
                pe.wait_ge(r_out, t + 1)
                ins = pe.transpose(psx[0][:, 64 * t:64 * t + 64], r_log_t[:, P * t:P * t + P], ident[0:64, 0:64])
            ins.then_inc(r_back, 1)
            pe.wait_ge(r_chose, 1)
            for t in range(TT):
                for s in range(t + 1):
                    ins = pe.matmul(psx[0][:, NE * t:NE * t + NE], before[:, :] if s == t else ones_sq[:, :],
                                    chose[:, s, :], start=(s == 0), stop=(s == t))
            for s in range(TT):
                ins = pe.matmul(psx[1][:, 0:NE], ones_sq[:, :], chose[:, s, :], start=(s == 0), stop=(s == TT - 1))
            ins.then_inc(r_rank, 1)

            def turn_rows(b):
                wait_alone(pe, xg_land, b * 16 + 16, consts, 2)
                for k in range(KT):
                    ins = pe.transpose(psx[2 + k // 8][:, BLOCK * (k % 8):BLOCK * (k % 8) + BLOCK],
                                       xg[:, k:D:KT], ident[0:BLOCK, 0:BLOCK])
                ins.then_inc(xg_turned, 1)

            def passes(o, x_hi, x_lo, w_hi_, w_lo_, start, stop):
                pe.matmul(o, x_hi, w_hi_, start=start, stop=False)
                pe.matmul(o, x_hi, w_lo_, start=False, stop=False)
                return pe.matmul(o, x_lo, w_hi_, start=False, stop=stop)

            def gate_up(b):
                pe.wait_ge(xg_out, b * 2 + 2)
                for r in range(8):
                    u, q = r // 4, r % 4
                    pe.wait_ge(e_lo_done, b * 12 + (r + 1))
                    for k in range(4):
                        c = slice(512 * k, 512 * k + 512)
                        ins = passes(psx[u][0:BLOCK, :], xt_hi[:, 4 * q + k, :], xt_lo[:, 4 * q + k, :],
                                     e_hi[r % 3][:, c], e_lo[r % 3][:, c], q == 0 and k == 0, q == 3 and k == 3)
                    ins.then_inc(e_used, 1)

            def down(b):
                wait_alone(pe, he_done, b + 1, consts, 2)
                for f in range(FT):
                    ins = pe.transpose(psx[0][:, BLOCK * f:BLOCK * f + BLOCK], he[:, P * f:P * f + P], ident[0:BLOCK, 0:BLOCK])
                ins.then_inc(he_turned, 1)
                if not (isinstance(b, int) and b == 0):
                    pe.wait_ge(y_out_a, b * 2)
                    pe.wait_ge(y_out_d, b * 2)
                pe.wait_ge(he_split_a, b + 1)
                pe.wait_ge(he_split_d, b + 1)
                for f in range(FT):
                    r = 8 + f
                    pe.wait_ge(e_lo_done, b * 12 + (r + 1))
                    for m in range(4):
                        c = slice(512 * m, 512 * m + 512)
                        ins = passes(psd[m][0:BLOCK, :], he_hi[:, f, :], he_lo[:, f, :], e_hi[r % 3][:, c],
                                     e_lo[r % 3][:, c], f == 0, f == FT - 1)
                    ins.then_inc(e_used, 1)

            turn_rows(0)
            gate_up(0)
            turn_rows(1)
            down(0)
            with pe.Fori(1, NE - 1) as b:
                gate_up(b)
                turn_rows(b + 1)
                down(b)
            gate_up(NE - 1)
            down(NE - 1)
            pe.wait_ge(more_done, 1)
            n_more = pe.value_load(more_i[0:1, MAX_MORE:MAX_MORE + 1], min_val=0, max_val=MAX_MORE)
            with pe.If(n_more > 0):
                with pe.Fori(0, MAX_MORE) as b:
                    with pe.If(n_more > b):
                        turn_rows(b + NE)
                        gate_up(b + NE)
                        down(b + NE)

        @block.scalar
        def _(act):
            def split(name, i, j):
                b = first[name] + i
                w = piece_width(name, i, j)
                act.wait_ge(w_land[j % 4], (b * 2 + (j // 4 + 1)) * 16)
                if j == 9:
                    act.wait_ge(bank_done[3], b + 1)
                elif j >= 2:
                    act.wait_ge(w_used, b * 7 + min(j - 1, 7))
                act.activation(w_hi[j % 2][:, :, 0:w], w_raw[j % 4][:, :, 0:w], ACT.Copy).then_inc(hi_done, 1)

            def dense(name, evac, behind=None, before_last=None, beside=None, banks=lambda i: (0, 2),
                      ahead=None):
                base, n = first[name], SEG_N[name]

                def one(i, top, bottom=2):
                    for j in range(bottom, min(top, 9)):
                        split(name, i, j)
                        if beside is not None:
                            beside(i, j - 2)
                    if evac is not None:
                        for m in banks(i):
                            act.wait_ge(bank_done[m], base + i + 1)
                            evac(i, m).then_inc(bank_free[m], 1)
                    if top > 9:
                        split(name, i, 9)
                        if beside is not None:
                            beside(i, 7)
                    if behind is not None:
                        behind(i)

                if beside is not None:
                    for i in range(n - 1):
                        one(i, 10)
                elif n > 1:
                    if ahead:
                        one(0, 10, ahead)
                    with act.Fori(1 if ahead else 0, n - 1) as i:
                        one(i, 10)
                if before_last is not None:
                    before_last()
                one(n - 1, 10 if name in NEXT else 8)
                act.wait_ge(bank_done[3], base + n)
                for m in range(4):
                    act.wait_ge(bank_free[m], base + n)

            roots = [0]

            def root(c0, n):
                roots[0] += 1
                act.wait_ge(n_var, roots[0])
                act.activation(stats[:, 3, c0:c0 + n], stats[:, 1, c0:c0 + n], ACT.Sqrt).then_inc(n_sd, 1)

            squares = [0]

            def square(src, junk_, t):
                if squares[0]:
                    act.wait_ge(n_sq, squares[0])
                squares[0] += 1
                act.activation(junk_, src, ACT.Square, accum_out=stats[:, 0, t:t + 1]).then_inc(n_sq, 1)

            def turned_tile(name, t, turned_out):
                for g in range(4):
                    act.wait_ge(n_turned, 4 * (NORM_AT[name] + t) + g + 1)
                    turned_out(t, g)

            def part_squares(name):
                def go(i):
                    for m in range(TT):
                        act.wait_ge(bank_free[m], i + (first[name] + 1))
                        c = span(i * 512, 512)
                        part = sq_part[:, m, span(i, 1)]
                        act.wait_ge(q_sq, i * TT + (SQ_AT[name] + m))
                        act.activation(sq_part_junk[:, :], x_res[:, m, c], ACT.Square, accum_out=part).then_inc(q_sq, 1)
                return go

            def turned_to(hi):
                def go(t, g):
                    act.activation(hi[:, 4 * g:4 * g + 4, P * t:P * t + P],
                                   psx[g][:, :].rearrange("p (k n) -> p k n", k=4), ACT.Copy).then_inc(n_hi, 1)
                return go

            for t in range(TT):
                act.wait_ge(x_land[t], 16)
                square(x_in[:, t, :], junk[:, :], t)
                root(t, 1)
                if t:
                    turned_tile("mix", t - 1, turned_to(act_hi))
            for j in range(2):
                split("misc", 0, j)
            turned_tile("mix", TT - 1, turned_to(act_hi))

            dense("misc", lambda i, m: act.activation(misc[:, m, :], psd[m][:, 0:MISC], ACT.Copy))
            act.wait_ge(n_xs, 4)
            for t in range(TT):
                if t:
                    act.wait_ge(k_sq, t)
                act.activation(relu_dot[0][:, 0:DSA_C], misc[:, t, 0:DSA_C], ACT.Square,
                               accum_out=stats[:, 0, t:t + 1]).then_inc(k_sq, 1)
            for t in range(TT):
                act.wait_ge(k_sq, TT + t)
                act.activation(relu_dot[0][:, 256:256 + IDX_D], misc[:, t, DSA_C:DSA_C + IDX_D], ACT.Square, scale=2.0,
                               accum_out=stats[:, 0, TT + t:TT + t + 1]).then_inc(k_sq, 1)
            root(0, 8)
            dense("head_t", lambda i, m: act.activation(proj_t[:, span(i * 4 + m, 1), :], psd[m][:, :], ACT.Copy))
            act.wait_ge(k_turned, 1)
            act.activation(c_kv_t[:, 0, :], psx[0][:, :], ACT.Copy).then_inc(k_out_a, 1)
            act.wait_ge(k_turned, 3)
            act.activation(k_idx_t[:, :], psx[2][:, :], ACT.Copy).then_inc(k_out_a, 1)
            for h in range(0, DSA_H, 2):
                act.wait_ge(kh_done, h + 1)
                act.activation(k_t[:, h, :], psx[h % 4][:, :], ACT.Copy).then_inc(kh_out_a, 1)
            for n in range(3 * IDX_H):
                i = 1 + n // IDX_H
                act.wait_ge(dot_done, n + 1)
                if n >= 2:
                    act.wait_ge(score_done, n - 1)
                act.activation(relu_dot[n % 2][:, 0:P * (i + 1)], psx[n % 4][:, 0:P * (i + 1)],
                               ACT.Relu).then_inc(relu_done, 1)

            def head_n_out(i, m):
                return act.activation(proj_n[:, m, 512 * i:512 * i + 512], psd[m][:, :], ACT.Copy if i < 2 else ACT.Sigmoid)

            def gates_and_silu(i, k):
                if (i, k) == (0, 2):
                    act.wait_ge(g_abs, 1)
                    act.activation(rows[2][:, :], rows[2][:, :], ACT.Exp).then_inc(act_own, 1)
                    act.wait_ge(act_own, 1)
                    act.activation(rows[2][:, :], rows[2][:, :], ACT.Ln, bias=1.0).then_inc(g_ln, 1)
                if (i, k) == (0, 4):
                    act.wait_ge(g_sumd, 1)
                    act.activation(rows[6][:, :], rows[6][:, :], ACT.Exp, scale=-1.0).then_inc(g_em, 1)
                f = 2 * i + k // 4
                if k % 4 == 3:
                    act.wait_ge(conv_done, f + 1)
                    act.activation(proj_t[:, 12 + f, :], conv_out[f % 2][:, :], ACT.Silu).then_inc(silu_done, 1)

            dense("head_n", head_n_out, beside=gates_and_silu, banks=lambda i: (0, 2) if i < 2 else (0, 1, 2, 3))
            def exp(n):
                act.wait_ge(lg_max, n + 1)
                c = slice(n % 16, n % 16 + 1)
                p = prob[n % 3][:, 0:P * (n // DSA_H + 1)]
                act.activation(p, p, ACT.Exp, bias=head_neg[:, c], accum_out=head_sum[:, c]).then_inc(exp_done, 1)

            def turned(n):
                i = n // DSA_H
                act.wait_ge(pt_done, n + 1)
                if n >= 3:
                    act.wait_ge(pv_done, n - 2)
                act.activation(prob_t[n % 3][:, 0:i + 1, :],
                               psd[2 + n % 2][:, 0:P * (i + 1)].rearrange("p (k q) -> p k q", k=i + 1),
                               ACT.Copy).then_inc(pt_out, 1)

            def heads_out(b):
                act.wait_ge(pv_done, 4 * b + 4)
                i, g = b // 2, b % 2
                act.activation(act_hi[:, 4 * g:4 * g + 4, P * i:P * i + P],
                               psd[b % 2][:, :].rearrange("p (h q) -> p h q", h=4), ACT.Copy).then_inc(o_hi, 1)

            exp(0)
            exp(1)
            for t in range(TT):
                act.wait_ge(vh_done, 2 * t + 1)
                act.activation(v_n[:, t, 0:512], psd[0][:, :], ACT.Copy).then_inc(vh_out_a, 1)
            for n in range(TT * DSA_H):
                turned(n)
                if n + 2 < TT * DSA_H:
                    exp(n + 2)
                if n > 4 and n % 4 == 2:
                    heads_out(n // 4 - 1)
            heads_out(2 * TT - 1)

            act.wait_ge(g_tok_out, 2)
            act.wait_ge(score_done, 3 * IDX_H)

            def decay(h):
                for j in range(TT):
                    n = 4 * h + j
                    act.wait_ge(m_row, h + 1)
                    if n >= 2:
                        act.wait_ge(m_p, n - 1)
                    act.activation(w_exp[n % 2][:, 0:T - P * j], psx[h % 2][:, P * j:T], ACT.Exp, scale=-1.0,
                                   bias=u_tok[:, j, h:h + 1]).then_inc(m_exp, 1)

            decay(0)
            for h in range(ML_H):
                if h + 1 < ML_H:
                    decay(h + 1)
                act.wait_ge(m_den, h + 1)
                for i in range(TT):
                    act.activation(hs[:, i, ML_V * h:ML_V * h + ML_V], psd[2 * (h % 2) + i // 2][:, 256 * (i % 2):256 * (i % 2) + 256],
                                   ACT.Copy, scale=den_inv[:, i, h:h + 1]).then_inc(m_hs, 1)
                for i in range(TT):
                    act.wait_ge(m_hs, 4 * h + i + 1)
                    if h or i:
                        act.wait_ge(m_sq, 4 * h + i)
                    act.activation(sq_junk[:, :], hs[:, i, ML_V * h:ML_V * h + ML_V], ACT.Square,
                                   accum_out=stats[:, 0, 4 * h + i:4 * h + i + 1]).then_inc(m_sq, 1)
            root(0, 16)
            for j in range(2, 6):
                split("out", 0, j)
            for f in range(8):
                act.wait_ge(m_turned, f + 1)
                act.activation(act_hi[:, 8 + f, :], psx[f % 4][:, :], ACT.Copy).then_inc(m_hi, 1)
            dense("out", None, behind=part_squares("out"), ahead=6)
            root(0, TT)
            for t in range(TT):
                turned_tile("x", t, turned_to(act_hi))

            def mem_squares():
                act.wait_ge(mem_land, 16)
                for t in range(MT):
                    square(mem_in[:, t, :], mem_xs[t][:, :], t)
                root(0, MT)

            dense("cq", lambda i, m: act.activation(x_q[:, span(i * 4 + m, 1), :], psd[m][:, :], ACT.Copy),
                  before_last=mem_squares)
            for t in range(MT):
                turned_tile("mem", t, turned_to(mem_hi))
            dense("k", lambda i, m: act.activation(x_k[:, span(i * 4 + m, 1), :], psd[m][:, 0:N_MEM], ACT.Copy))

            def v_out(i, m):
                c = 256 * (m % 2)
                c = span(i * 512 + c, 256)
                return act.activation(x_v[:, m // 2, c], psd[m][:, 0:256], ACT.Copy)

            dense("v", v_out)

            def x_soft(n):
                act.wait_ge(xl_max, n + 1)
                if n >= 3:
                    act.wait_ge(xt_done, n - 2)
                act.activation(xp[n % 3][:, :], psx[n % 3][:, 0:N_MEM], ACT.Exp, scale=float(X_D) ** -0.5,
                               bias=head_neg[:, n:n + 1], accum_out=head_sum[:, n:n + 1]).then_inc(x_exp, 1)

            def x_turned(n):
                h, i = n // TT, n % TT
                act.wait_ge(xt_done, n + 1)
                if i == 0 and h >= 2:
                    act.wait_ge(xo_done, 4 * (h - 1))
                act.activation(xp_t[:, h % 2, :, P * i:P * i + P],
                               psx[3][:, 0:2 * P].rearrange("p (m q) -> p m q", m=2), ACT.Copy).then_inc(xt_out, 1)

            def x_out(h, half):
                for d in (2 * half, 2 * half + 1):
                    k = 4 * h + d
                    act.wait_ge(xo_done, k + 1)
                    act.activation(act_hi[:, k, :], psd[d][:, :], ACT.Copy).then_inc(xo_hi, 1)

            x_soft(0)
            x_soft(1)
            for n in range(X_H * TT):
                x_turned(n)
                if n + 2 < X_H * TT:
                    x_soft(n + 2)
                if n > TT and n % TT in (1, 2):
                    x_out(n // TT - 1, n % TT - 1)
            x_out(X_H - 1, 0)
            x_out(X_H - 1, 1)
            dense("co", None, behind=part_squares("co"))

            def h_out(t, g):
                if g % 2 == 0:
                    act.activation(h_t[:, 4 * g:4 * g + 4, P * t:P * t + P],
                                   psx[g][:, :].rearrange("p (k n) -> p k n", k=4), ACT.Copy).then_inc(n_hi, 1)

            root(0, TT)
            for t in range(TT):
                turned_tile("ffn", t, h_out)
            def e_split(b, r):
                act.wait_ge(e_land[r % 6], b * 32 + (r // 6 + 1) * 16)
                if not (isinstance(b, int) and b == 0 and r < 3):
                    act.wait_ge(e_used, b * 12 + (r - 2))
                act.activation(e_hi[r % 3][:, :], e_raw[r % 6][:, :], ACT.Copy).then_inc(e_hi_done, 1)

            for t in range(TT):
                act.wait_ge(r_done, t + 1)
                act.activation(r_log_t[:, P * t:P * t + P], psd[t][0:64, 0:P], ACT.Copy).then_inc(r_out, 1)
            for t in range(TT):
                act.wait_ge(r_neg, 1)
                act.activation(g_exp[:, t, :], r_log[:, t, 0:G], ACT.Exp, bias=neg_m[:, 0, t:t + 1],
                               accum_out=g_sum[:, t:t + 1]).then_inc(r_exp, 1)
            for t in range(TT):
                act.wait_ge(r_neg, 2)
                act.activation(e_exp[:, t, :], e_log[:, t, :], ACT.Exp, bias=neg_m[:, 1, t:t + 1]).then_inc(r_exp, 1)
            for r in range(3):
                e_split(0, r)

            def rows_out(b):
                act.wait_ge(xg_turned, b + 1)
                for k in range(2):
                    act.activation(xt_hi[:, 8 * k:8 * k + 8, :], psx[2 + k][:, :].rearrange("p (k s) -> p k s", k=8),
                                   ACT.Copy).then_inc(xt_high, 1)

            def expert(b, ahead):
                for r in range(3, 7):
                    e_split(b, r)
                act.wait_ge(e_used, b * 12 + 4)
                act.activation(he_g[:, :], psx[0][0:BLOCK, :], ACT.Silu).then_inc(he_silu, 1)
                for r in range(7, 10):
                    e_split(b, r)
                act.wait_ge(he_turned, b + 1)
                act.activation(he_hi[:, :, :], psx[0][:, 0:FT * BLOCK].rearrange("p (f s) -> p f s", f=FT),
                               ACT.Copy).then_inc(he_split_a, 1)
                e_split(b, 10)
                if ahead:
                    rows_out(b + 1)
                for r in range(11, 15 if ahead else 12):
                    e_split(b, r)
                act.wait_ge(put_copied, b + 1)
                act.wait_ge(e_used, b * 12 + 12)
                for m in (0, 2):
                    act.activation(y_sb[:, 512 * m:512 * m + 512], psd[m][0:BLOCK, :], ACT.Copy,
                                   scale=put_idx[:, 2:3].bitcast(F32)).then_inc(y_out_a, 1)

            rows_out(0)
            with act.Fori(0, NE - 1) as b:
                expert(b, True)
            expert(NE - 1, False)
            act.wait_ge(more_done, 1)
            n_more = act.value_load(more_i[0:1, MAX_MORE:MAX_MORE + 1], min_val=0, max_val=MAX_MORE)
            with act.If(n_more > 0):
                with act.Fori(0, MAX_MORE) as b:
                    with act.If(n_more > b):
                        for r in range(3):
                            e_split(b + NE, r)
                        rows_out(b + NE)
                        expert(b + NE, False)
            for t in range(TT):
                act.wait_ge(f_add, t + 1)
                if t:
                    act.wait_ge(f_sq, t)
                act.activation(xs_f[:, :], x_res[:, t, :], ACT.Square, accum_out=stats[:, 0, t:t + 1]).then_inc(f_sq, 1)
                root(t, 1)

        @block.vector
        def _(dve):
            own = [0]

            def link(ins):
                own[0] += 1
                ins.then_inc(dve_own, 1)
                dve.wait_ge(dve_own, own[0])

            def split(name, i, j):
                b = first[name] + i
                w = piece_width(name, i, j)
                dve.wait_ge(hi_done, b * 8 + (j + 1))
                dve.tensor_tensor(w_lo[j % 2][:, :, 0:w], w_raw[j % 4][:, :, 0:w], w_hi[j % 2][:, :, 0:w].bitcast(F32),
                                  ALU.subtract).then_inc(lo_done, 1)

            def dense(name, evac, banks=lambda i: (1, 3), beside=None, before_last=None, ahead=None):
                base, n = first[name], SEG_N[name]

                def one(i, top, bottom=2):
                    for j in range(bottom, min(top, 9)):
                        split(name, i, j)
                        if beside is not None:
                            beside(i, j - 2)
                    for m in banks(i):
                        dve.wait_ge(bank_done[m], base + i + 1)
                        evac(i, m).then_inc(bank_free[m], 1)
                    if top > 9:
                        split(name, i, 9)
                        if beside is not None:
                            beside(i, 7)

                if beside is not None:
                    for i in range(n - 1):
                        one(i, 10)
                elif n > 1:
                    if ahead:
                        one(0, 10, ahead)
                    with dve.Fori(1 if ahead else 0, n - 1) as i:
                        one(i, 10)
                if before_last is not None:
                    before_last()
                one(n - 1, 10 if name in NEXT else 8)
                dve.wait_ge(bank_done[3], base + n)
                for m in range(4):
                    dve.wait_ge(bank_free[m], base + n)

            roots = [0]

            def rstd(c0, n, inv):
                roots[0] += 1
                var, r, t = stats[:, 1, c0:c0 + n], stats[:, 2, c0:c0 + n], stats[:, 3, c0:c0 + n]
                dve.tensor_scalar(var, stats[:, 0, c0:c0 + n], inv, EPS, ALU.mult, ALU.add).then_inc(n_var, 1)
                dve.wait_ge(n_sd, roots[0])
                link(dve.reciprocal(r, t))
                link(dve.tensor_tensor(t, r, r, ALU.mult))
                link(dve.tensor_tensor(t, t, var, ALU.mult))
                link(dve.tensor_scalar(t, t, -0.5, 1.5, ALU.mult, ALU.add))
                link(dve.tensor_tensor(r, r, t, ALU.mult))

            def scale(src, dst, g, t):
                dve.scalar_tensor_tensor(dst[t % 2][:, :], src, stats[:, 2, t:t + 1], g[:, :], ALU.mult,
                                         ALU.mult).then_inc(n_xs, 1)

            def turned_tile(name, t, lo):
                base = NORM_AT[name]
                for k in range(4):
                    q = 4 * (base + t) + k
                    if lo is not None:
                        hi_t, lo_t = lo
                        dve.wait_ge(n_hi, q + 1)
                        s = (slice(None), slice(4 * k, 4 * k + 4), slice(P * t, P * t + P))
                        dve.tensor_tensor(lo_t[s], psx[k][:, :].rearrange("p (k n) -> p k n", k=4),
                                          hi_t[s].bitcast(F32), ALU.subtract).then_inc(n_lo, 1)
                    elif k % 2:
                        dve.wait_ge(n_turned, q + 1)
                        dve.wait_ge(n_hi, 4 * base + 2 * t + k // 2 + 1)
                        dve.tensor_copy(h_t[:, 4 * k:4 * k + 4, P * t:P * t + P],
                                        psx[k][:, :].rearrange("p (k n) -> p k n", k=4)).then_inc(n_lo, 2)

            def norm(name, dst, g, lo, n_gain):
                base = NORM_AT[name]
                dve.wait_ge(q_sq, SQ_AT[name] + 4 * TT)
                link(dve.tensor_reduce(stats[:, 0, 0:TT], sq_part[:, :, :], AX.X, ALU.add))
                rstd(0, TT, 1.0 / D)
                dve.wait_ge(gain_land, 16 * n_gain)
                scale(x_res[:, 0, :], dst, g, 0)
                for t in range(TT):
                    if t + 1 < TT:
                        if t >= 1:
                            dve.wait_ge(n_turned, 4 * (base + t))
                            if name == "ffn":
                                dve.wait_ge(h_store[(t + 1) % 2], 16 * ((t + 1) // 2))
                        scale(x_res[:, t + 1, :], dst, g, t + 1)
                    turned_tile(name, t, lo)

            def one_of(i, m):
                return span(i * 4 + m, 1)

            dve.wait_ge(gain_land, 16)
            for t in range(TT):
                dve.wait_ge(n_sq, t + 1)
                rstd(t, 1, 1.0 / D)
                if t >= 2:
                    dve.wait_ge(n_turned, 4 * (t - 1))
                scale(x_in[:, t, :], xs, gain, t)
                if t:
                    turned_tile("mix", t - 1, (act_hi, act_lo))
            for j in range(2):
                split("misc", 0, j)
            turned_tile("mix", TT - 1, (act_hi, act_lo))
            dense("misc", lambda i, m: dve.tensor_copy(misc[:, m, :], psd[m][:, 0:MISC]))
            dve.wait_ge(k_sq, 8)
            rstd(0, 8, 1.0 / DSA_C)
            dve.tensor_scalar(idx_w[:, :, :], misc[:, :, DSA_C + IDX_D:DSA_C + IDX_D + IDX_H],
                              float(IDX_H * IDX_D) ** -0.5, None, ALU.mult).then_inc(consts, 1)
            dve.wait_ge(kv_land, 32)
            for t in range(TT):
                dve.scalar_tensor_tensor(c_kv[:, t, :], misc[:, t, 0:DSA_C], stats[:, 2, t:t + 1], kv_gain[:, :],
                                         ALU.mult, ALU.mult).then_inc(k_norm, 1)
                for c in range(2):
                    dve.scalar_tensor_tensor(k_idx_n[:, t, IDX_D * c:IDX_D * c + IDX_D], misc[:, t, DSA_C:DSA_C + IDX_D],
                                             stats[:, 2, TT + t:TT + t + 1], ki_gain[:, :], ALU.mult,
                                             ALU.mult).then_inc(k_norm, 1)
            dense("head_t", lambda i, m: dve.tensor_copy(proj_t[:, one_of(i, m), :], psd[m][:, :]))
            dve.wait_ge(k_turned, 2)
            dve.tensor_copy(c_kv_t[:, 1, :], psx[1][:, :]).then_inc(k_out_d, 1)
            dve.wait_ge(c_turned, 1)
            dve.tensor_copy(conv_t[:, :], psx[3][:, 0:(CONV + 1) * 8]).then_inc(c_out, 1)
            dve.wait_ge(c_out, 1)
            for h in range(1, DSA_H, 2):
                dve.wait_ge(kh_done, h + 1)
                dve.tensor_copy(k_t[:, h, :], psx[h % 4][:, :]).then_inc(kh_out_d, 1)
            dve.wait_ge(consts, 3)
            for n in range(3 * IDX_H):
                i, h = 1 + n // IDX_H, n % IDX_H
                s = P * (i + 1)
                dve.wait_ge(relu_done, n + 1)
                if h == 0:
                    dve.tensor_scalar(chosen[i][:, :], relu_dot[n % 2][:, 0:s], idx_w[:, i, h:h + 1], None,
                                      ALU.mult).then_inc(score_done, 1)
                else:
                    dve.wait_ge(score_done, n)
                    dve.scalar_tensor_tensor(chosen[i][:, :], relu_dot[n % 2][:, 0:s], idx_w[:, i, h:h + 1],
                                             chosen[i][:, :], ALU.mult, ALU.add).then_inc(score_done, 1)
            dve.wait_ge(score_done, 3 * IDX_H)
            for i in (1, 2, 3):
                link(dve.memset(chosen[i][0:CHUNK, P * (i + 1) - CHUNK:P * (i + 1)], NEG))
            dve.sem_inc(round_done, 1)

            assert TOPK // 8 * 2 == SEG_N["head_n"] * 8

            def best_keys(i, k):
                n = 24 * i + 6 * (k // 2) + 2 * (k % 2) + 1
                for q, c in enumerate((2, 1) if k % 2 else (3,)):
                    dve.wait_ge(round_done, n + 2 * q)
                    dve.max(best[:, c, :], chosen[c][:, :]).then_inc(round_done, 1)
                    dve.wait_ge(round_done, n + 2 * q + 1)
                    dve.match_replace(out=chosen[c][:, :], in_to_replace=best[:, c, :], in_values=chosen[c][:, :],
                                      imm_value=TAKEN).then_inc(round_done, 1)

            def gates_in():
                dve.wait_ge(g_turned, 2)
                dve.wait_ge(const_land, 5 * 16)
                link(dve.tensor_scalar(rows[0][:, :], psx[0][0:ML_H, :], gate_i[:, :], None, ALU.add))
                link(dve.tensor_scalar(rows[1][:, :], psx[1][0:ML_H, :], gate_f[:, :], None, ALU.add))
                link(dve.tensor_scalar(rows[2][:, :], rows[1][:, :], -1.0, None, ALU.mult))
                dve.tensor_tensor(rows[2][:, :], rows[1][:, :], rows[2][:, :], ALU.min).then_inc(g_abs, 1)
                link(dve.memset(r_ones[:, :], 1.0))

            def gates_summed():
                dve.wait_ge(g_ln, 1)
                link(dve.scalar_tensor_tensor(rows[1][:, :], rows[1][:, :], 0.0, rows[2][:, :], ALU.min, ALU.subtract))
                link(dve.tensor_tensor_scan(rows[3][:, :], r_ones[:, :], rows[1][:, :], 0.0, ALU.mult, ALU.add))
                link(dve.tensor_tensor(rows[4][:, :], rows[0][:, :], rows[3][:, :], ALU.subtract))
                link(dve.tensor_tensor_scan(rows[5][:, :], r_ones[:, :], rows[4][:, :], 0.0, ALU.mult, ALU.max))
                dve.tensor_tensor(rows[6][:, :], rows[3][:, :], rows[5][:, :], ALU.add).then_inc(g_sumd, 1)

            def convolved(f):
                src, dst = proj_t[:, 12 + f, :], conv_out[f % 2][:, :]
                tap = lambda j: conv_t[:, 8 * j + f:8 * j + f + 1]
                if f >= 2:
                    dve.wait_ge(silu_done, f - 1)
                link(dve.tensor_scalar(dst, src, tap(3), tap(4), ALU.mult, ALU.add))
                for j in (2, 1):
                    s = 3 - j
                    link(dve.scalar_tensor_tensor(dst[:, s:T], src[:, 0:T - s], tap(j), dst[:, s:T], ALU.mult, ALU.add))
                dve.scalar_tensor_tensor(dst[:, 3:T], src[:, 0:T - 3], tap(0), dst[:, 3:T], ALU.mult,
                                         ALU.add).then_inc(conv_done, 1)

            def keys_gates_conv(i, k):
                best_keys(i, k)
                if (i, k) == (0, 0):
                    gates_in()
                if (i, k) == (0, 3):
                    gates_summed()
                if k % 4 == 1:
                    convolved(2 * i + k // 4)

            dense("head_n", lambda i, m: dve.tensor_copy(proj_n[:, m, 512 * i:512 * i + 512], psd[m][:, :]),
                  banks=lambda i: (1, 3) if i < 2 else (), beside=keys_gates_conv)
            dve.wait_ge(g_tok, 1)
            dve.tensor_copy(u_tok[:, :, :], psx[2][:, 0:16].rearrange("p (t h) -> p t h", t=TT)).then_inc(g_tok_out, 1)
            dve.tensor_copy(em_tok[:, :, :], psx[2][:, 16:32].rearrange("p (t h) -> p t h", t=TT)).then_inc(g_tok_out, 1)
            dve.wait_ge(round_done, 6 * TOPK // 8 + 1)
            for c in (1, 2, 3):
                link(dve.tensor_scalar(chosen[c][:, :], chosen[c][:, :], TAKEN, HIDE, ALU.not_equal, ALU.mult))
            dve.wait_ge(bias_done, 1)
            def masked(n):
                i = n // DSA_H
                s = P * (i + 1)
                c = slice(n % 16, n % 16 + 1)
                dve.wait_ge(lg_done, n + 1)
                if n >= 3:
                    dve.wait_ge(pt_done, n - 2)
                dve.tensor_tensor_reduce(out=prob[n % 3][:, 0:s], in0=psx[n % 4][:, 0:s],
                                         in1=bias0[:, :] if i == 0 else chosen[i][:, :], scale=float(DSA_D) ** -0.5,
                                         scalar=-3.0e38, op0=ALU.add, op1=ALU.max,
                                         accum_out=head_max[:, c]).then_inc(lg_masked, 1)
                dve.wait_ge(lg_masked, n + 1)
                dve.tensor_scalar(head_neg[:, c], head_max[:, c], -1.0, None, ALU.mult).then_inc(lg_max, 1)

            def normed(n):
                s = P * (n // DSA_H + 1)
                c = slice(n % 16, n % 16 + 1)
                dve.wait_ge(exp_done, n + 1)
                link(dve.reciprocal(head_inv[:, c], head_sum[:, c]))
                dve.tensor_scalar(prob[n % 3][:, 0:s], prob[n % 3][:, 0:s], head_inv[:, c], None,
                                  ALU.mult).then_inc(prob_done, 1)

            def heads_out(b):
                i, g = b // 2, b % 2
                dve.wait_ge(o_hi, b + 1)
                a = (slice(None), slice(4 * g, 4 * g + 4), slice(P * i, P * i + P))
                dve.tensor_tensor(act_lo[a], psd[b % 2][:, :].rearrange("p (h q) -> p h q", h=4),
                                  act_hi[a].bitcast(F32), ALU.subtract).then_inc(o_lo, 1)

            masked(0)
            masked(1)
            for t in range(TT):
                dve.wait_ge(vh_done, 2 * t + 2)
                dve.tensor_copy(v_n[:, t, 512:1024], psd[1][:, :]).then_inc(vh_out_d, 1)
            for n in range(TT * DSA_H):
                normed(n)
                if n + 2 < TT * DSA_H:
                    masked(n + 2)
                if n > 4 and n % 4 == 3:
                    heads_out(n // 4 - 1)
            heads_out(2 * TT - 1)

            dve.tensor_copy(pick_row[:, :, :], ident[0:ML_H, 0:ML_H].unsqueeze(2).to_broadcast([ML_H, ML_H, P])).then_inc(g_pick, 1)
            dve.wait_ge(g_tok_out, 2)

            def weigh(h):
                for j in range(TT):
                    n = 4 * h + j
                    dve.wait_ge(m_qk, n + 1)
                    dve.wait_ge(m_sel, n + 1)
                    if j == 0 and h >= 2:
                        dve.wait_ge(m_pv, 4 * (h - 1))
                    dve.scalar_tensor_tensor(p_ml[h % 2][:, j, P * j:T], psx[2 + n % 2][:, 0:T - P * j], float(ML_K) ** -0.5,
                                             w_exp[n % 2][:, 0:T - P * j], ALU.mult, ALU.mult).then_inc(m_p, 1)

            weigh(0)
            for h in range(ML_H):
                if h + 1 < ML_H:
                    weigh(h + 1)
                dve.wait_ge(m_pv, 4 * h + 4)
                den = psx[h % 2][:, 0:TT]
                link(dve.scalar_tensor_tensor(den_inv[:, :, h], den, -1.0, em_tok[:, :, h], ALU.mult, ALU.max))
                link(dve.tensor_tensor(den_inv[:, :, h], den, den_inv[:, :, h], ALU.max))
                dve.reciprocal(den_inv[:, :, h], den_inv[:, :, h]).then_inc(m_den, 1)
            dve.wait_ge(m_sq, 16)
            rstd(0, 16, 1.0 / ML_V)
            dve.wait_ge(ml_land, 16)
            for i in range(TT):
                for h in range(ML_H):
                    c = slice(ML_V * h, ML_V * h + ML_V)
                    link(dve.scalar_tensor_tensor(hs[:, i, c], hs[:, i, c], stats[:, 2, 4 * h + i:4 * h + i + 1],
                                                  ml_gain[:, c], ALU.mult, ALU.mult))
                dve.tensor_tensor(hs[:, i, :], hs[:, i, :], proj_n[:, i, 1024:2048], ALU.mult).then_inc(m_norm, 1)
                if i in (0, 1):
                    split("out", 0, 2 + i)
            for j in (4, 5):
                split("out", 0, j)
            for f in range(8):
                dve.wait_ge(m_hi, f + 1)
                dve.tensor_tensor(act_lo[:, 8 + f, :], psx[f % 4][:, :], act_hi[:, 8 + f, :].bitcast(F32),
                                  ALU.subtract).then_inc(m_lo, 1)

            def add_res(i, m):
                if isinstance(i, int) and i == 0 and m == 0:
                    dve.wait_ge(res_land, 16)
                c = span(i * 512, 512)
                return dve.tensor_tensor(x_res[:, m, c], psd[m][:, :], x_res[:, m, c], ALU.add)

            dve.sem_inc(q_sq, 1)
            dense("out", add_res, banks=lambda i: (0, 1, 2, 3), ahead=6)
            norm("x", xs, gain, (act_hi, act_lo), 2)

            def mem_normed():
                dve.wait_ge(n_sq, NORM_N["mix"] + MT)
                rstd(0, MT, 1.0 / D)
                dve.wait_ge(gain_land, 16 * 3)
                for t in range(MT):
                    scale(mem_in[:, t, :], mem_xs, mem_gain, t)

            dense("cq", lambda i, m: dve.tensor_copy(x_q[:, one_of(i, m), :], psd[m][:, :]), before_last=mem_normed)
            for t in range(MT):
                turned_tile("mem", t, (mem_hi, mem_lo))
            dense("k", lambda i, m: dve.tensor_copy(x_k[:, one_of(i, m), :], psd[m][:, 0:N_MEM]))

            def v_out(i, m):
                c = 256 * (m % 2)
                c = span(i * 512 + c, 256)
                return dve.tensor_copy(x_v[:, m // 2, c], psd[m][:, 0:256])

            dense("v", v_out)

            def x_max(n):
                dve.wait_ge(xl_done, n + 1)
                link(dve.tensor_reduce(head_max[:, n:n + 1], psx[n % 3][:, 0:N_MEM], AX.X, ALU.max))
                dve.tensor_scalar(head_neg[:, n:n + 1], head_max[:, n:n + 1], -float(X_D) ** -0.5, None,
                                  ALU.mult).then_inc(xl_max, 1)

            def x_out(h, half):
                for d in (2 * half, 2 * half + 1):
                    k = 4 * h + d
                    dve.wait_ge(xo_hi, k + 1)
                    dve.tensor_tensor(act_lo[:, k, :], psd[d][:, :], act_hi[:, k, :].bitcast(F32),
                                      ALU.subtract).then_inc(xo_lo, 1)

            x_max(0)
            x_max(1)
            for n in range(X_H * TT):
                dve.wait_ge(x_exp, n + 1)
                link(dve.reciprocal(head_inv[:, n:n + 1], head_sum[:, n:n + 1]))
                dve.tensor_scalar(xp[n % 3][:, :], xp[n % 3][:, :], head_inv[:, n:n + 1], None,
                                  ALU.mult).then_inc(x_prob, 1)
                if n + 2 < X_H * TT:
                    x_max(n + 2)
                if n > TT and n % TT in (2, 3):
                    x_out(n // TT - 1, n % TT - 2)
            x_out(X_H - 1, 0)
            x_out(X_H - 1, 1)
            dense("co", add_res, banks=lambda i: (0, 1, 2, 3))
            norm("ffn", ffn_xs, gain, None, 4)

            def spread(ap, shape, axis):
                return ap.unsqueeze(axis).to_broadcast(shape)

            def e_split(b, r):
                dve.wait_ge(e_hi_done, b * 12 + (r + 1))
                dve.tensor_tensor(e_lo[r % 3][:, :], e_raw[r % 6][:, :], e_hi[r % 3][:, :].bitcast(F32),
                                  ALU.subtract).then_inc(e_lo_done, 1)

            dve.wait_ge(r_land, 64)
            dve.wait_ge(route_consts, 2)
            dve.wait_ge(r_back, 1)
            link(dve.tensor_tensor(r_log[:, :, :], psx[0][:, 0:64 * TT].rearrange("p (t r) -> p t r", t=TT)[:, :, 0:G + NE],
                                   spread(r_bias[:, :], [P, TT, G + NE], 1), ALU.add))
            link(dve.tensor_copy(g_log8[:, :, 0:G], r_log[:, :, 0:G]))
            for t in range(TT):
                link(dve.max(g_top[:, t, :], g_log8[:, t, :]))
                link(dve.max_index(g_idx[:, t, :], g_top[:, t, :], g_log8[:, t, :]))
            dve.tensor_scalar(neg_m[:, 0, :], g_top[:, :, 0], -1.0, None, ALU.mult).then_inc(r_neg, 1)
            link(dve.tensor_copy(g_sel[:, :], g_idx[:, :, 0]))
            link(dve.tensor_tensor(g_oh[:, :, :], spread(iota_e[:, 0:G], [P, TT, G], 1),
                                   spread(g_sel[:, :], [P, TT, G], 2), ALU.is_equal))
            for t in range(TT):
                link(dve.tensor_tensor(e_mul[:, t, :, :], r_log[:, t, G:G + NE].rearrange("p (g e) -> p g e", g=G),
                                       spread(g_oh[:, t, :], [P, G, EG], 2), ALU.mult))
            link(dve.tensor_reduce(e_log[:, :, :], e_mul[:, :, :, :].rearrange("p t g e -> p t e g"), AX.X, ALU.add))
            for t in range(TT):
                link(dve.max(e_top[:, t, :], e_log[:, t, :]))
            dve.tensor_scalar(neg_m[:, 1, :], e_top[:, :, 0], -1.0, None, ALU.mult).then_inc(r_neg, 1)
            dve.wait_ge(r_exp, 8)
            for t in range(TT):
                link(dve.max(e_best[:, t, :], e_exp[:, t, :]))
                link(dve.max_index(e_idx[:, t, :], e_best[:, t, :], e_exp[:, t, :]))
            link(dve.tensor_copy(e_id[:, :, :], e_idx[:, :, 0:2]))
            link(dve.scalar_tensor_tensor(e_id[:, :, :], spread(g_sel[:, :], [P, TT, 2], 2), float(EG), e_id[:, :, :],
                                          ALU.mult, ALU.add))
            link(dve.tensor_tensor(e_den[:, :], e_best[:, :, 0], e_best[:, :, 1], ALU.add))
            link(dve.tensor_tensor(e_den[:, :], e_den[:, :], g_sum[:, :], ALU.mult))
            link(dve.reciprocal(e_den[:, :], e_den[:, :]))
            link(dve.tensor_tensor(gate[:, :, :], e_best[:, :, 0:2], spread(e_den[:, :], [P, TT, 2], 2), ALU.mult))
            for t in range(TT):
                link(dve.tensor_tensor(one_hot[:, t, :, :], spread(iota_e[:, :], [P, 2, NE], 1),
                                       spread(e_id[:, t, :], [P, 2, NE], 2), ALU.is_equal))
            dve.tensor_tensor(chose[:, :, :], one_hot[:, :, 0, :], one_hot[:, :, 1, :], ALU.add).then_inc(r_chose, 1)
            for r in range(3):
                e_split(0, r)
            dve.wait_ge(r_rank, 1)
            link(dve.tensor_copy(rank[:, :, :], psx[0][:, 0:TT * NE].rearrange("p (t e) -> p t e", t=TT)))
            link(dve.tensor_copy(count[:, :], psx[1][:, 0:NE]))
            link(dve.tensor_tensor(full[:, :, :], spread(count[:, :], [P, NE, 8], 2), spread(iota_m[:, :], [P, NE, 8], 1),
                                   ALU.is_gt))
            link(dve.tensor_reduce(more[:, :], full[:, :, :], AX.X, ALU.add))
            link(dve.tensor_tensor_scan(more_end[:, :], ones32[:, :], more[:, :], 0.0, ALU.mult, ALU.add))
            link(dve.tensor_tensor(more_at[:, :], more_end[:, :], more[:, :], ALU.subtract))
            for src, dst in ((rank, pos), (more_at, pos_at)):
                for t in range(TT):
                    s = spread(src[:, t, :] if src is rank else src[:, :], [P, 2, NE], 1)
                    link(dve.tensor_tensor(picked[:, t, :, :], one_hot[:, t, :, :], s, ALU.mult))
                link(dve.tensor_reduce(dst[:, :, :], picked[:, :, :, :], AX.X, ALU.add))
            for t in range(TT):
                link(dve.tensor_tensor(pos_full[:, t, :, :], spread(pos[:, t, :], [P, 2, 8], 2),
                                       spread(iota_m[:, :], [P, 2, 8], 1), ALU.is_ge))
            link(dve.tensor_reduce(pos_q[:, :, :], pos_full[:, :, :, :], AX.X, ALU.add))
            link(dve.tensor_tensor(row_f[:, :, :], pos_at[:, :, :], pos_q[:, :, :], ALU.add))
            link(dve.tensor_scalar(row_f[:, :, :], row_f[:, :, :], float(NE - 1), None, ALU.add))
            link(dve.tensor_tensor(row_f[:, :, :], row_f[:, :, :], e_id[:, :, :], ALU.subtract))
            link(dve.tensor_scalar(row_t[:, :, :], pos_q[:, :, :], 0.0, None, ALU.is_gt))
            link(dve.tensor_tensor(row_f[:, :, :], row_f[:, :, :], row_t[:, :, :], ALU.mult))
            link(dve.tensor_tensor(row_f[:, :, :], row_f[:, :, :], e_id[:, :, :], ALU.add))
            link(dve.tensor_tensor(row_f[:, :, :], row_f[:, :, :], pos_q[:, :, :], ALU.subtract))
            link(dve.scalar_tensor_tensor(row_f[:, :, :], row_f[:, :, :], float(BLOCK), pos[:, :, :], ALU.mult, ALU.add))
            link(dve.tensor_copy(slot_new[:, :, :, 0:2], tok_f[:, :, :, :]))
            link(dve.tensor_copy(slot_new[:, :, :, 2].bitcast(F32), gate[:, :, :]))
            dve.tensor_copy(row_i[:, :, :], row_f[:, :, :]).then_inc(r_row, 1)
            link(dve.tensor_tensor(more_cmp[:, :, :], spread(iota_b[:, :], [1, MAX_MORE, NE], 2),
                                   spread(more_end[0:1, :], [1, MAX_MORE, NE], 1), ALU.is_ge))
            link(dve.tensor_reduce(more_f[:, 0:MAX_MORE], more_cmp[:, :, :], AX.X, ALU.add))
            link(dve.tensor_scalar(more_f[:, 0:MAX_MORE], more_f[:, 0:MAX_MORE], float(NE - 1), None, ALU.min))
            link(dve.tensor_copy(more_f[:, MAX_MORE:MAX_MORE + 1], more_end[0:1, NE - 1:NE]))
            dve.tensor_copy(more_i[:, :], more_f[:, :]).then_inc(more_done, 1)

            def rows_out(b):
                for k in range(2):
                    dve.wait_ge(xt_high, b * 2 + (k + 1))
                    dve.tensor_tensor(xt_lo[:, 8 * k:8 * k + 8, :], psx[2 + k][:, :].rearrange("p (k s) -> p k s", k=8),
                                      xt_hi[:, 8 * k:8 * k + 8, :].bitcast(F32), ALU.subtract).then_inc(xg_out, 1)

            def expert(b, ahead):
                for r in range(3, 10):
                    e_split(b, r)
                dve.wait_ge(he_silu, b + 1)
                dve.wait_ge(e_used, b * 12 + 8)
                dve.tensor_tensor(he[:, :], psx[1][0:BLOCK, :], he_g[:, :], ALU.mult).then_inc(he_done, 1)
                dve.wait_ge(he_split_a, b + 1)
                dve.tensor_tensor(he_lo[:, :, :], psx[0][:, 0:FT * BLOCK].rearrange("p (f s) -> p f s", f=FT),
                                  he_hi[:, :, :].bitcast(F32), ALU.subtract).then_inc(he_split_d, 1)
                e_split(b, 10)
                if ahead:
                    rows_out(b + 1)
                for r in range(11, 15 if ahead else 12):
                    e_split(b, r)
                dve.wait_ge(put_copied, b + 1)
                dve.wait_ge(e_used, b * 12 + 12)
                for m in (1, 3):
                    dve.tensor_scalar(y_sb[:, 512 * m:512 * m + 512], psd[m][0:BLOCK, :], put_idx[:, 2:3].bitcast(F32),
                                      None, ALU.mult).then_inc(y_out_d, 1)

            rows_out(0)
            with dve.Fori(0, NE - 1) as b:
                expert(b, True)
            expert(NE - 1, False)
            n_more = dve.value_load(more_i[0:1, MAX_MORE:MAX_MORE + 1], min_val=0, max_val=MAX_MORE)
            with dve.If(n_more > 0):
                with dve.Fori(0, MAX_MORE) as b:
                    with dve.If(n_more > b):
                        for r in range(3):
                            e_split(b + NE, r)
                        rows_out(b + NE)
                        expert(b + NE, False)
            dve.wait_ge(fg_land, 16)

            def finish(t):
                dve.wait_ge(f_sq, t + 1)
                rstd(t, 1, 1.0 / D)
                if t >= 2:
                    dve.wait_ge(f_store[t % 2], 16 * (t // 2))
                dve.scalar_tensor_tensor(fin_o[t % 2][:, :], x_res[:, t, :], stats[:, 2, t:t + 1], fin_gain[:, :],
                                         ALU.mult, ALU.mult).then_inc(f_out, 1)

            for t in range(TT):
                if t == 0:
                    dve.wait_ge(back_land[t], 16)
                    link(dve.tensor_tensor(y_back[t][:, 0, :], y_back[t][:, 0, :], y_back[t][:, 1, :], ALU.add))
                else:
                    dve.wait_ge(f_pair, t)
                dve.tensor_tensor(x_res[:, t, :], x_res[:, t, :], y_back[t][:, 0, :], ALU.add).then_inc(f_add, 1)
                if t:
                    finish(t - 1)
            finish(TT - 1)


_INS = ["x", "mem", "norm_mix_g", "w_in", "kv_norm_g", "k_idx_norm_g", "w_uk", "w_uv", "conv_w", "conv_b", "gate_b",
        "ml_norm_g", "w_out", "norm_x_g", "mem_norm_g", "w_cq", "w_ckv", "w_co", "norm_ffn_g", "w_group", "b_group",
        "w_router", "b_router", "w_gate", "w_up", "w_down", "final_norm_g"]
_OUTS = [((1, T, D), "float32")]


def _w_in_columns(w):
    sizes = [DSA_H * DSA_D, DSA_C, IDX_H * IDX_D, IDX_D, IDX_H, ML_H * ML_K, ML_H * ML_K, ML_H * ML_V, ML_H, ML_H,
             ML_H * ML_V]
    dq, ckv, qi, ki, wi, mq, mk, mv, mi, mf, mo = np.split(np.asarray(w), np.cumsum(sizes)[:-1], axis=-1)
    return np.concatenate([ckv, ki, wi, mi, mf, dq, qi, mq, mk, mv, mo], axis=-1)


def kernel(**inputs):
    import concourse.bacc as _bacc
    from concourse import mybir as _mybir
    from concourse.bass_utils import run_bass_kernel_spmd as _run

    nc = _bacc.Bacc("TRN2", target_bir_lowering=False, num_devices=1)
    arrays, args = {}, []
    for name in _INS:
        a = _w_in_columns(inputs[name]) if name == "w_in" else inputs[name]
        a = np.ascontiguousarray(a)
        arrays[f"in_{name}_dram"] = a
        args.append(nc.dram_tensor(f"in_{name}_dram", a.shape, _mybir.dt.from_np(a.dtype), kind="ExternalInput").ap())
    for i, (shape, dtype) in enumerate(_OUTS):
        dt = _mybir.dt.from_np(np.dtype(dtype))
        args.append(nc.dram_tensor(f"out_{i}_dram", shape, dt, kind="ExternalOutput").ap())
    layer(nc, *args)
    r = _run(nc, [arrays], core_ids=[0])
    return r.results[0]["out_0_dram"]
```
